# Optimizing a Trainium2 kernel written in Bass

```python
import jax, jax.numpy as jnp
from jax import lax
import numpy as np

D_MODEL = 2048
BATCH = 1
SEQ = 256
DEPTH = 1

MLSTM_HEADS = 8
MLSTM_QK_DIM = 128
MLSTM_V_DIM = 256
MLSTM_QK_WIDTH = MLSTM_HEADS * MLSTM_QK_DIM
MLSTM_V_WIDTH = MLSTM_HEADS * MLSTM_V_DIM
CHUNK = 64
CONV_WIDTH = D_MODEL
CONV_GROUPS = 16
CONV_K = 3
EPS = 1e-6

SPLIT_WIDTHS = (
    MLSTM_QK_WIDTH, MLSTM_QK_WIDTH,
    MLSTM_V_WIDTH, MLSTM_V_WIDTH, MLSTM_V_WIDTH,
    MLSTM_HEADS, MLSTM_HEADS,
    CONV_WIDTH, CONV_WIDTH, CONV_WIDTH, CONV_WIDTH,
    D_MODEL, D_MODEL,
)
IN_WIDTH = sum(SPLIT_WIDTHS)


def _split_offsets():
    offs, acc = [], 0
    for w in SPLIT_WIDTHS:
        offs.append(acc)
        acc += w
    return offs

def rms_norm(x, w):
    xf = x.astype(jnp.float32)
    y = xf * lax.rsqrt(jnp.mean(xf * xf, axis=-1, keepdims=True) + EPS)
    return (y * w.astype(jnp.float32)).astype(x.dtype)

def mlstm_chunkwise(q, k, v, i_pre, f_pre):
    f32 = jnp.float32
    bsz, s, h, dk = q.shape
    dv = v.shape[-1]
    nc = s // CHUNK

    def to_chunks(t):
        t = t.astype(f32).reshape((bsz, nc, CHUNK, h) + t.shape[3:])
        return jnp.moveaxis(t, (1, 3), (0, 2))

    qc = to_chunks(q) * (dk ** -0.5)
    kc = to_chunks(k)
    vc = to_chunks(v)
    log_i = to_chunks(i_pre)
    log_f = to_chunks(jax.nn.log_sigmoid(f_pre.astype(f32)))
    causal = jnp.tril(jnp.ones((CHUNK, CHUNK), dtype=bool))

    def step(carry, inp):
        c_state, n_state, m_state = carry
        qb, kb, vb, li, lf = inp
        b = jnp.cumsum(lf, axis=-1)
        g = b[..., -1]
        d_intra = b[..., :, None] - b[..., None, :] + li[..., None, :]
        d_intra = jnp.where(causal, d_intra, -jnp.inf)
        d_inter = b + m_state[..., None]
        m_row = jnp.maximum(d_inter, jnp.max(d_intra, axis=-1))
        w_intra = jnp.exp(d_intra - m_row[..., None])
        w_inter = jnp.exp(d_inter - m_row)
        scores = jnp.einsum('bhld,bhsd->bhls', qb, kb) * w_intra
        num = jnp.einsum('bhls,bhsv->bhlv', scores, vb) \
            + w_inter[..., None] * jnp.einsum('bhld,bhdv->bhlv', qb, c_state)
        den = jnp.sum(scores, axis=-1) + w_inter * jnp.einsum('bhld,bhd->bhl', qb, n_state)
        h_out = num / jnp.maximum(jnp.abs(den), jnp.exp(-m_row))[..., None]
        d_state = g[..., None] - b + li
        m_new = jnp.maximum(g + m_state, jnp.max(d_state, axis=-1))
        ws = jnp.exp(d_state - m_new[..., None])
        keep = jnp.exp(g + m_state - m_new)
        c_new = keep[..., None, None] * c_state + jnp.einsum('bhs,bhsd,bhsv->bhdv', ws, kb, vb)
        n_new = keep[..., None] * n_state + jnp.einsum('bhs,bhsd->bhd', ws, kb)
        return (c_new, n_new, m_new), h_out

    init = (jnp.zeros((bsz, h, dk, dv), f32), jnp.zeros((bsz, h, dk), f32), jnp.zeros((bsz, h), f32))
    _, hs = lax.scan(step, init, (qc, kc, vc, log_i, log_f))
    hs = jnp.moveaxis(hs, (0, 2), (1, 3))
    return hs.reshape(bsz, s, h, dv)

def causal_depthwise_conv(u, w):
    ch = u.shape[-1]
    return lax.conv_general_dilated(
        u, w[:, None, :].astype(u.dtype), window_strides=(1,), padding=[(CONV_K - 1, 0)],
        dimension_numbers=('NWC', 'WIO', 'NWC'), feature_group_count=ch)

def first_inputs(seed: int = 0) -> dict:
    key = jax.random.key(seed)
    ks = jax.random.split(key, 16)
    d = D_MODEL
    nrm = jax.random.normal
    x = nrm(ks[0], (BATCH, SEQ, d), jnp.float32)
    c = nrm(ks[1], (BATCH, d), jnp.float32)
    norm1_w = 1.0 + 0.05 * nrm(ks[2], (DEPTH, d), jnp.float32)
    w_ada = 0.3 * d ** -0.5 * nrm(ks[3], (DEPTH, d, 3 * d), jnp.float32)
    b_ada = 0.02 * nrm(ks[4], (DEPTH, 3 * d), jnp.float32)
    w_in = d ** -0.5 * nrm(ks[5], (DEPTH, d, IN_WIDTH), jnp.float32)
    b_in = 0.02 * nrm(ks[6], (DEPTH, IN_WIDTH), jnp.float32)
    offs = _split_offsets()
    f_off = offs[6]
    b_in = b_in.at[:, f_off:f_off + MLSTM_HEADS].add(jnp.linspace(3.0, 6.0, MLSTM_HEADS, dtype=jnp.float32))
    conv_w = CONV_K ** -0.5 * nrm(ks[7], (DEPTH, CONV_K, CONV_WIDTH), jnp.float32)
    headnorm_w = 1.0 + 0.05 * nrm(ks[8], (DEPTH, MLSTM_V_WIDTH), jnp.float32)
    w_proj_a = MLSTM_V_WIDTH ** -0.5 * nrm(ks[9], (DEPTH, MLSTM_V_WIDTH, d), jnp.float32)
    w_proj_b = CONV_WIDTH ** -0.5 * nrm(ks[10], (DEPTH, CONV_WIDTH, d), jnp.float32)
    w_out = d ** -0.5 * nrm(ks[11], (DEPTH, d, d), jnp.float32)
    normf_w = 1.0 + 0.05 * nrm(ks[12], (d,), jnp.float32)
    return {"x": x, "c": c, "norm1_w": norm1_w, "w_ada": w_ada, "b_ada": b_ada,
            "w_in": w_in, "b_in": b_in, "conv_w": conv_w, "headnorm_w": headnorm_w,
            "w_proj_a": w_proj_a, "w_proj_b": w_proj_b, "w_out": w_out, "normf_w": normf_w}

def first_block(x, c, norm1_w, w_ada, b_ada, w_in, b_in, conv_w, headnorm_w,
              w_proj_a, w_proj_b, w_out, normf_w):
    bsz, s, d = x.shape
    offs = _split_offsets()
    split_points = offs[1:]
    c_act = jax.nn.silu(c)
    for l in range(DEPTH):
        mod = c_act @ w_ada[l] + b_ada[l]
        shift, scale, gate = jnp.split(mod, 3, axis=-1)
        h = rms_norm(x, norm1_w[l]) * (1.0 + scale[:, None, :]) + shift[:, None, :]
        proj = h @ w_in[l] + b_in[l]
        (q, k, v, o, z_a, i_pre, f_pre, u, b_gate, c_gate, z_b, g_a, g_b) = \
            jnp.split(proj, split_points, axis=-1)
        h_a = mlstm_chunkwise(
            q.reshape(bsz, s, MLSTM_HEADS, MLSTM_QK_DIM),
            k.reshape(bsz, s, MLSTM_HEADS, MLSTM_QK_DIM),
            v.reshape(bsz, s, MLSTM_HEADS, MLSTM_V_DIM),
            i_pre, f_pre)
        h_a = jax.nn.sigmoid(o.astype(jnp.float32)).reshape(bsz, s, MLSTM_HEADS, MLSTM_V_DIM) * h_a
        h_a = rms_norm(h_a, headnorm_w[l].reshape(MLSTM_HEADS, MLSTM_V_DIM))
        h_a = h_a.reshape(bsz, s, MLSTM_V_WIDTH).astype(x.dtype) * jax.nn.silu(z_a)
        y_a = h_a @ w_proj_a[l]
        h_b = b_gate * causal_depthwise_conv(c_gate * u, conv_w[l])
        y_b = (h_b * jax.nn.silu(z_b)) @ w_proj_b[l]
        merged = jax.nn.sigmoid(g_a) * y_a + jax.nn.sigmoid(g_b) * y_b
        x = x + gate[:, None, :] * (merged @ w_out[l])
    return rms_norm(x, normf_w)


A_HEADS = 8
A_DK = 128
A_DV = 128
A_WIDTH = A_HEADS * A_DV

B_QK_HEADS = 4
B_V_HEADS = 8
B_DK = 128
B_DV = 128
B_WIDTH = B_V_HEADS * B_DV
CONV = 4
B_CONV_CH = 2 * B_QK_HEADS * B_DK + B_WIDTH

MIX_WIDTH = A_WIDTH + B_WIDTH

IN_SIZES = (A_HEADS * A_DK, A_HEADS * A_DK, A_WIDTH, A_WIDTH,
            B_QK_HEADS * B_DK, B_QK_HEADS * B_DK, B_WIDTH, B_WIDTH,
            B_V_HEADS, B_V_HEADS)
IN_WIDTH_2 = 4 * A_HEADS * A_DK + 2 * B_QK_HEADS * B_DK + 2 * B_WIDTH + 2 * B_V_HEADS

P_HEADS = 8
N_KEYS = 128
N_EXPERTS = N_KEYS * N_KEYS
P_DKEY = 256
P_TOPK = 16
P_BLOCK = 128


def _rmsnorm(x, g):
    xf = x.astype(jnp.float32)
    y = xf * lax.rsqrt(jnp.mean(xf * xf, axis=-1, keepdims=True) + EPS)
    return (y * g.astype(jnp.float32)).astype(x.dtype)

def _gated_rmsnorm(o, z, g):
    of = o.astype(jnp.float32)
    y = of * lax.rsqrt(jnp.mean(of * of, axis=-1, keepdims=True) + EPS)
    return y * g.astype(jnp.float32) * jax.nn.silu(z.astype(jnp.float32))

def _l2norm(x):
    xf = x.astype(jnp.float32)
    return xf * lax.rsqrt(jnp.sum(xf * xf, axis=-1, keepdims=True) + EPS)

def _chunk(t):
    b, s, h = t.shape[:3]
    rest = t.shape[3:]
    t = t.reshape((b, s // CHUNK, CHUNK, h) + rest)
    return t.transpose((1, 0, 3, 2) + tuple(range(4, t.ndim)))

def _unchunk(t):
    n, b, h, c, d = t.shape
    return t.transpose(1, 0, 3, 2, 4).reshape(b, n * c, h, d)

def _causal_conv_silu(x, w):
    s = x.shape[1]
    xp = jnp.pad(x, ((0, 0), (CONV - 1, 0), (0, 0)))
    y = xp[:, 0:s, :] * w[0]
    for j in range(1, CONV):
        y = y + xp[:, j:j + s, :] * w[j]
    return jax.nn.silu(y)

def _hgrn2(q, f_logit, v, lb):
    q = q.astype(jnp.float32)
    z = f_logit.astype(jnp.float32)
    v = v.astype(jnp.float32)
    lb = lb.astype(jnp.float32)
    log_f = jnp.log(lb + (1.0 - lb) * jax.nn.sigmoid(z))
    k = (1.0 - lb) * jax.nn.sigmoid(-z)
    qc, kc, vc = _chunk(q), _chunk(k), _chunk(v)
    bc = jnp.cumsum(_chunk(log_f), axis=-2)
    causal = jnp.tril(jnp.ones((CHUNK, CHUNK), dtype=bool))

    def step(S, inp):
        q_c, k_c, v_c, b_c = inp
        diff = b_c[..., :, None, :] - b_c[..., None, :, :]
        decay = jnp.exp(jnp.where(causal[:, :, None], diff, -jnp.inf))
        att = jnp.einsum('bhtd,bhsd,bhtsd->bhts', q_c, k_c, decay)
        o = (jnp.einsum('bhtd,bhdv->bhtv', q_c * jnp.exp(b_c), S)
             + jnp.einsum('bhts,bhsv->bhtv', att, v_c))
        b_last = b_c[..., -1:, :]
        S = (S * jnp.exp(b_last[..., 0, :, None])
             + jnp.einsum('bhsd,bhsv->bhdv', k_c * jnp.exp(b_last - b_c), v_c))
        return S, o

    S0 = jnp.zeros((q.shape[0], q.shape[2], A_DK, A_DV), jnp.float32)
    _, o = lax.scan(step, S0, (qc, kc, vc, bc))
    return _unchunk(o)

def _gated_delta(q, k, v, beta, g):
    q = _chunk(q.astype(jnp.float32) * (B_DK ** -0.5))
    k = _chunk(k.astype(jnp.float32))
    v = _chunk(v.astype(jnp.float32))
    beta = _chunk(beta.astype(jnp.float32))
    gc = jnp.cumsum(_chunk(g.astype(jnp.float32)), axis=-1)
    incl = jnp.tril(jnp.ones((CHUNK, CHUNK), dtype=bool))
    strict = jnp.tril(jnp.ones((CHUNK, CHUNK), dtype=bool), k=-1)
    L = jnp.exp(jnp.where(incl, gc[..., :, None] - gc[..., None, :], -jnp.inf))
    kb = k * beta[..., None]
    M = jnp.eye(CHUNK, dtype=jnp.float32) + jnp.where(
        strict, jnp.einsum('...td,...sd->...ts', kb, k) * L, 0.0)
    u = lax.linalg.triangular_solve(M, v * beta[..., None], left_side=True,
                                    lower=True, unit_diagonal=True)
    w = lax.linalg.triangular_solve(M, kb * jnp.exp(gc)[..., None], left_side=True,
                                    lower=True, unit_diagonal=True)
    a_qk = jnp.einsum('...td,...sd->...ts', q, k) * L
    qg = q * jnp.exp(gc)[..., None]
    g_last = gc[..., -1:]
    kd = k * jnp.exp(g_last - gc)[..., None]
    dl = jnp.exp(g_last)[..., None]

    def step(S, inp):
        qg_c, kd_c, u_c, w_c, a_c, dl_c = inp
        v_new = u_c - jnp.einsum('bhtd,bhdv->bhtv', w_c, S)
        o = (jnp.einsum('bhtd,bhdv->bhtv', qg_c, S)
             + jnp.einsum('bhts,bhsv->bhtv', a_c, v_new))
        S = S * dl_c + jnp.einsum('bhsd,bhsv->bhdv', kd_c, v_new)
        return S, o

    S0 = jnp.zeros((qg.shape[1], qg.shape[2], B_DK, B_DV), jnp.float32)
    _, o = lax.scan(step, S0, (qg, kd, u, w, a_qk, dl))
    return _unchunk(o)

def _peer(xn, w_query, sub_keys, u_tab, v_tab):
    b, s, d = xn.shape
    t = b * s
    xt = xn.reshape(t, d)
    qry = jnp.einsum('td,dhk->thk', xt, w_query).astype(jnp.float32)
    half = P_DKEY // 2
    s1 = jnp.einsum('thk,hnk->thn', qry[..., :half], sub_keys[0].astype(jnp.float32))
    s2 = jnp.einsum('thk,hnk->thn', qry[..., half:], sub_keys[1].astype(jnp.float32))
    v1, i1 = lax.top_k(s1, P_TOPK)
    v2, i2 = lax.top_k(s2, P_TOPK)
    cand = (v1[..., :, None] + v2[..., None, :]).reshape(t, P_HEADS, P_TOPK * P_TOPK)
    best, pos = lax.top_k(cand, P_TOPK)
    expert = (jnp.take_along_axis(i1, pos // P_TOPK, axis=-1) * N_KEYS
              + jnp.take_along_axis(i2, pos % P_TOPK, axis=-1))
    gate = jax.nn.softmax(best, axis=-1)
    nblk = t // P_BLOCK

    def blk(args):
        xb, eb, gb = args
        hid = jax.nn.gelu(jnp.einsum('pd,phkd->phk', xb, u_tab[eb]).astype(jnp.float32),
                          approximate=False)
        return jnp.einsum('phk,phkd->pd', (gb * hid).astype(xb.dtype), v_tab[eb])

    y = lax.map(blk, (xt.reshape(nblk, P_BLOCK, d),
                      expert.reshape(nblk, P_BLOCK, P_HEADS, P_TOPK),
                      gate.reshape(nblk, P_BLOCK, P_HEADS, P_TOPK)))
    return y.reshape(b, s, d)

def second_inputs(seed: int = 0) -> dict:
    key = jax.random.key(seed)
    ks = jax.random.split(key, 20)
    f32 = jnp.float32
    nrm = lambda k, shape, scale: jax.random.normal(k, shape, f32) * scale
    gain = lambda k, shape: 1.0 + 0.02 * jax.random.normal(k, shape, f32)
    dt = jnp.exp(jax.random.uniform(ks[8], (DEPTH, B_V_HEADS), f32,
                                    minval=np.log(1e-3), maxval=np.log(1e-1)))
    return {
        "x": nrm(ks[0], (BATCH, SEQ, D_MODEL), 1.0),
        "attn_norm_g": gain(ks[1], (DEPTH, D_MODEL)),
        "w_in": nrm(ks[2], (DEPTH, D_MODEL, IN_WIDTH_2), D_MODEL ** -0.5),
        "hgrn_lb_logits": nrm(ks[3], (DEPTH + 1, A_HEADS, A_DK), 0.1),
        "hgrn_norm_g": gain(ks[4], (DEPTH, A_DV)),
        "gdn_conv_w": nrm(ks[5], (DEPTH, CONV, B_CONV_CH), CONV ** -0.5),
        "gdn_A_log": jnp.log(jax.random.uniform(ks[6], (DEPTH, B_V_HEADS), f32,
                                                minval=1.0, maxval=16.0)),
        "gdn_dt_bias": dt + jnp.log(-jnp.expm1(-dt)),
        "gdn_norm_g": gain(ks[7], (DEPTH, B_DV)),
        "w_out": nrm(ks[9], (DEPTH, MIX_WIDTH, D_MODEL), MIX_WIDTH ** -0.5),
        "ffn_norm_g": gain(ks[10], (DEPTH, D_MODEL)),
        "peer_w_query": nrm(ks[11], (DEPTH, D_MODEL, P_HEADS, P_DKEY), D_MODEL ** -0.5),
        "peer_sub_keys": nrm(ks[12], (DEPTH, 2, P_HEADS, N_KEYS, P_DKEY // 2),
                             (P_DKEY // 2) ** -0.5),
        "peer_u": nrm(ks[13], (DEPTH, N_EXPERTS, D_MODEL), D_MODEL ** -0.5),
        "peer_v": nrm(ks[14], (DEPTH, N_EXPERTS, D_MODEL), P_HEADS ** -0.5),
        "final_norm_g": gain(ks[15], (D_MODEL,)),
    }

def second_block(x, attn_norm_g, w_in, hgrn_lb_logits, hgrn_norm_g, gdn_conv_w, gdn_A_log,
              gdn_dt_bias, gdn_norm_g, w_out, ffn_norm_g, peer_w_query, peer_sub_keys,
              peer_u, peer_v, final_norm_g):
    b, s, _ = x.shape
    lb_all = jnp.cumsum(jax.nn.softmax(hgrn_lb_logits.astype(jnp.float32), axis=0), axis=0)
    offs = []
    acc = 0
    for n in IN_SIZES[:-1]:
        acc += n
        offs.append(acc)
    rep = B_V_HEADS // B_QK_HEADS
    h = x
    for l in range(DEPTH):
        xn = _rmsnorm(h, attn_norm_g[l])
        proj = xn @ w_in[l]
        a_q, a_f, a_i, a_g, b_q, b_k, b_v, b_z, b_b, b_a = jnp.split(proj, offs, axis=-1)
        o_a = _hgrn2(a_q.reshape(b, s, A_HEADS, A_DK), a_f.reshape(b, s, A_HEADS, A_DK),
                     a_i.reshape(b, s, A_HEADS, A_DV), lb_all[l])
        o_a = _gated_rmsnorm(o_a, a_g.reshape(b, s, A_HEADS, A_DV), hgrn_norm_g[l])
        qkv = _causal_conv_silu(jnp.concatenate([b_q, b_k, b_v], axis=-1), gdn_conv_w[l])
        nqk = B_QK_HEADS * B_DK
        gq = _l2norm(qkv[..., :nqk].reshape(b, s, B_QK_HEADS, B_DK))
        gk = _l2norm(qkv[..., nqk:2 * nqk].reshape(b, s, B_QK_HEADS, B_DK))
        gv = qkv[..., 2 * nqk:].reshape(b, s, B_V_HEADS, B_DV)
        gq = jnp.repeat(gq, rep, axis=2)
        gk = jnp.repeat(gk, rep, axis=2)
        beta = jax.nn.sigmoid(b_b.astype(jnp.float32))
        g = -jnp.exp(gdn_A_log[l].astype(jnp.float32)) * jax.nn.softplus(
            b_a.astype(jnp.float32) + gdn_dt_bias[l].astype(jnp.float32))
        o_b = _gated_delta(gq, gk, gv, beta, g)
        o_b = _gated_rmsnorm(o_b, b_z.reshape(b, s, B_V_HEADS, B_DV), gdn_norm_g[l])
        mix = jnp.concatenate([o_a.reshape(b, s, A_WIDTH), o_b.reshape(b, s, B_WIDTH)],
                              axis=-1).astype(x.dtype)
        h = h + mix @ w_out[l]
        hn = _rmsnorm(h, ffn_norm_g[l])
        h = h + _peer(hn, peer_w_query[l], peer_sub_keys[l], peer_u[l], peer_v[l])
    return _rmsnorm(h, final_norm_g)


def setup_inputs(seed=0):
    out = dict(first_inputs(seed))
    for name, value in second_inputs(seed + 1).items():
        if name != "x":
            out[name + "_2"] = value
    return out


def reference(
    x, c, norm1_w, w_ada, b_ada, w_in, b_in, conv_w, headnorm_w, w_proj_a, w_proj_b, w_out,
    normf_w, attn_norm_g_2, w_in_2, hgrn_lb_logits_2, hgrn_norm_g_2, gdn_conv_w_2, gdn_A_log_2,
    gdn_dt_bias_2, gdn_norm_g_2, w_out_2, ffn_norm_g_2, peer_w_query_2, peer_sub_keys_2,
    peer_u_2, peer_v_2, final_norm_g_2,
):
    x = first_block(
        x, c, norm1_w, w_ada, b_ada, w_in, b_in, conv_w, headnorm_w, w_proj_a, w_proj_b, w_out,
        normf_w,
    )
    return second_block(
        x, attn_norm_g_2, w_in_2, hgrn_lb_logits_2, hgrn_norm_g_2, gdn_conv_w_2, gdn_A_log_2,
        gdn_dt_bias_2, gdn_norm_g_2, w_out_2, ffn_norm_g_2, peer_w_query_2, peer_sub_keys_2,
        peer_u_2, peer_v_2, final_norm_g_2,
    )


_drawn_inputs = setup_inputs


def setup_inputs(seed=0):
    import zlib

    import numpy as np

    out = dict(_drawn_inputs(seed))
    spreads = {}
    factors = {'headnorm_w': 5.104,
     'hgrn_norm_g_2': 60.108,
     'gdn_norm_g_2': 61.043,
     'final_norm_g_2': 24.584,
     'ffn_norm_g_2': 20.365}
    for name, (base, spread) in spreads.items():
        noise = np.random.default_rng([zlib.crc32(name.encode()), seed]).standard_normal(out[name].shape)
        drawn = base * np.exp(spread * noise) if base else spread * noise
        out[name] = __import__('jax').numpy.asarray(drawn.astype(out[name].dtype))
    for name, factor in factors.items():
        out[name] = (out[name] * factor).astype(out[name].dtype)
    return out
```

```python
from contextlib import ExitStack, contextmanager

import concourse.bass as bass
from concourse import mybir

ALU = mybir.AluOpType
ACT = mybir.ActivationFunctionType
AX = mybir.AxisListType
F32 = mybir.dt.float32
U32 = mybir.dt.uint32
ds = bass.ds

P = 128
T = 256
TT = T // P
D = 2048
KT = D // P
EPS = 1e-6
HEADS = 8
QKW = HEADS * 128
VW = 2048
OFF_K, OFF_V, OFF_O, OFF_Z = QKW, 2 * QKW, 2 * QKW + VW, 2 * QKW + 2 * VW
OFF_I = 2 * QKW + 3 * VW
OFF_U = OFF_I + 2 * HEADS
OFF_B, OFF_C, OFF_ZB, OFF_GA, OFF_GB = (OFF_U + n * D for n in range(1, 6))
IN_1 = OFF_GB + D
OFF2_F, OFF2_I, OFF2_G = 1024, 2048, 3072
OFF2_BQ, OFF2_BK, OFF2_BV, OFF2_BZ = 4096, 4608, 5120, 6144
OFF2_BB = 7168
GROUPS = 4
TAPS = 4
N_KEYS = 128
TOPK = 16
LEVELS = [1, 2, 4, 8, 16, 32, 64]

PK_QKVOZ_B, PK_NORM1, PK_HEADN, PK_NORMF, PK_ATTN = 0, 64, 80, 96, 112
PK_REST_B, PK_FFN, PK_FINAL = 128, 128 + 96, 128 + 112
PK_CONV, PK_BADA, PK_C, PK_HGN, PK_GDN = 256, 256 + 48, 256 + 96, 256 + 112, 256 + 113
PK_GCONV, PK_LB = 384, 384 + 64
PACK_ROWS = [128, 128, 114, 80]

N_PARAMS = 21
SLOT = 8192
ADA_DVE = 6
PEER_SLOT = 4096


class Count:

    def __init__(self, sem, name=""):
        self.sem, self.n, self.lead, self.name = sem, 0, 0, name

    def value(self, more=0):
        return self.lead + (self.n + more)

    def up(self, k=1):
        self.n += k
        return self.value()


@contextmanager
def rounds(eng, count, *counts):
    with eng.Fori(0, count) as i:
        before = [c.n for c, _ in counts]
        for c, per in counts:
            c.lead = i * per
        yield i
        for (c, per), b in zip(counts, before):
            assert c.n - b == per, (c.name, c.n - b, per)
    for c, per in counts:
        c.lead = 0
        c.n += (count - 1) * per


def build(nc, a, out, stop=99):
    ctx = ExitStack()
    with ctx:
        def sb(name, shape, dt=F32):
            return ctx.enter_context(nc.sbuf_tensor(name, shape, dt))

        def sem(name):
            return ctx.enter_context(nc.semaphore(name))

        arena = sb("arena", [P, 45056])
        late = sb("late", [P, 4096])
        ident = sb("ident", [P, P])
        ones = sb("ones", [P, P])
        iota = sb("iota", [P, P])
        par = sb("par", [P, 512])
        eps_col = sb("eps_col", [P, 1])
        cact = sb("cact", [P, KT])
        mod = sb("mod", [P, 48])
        w1s = sb("w1s", [P, KT])
        lbc = sb("lbc", [P, 4, HEADS])
        rms_t = sb("rms_t", [P, 2, T])
        slt = sb("slt", [P, 3, T])
        carrier = sb("carrier", [P, 64])
        gact = sb("gact", [P, 2, T])

        def slab(n):
            return arena[:, n * 4096:(n + 1) * 4096].rearrange("p (k t) -> p k t", t=T)

        ring = [arena[:, s * SLOT:(s + 1) * SLOT] for s in range(2)]
        peer_ring = [arena[:, s * PEER_SLOT:(s + 1) * PEER_SLOT].rearrange("p (c d) -> p c d", d=D)
                     for s in range(2)]
        keys_rows = arena[:, 9 * 4096:9 * 4096 + 2048].rearrange("p (s n) -> p s n", n=P)
        G = arena[:, 2 * 4096:10 * 4096].rearrange("p (e t) -> p e t", t=T)
        XT, HA, HB, MG = slab(4), slab(5), slab(6), slab(7)
        HB2 = HB
        WK, WK2 = slab(8), slab(9)
        hT = slab(10)
        wk = arena[:, 8 * 4096:10 * 4096]

        ada_acc = [wk[:, 512 + n * 512:1024 + n * 512] for n in range(2)]
        mod_rows = wk[0:48, 1536:1664]
        mod_row = wk[0:1, 2048:2048 + 3 * D]
        dw0 = 6 * 4096

        def dw(at, n):
            return arena[:, dw0 + at:dw0 + at + n]

        def words(at, n):
            return wk[:, at:at + n]

        xrow = arena[:, 5 * 4096:6 * 4096].rearrange("p (c d) -> p c d", d=D)
        vbias = arena[0:1, 7 * 4096:7 * 4096 + VW]
        spread = arena[0:8, 9 * 4096:10 * 4096].rearrange("p (a h t) -> p a h t", a=2, t=T)
        xout = arena[:, 6 * 4096:7 * 4096].rearrange("p (c d) -> p c d", d=D)
        pack = words(0, 512).rearrange("p (k c) -> p k c", c=128)
        causal_mask = late[:, 896:1024]
        masks = late[:, 0:896].rearrange("p (l t) -> p l t", t=P)
        wg = late[:, 1024:1280].rearrange("p (k c) -> p k c", c=16)
        wg2 = late[:, 1280:1536].rearrange("p (k c) -> p k c", c=16)
        gbias = late[0:8, 1536:1544]
        colT = late[:, 1552:1600].rearrange("p (a c h) -> p a c h", a=3, c=TT)
        g8 = late[0:8, 1664:1664 + 8 * T].rearrange("p (a t) -> p a t", t=T)

        banks = [ctx.enter_context(nc.psum_tensor(f"bank{n}", [P, 512], F32)) for n in range(8)]
        xkeep = nc.dram_tensor("xkeep", [P, KT, T], F32, kind="Internal").ap()

        landed = [sem("slot0_landed"), sem("slot1_landed")]
        params_in = sem("params_in")
        x_in = sem("x_in")
        keys_in = sem("keys_in")
        vbias_in = sem("vbias_in")
        kept = sem("kept")
        x_back = sem("x_back")
        out_done = sem("out_done")
        consts = sem("consts")
        masks_done = sem("masks_done")
        tile_done = sem("tile_done")
        tile_evac = sem("tile_evac")
        act_step = sem("act_step")
        dve_step = sem("dve_step")
        pool_step = sem("pool_step")
        pads_done = sem("pads_done")
        c_ready = sem("c_ready")
        ada_part = sem("ada_part")
        mod_moved = sem("mod_moved")
        mod_turned = sem("mod_turned")
        mod_ready = sem("mod_ready")
        squares = sem("squares")
        ss_ready = sem("ss_ready")
        rms_ready = sem("rms_ready")
        normed = sem("normed")
        shifted = sem("shifted")
        conv_done = sem("conv_done")
        gates_mm = sem("gates_mm")
        gates_abs = sem("gates_abs")
        gates_log = sem("gates_log")
        gates_rows = sem("gates_rows")
        gates_tp = sem("gates_tp")
        gates_done = sem("gates_done")
        scores_ready = sem("scores_ready")
        expo_ready = sem("expo_ready")
        exp_done = sem("exp_done")
        floor_done = sem("floor_done")
        causal_done = sem("causal_done")
        att_ready = sem("att_ready")
        num_ready = sem("num_ready")
        h_ready = sem("h_ready")
        hsq_ready = sem("hsq_ready")
        hss_ready = sem("hss_ready")
        hrms_ready = sem("hrms_ready")
        mlstm_done = sem("mlstm_done")
        merge_done = sem("merge_done")
        resid_done = sem("resid_done")
        decay_in = sem("decay_in")
        decay_exp = sem("decay_exp")
        x_levels = sem("x_levels")
        decayed = sem("decayed")
        gram_done = sem("gram_done")
        gram_taken = sem("gram_taken")
        att_clear = sem("att_clear")
        o_ready = sem("o_ready")
        osq_ready = sem("osq_ready")
        oss_ready = sem("oss_ready")
        orms_ready = sem("orms_ready")
        hgrn_done = sem("hgrn_done")
        conv_in = sem("conv_in")
        silu_done = sem("silu_done")
        qk_sq = sem("qk_sq")
        qk_ss = sem("qk_ss")
        qk_rms = sem("qk_rms")
        qk_unit = sem("qk_unit")
        v_turned = sem("v_turned")
        bv_ready = sem("bv_ready")
        kk_ready = sem("kk_ready")
        bc_ready = sem("bc_ready")
        dex_ready = sem("dex_ready")
        dex_done = sem("dex_done")
        dmask_done = sem("dmask_done")
        mt_ready = sem("mt_ready")
        lv_mask = sem("lv_mask")
        lv_cd = sem("lv_cd")
        lv_cd_copied = sem("lv_cd_copied")
        lv_dd = sem("lv_dd")
        lv_new = sem("lv_new")
        u1_mm = sem("u1_mm")
        u1_copied = sem("u1_copied")
        r2_mm = sem("r2_mm")
        r2_ready = sem("r2_ready")
        u2_mm = sem("u2_mm")
        u2_copied = sem("u2_copied")
        delta_done = sem("delta_done")
        keyscore = sem("keyscore")
        keyscore_copied = sem("keyscore_copied")
        picked = sem("picked")
        best_in = sem("best_in")
        best_exp = sem("best_exp")
        slots_ready = sem("slots_ready")
        onehot = sem("onehot")
        gmat = sem("gmat")
        gmat_out = sem("gmat_out")
        turn_done = sem("turn_done")
        turn_out_act = sem("turn_out_act")
        turn_out_dve = sem("turn_out_dve")
        hid_done = sem("hid_done")
        gelu_done = sem("gelu_done")
        wmul = sem("wmul")
        zero_done = sem("zero_done")
        y_done = sem("y_done")
        y_added = sem("y_added")

        SETUP, ADA = 12, 12
        FINAL_TILES = SETUP + ADA + 3 * 64 + 16 + 32 + 24 + 16 + 4 + 16 + 2

        def b3(ap, n):
            return ap.unsqueeze(1).broadcast_to([ap.shape[0], n, ap.shape[1]])

        def w3(f, at, k, t=T):
            return f(at, k * t).rearrange("p (k t) -> p k t", t=t)

        upd = w3(words, 0, 8)
        sg, yy, prod = w3(words, 0, 4), w3(words, 1024, 4), w3(words, 2048, 4)
        cv, cu, cy = w3(words, 0, 8), w3(words, 2048, 2, T + 2), w3(words, 2564, 2)
        mqk, mv, mo, mz = (w3(words, n * 512, 2) for n in range(4))
        mE, mS, mfloor = words(2048, 384), words(2432, 384), words(2816, T)
        mden, mh = w3(words, 3072, 2), w3(words, 3584, 2)
        msq = arena[:, 7 * 4096 + 2048:7 * 4096 + 2560].rearrange("p (k t) -> p k t", t=T)
        hq, hv, hz = dw(0, T), w3(dw, T, 2, P), dw(512, T)
        hsig, hneg, hlf, hk, hb = (dw(768 + n * T, T) for n in range(5))
        hE, hX = w3(dw, 2048, 8), w3(dw, 4096, 8)
        hatt = w3(dw, 6144, 3, P)
        zrow, hsq, hon = dw(6528, T), dw(6784, T), dw(7040, T)
        draw, dy, dc = w3(dw, 0, 4, T + 3), w3(dw, 1036, 4), w3(dw, 2060, 4)
        dsq, drt, dqk = w3(dw, 3084, 2), w3(dw, 3596, 2), w3(dw, 4108, 2)
        dz = w3(dw, 4620, 2)
        dbv = w3(dw, 5132, 4, P)
        dW, dA, dM = w3(dw, 6028, 6, P), w3(dw, 6796, 6, P), w3(dw, 7564, 6, P)
        dC, dD, dcd = w3(dw, 8332, 4, P), w3(dw, 8844, 8, P), w3(dw, 9868, 4, P)
        du, dr2 = w3(dw, 10380, 4, P), w3(dw, 10892, 2, P)
        don, dosq = w3(dw, 11148, 2), w3(dw, 11660, 2)
        eq_h = dw(0, 1024).rearrange("p (a s t) -> p a s t", a=2, s=2)
        ekey = w3(dw, 1024, 16, P)
        esc = dw(3072, 1024).rearrange("p (a c s n) -> p a c s n", a=2, c=2, s=2)
        esc2 = dw(4096, 512).rearrange("p (c s n) -> p c s n", c=2, s=2)
        ev = dw(4608, 64).rearrange("p (c s k) -> p c s k", c=2, s=2)
        ei = dw(4672, 64).bitcast(U32).rearrange("p (c s k) -> p c s k", c=2, s=2)
        eif = dw(4736, 64).rearrange("p (c s k) -> p c s k", c=2, s=2)
        ecand, ecand2 = w3(dw, 4800, 2), w3(dw, 5312, 2)
        ebv, ebp = w3(dw, 5824, 2, 16), dw(5856, 32).bitcast(U32).rearrange("p (c k) -> p c k", k=16)
        ehl = dw(5888, 64).bitcast(U32).rearrange("p (s c k) -> p s c k", s=2, k=16)
        ehf = dw(5952, 64).rearrange("p (s c k) -> p s c k", s=2, k=16)
        eeq = dw(6016, 1024).rearrange("p (s c k j) -> p s c k j", s=2, c=2, k=16)
        e12 = dw(7040, 512).rearrange("p (s c n) -> p s c n", s=2, n=P)
        ebest, eexp, esum = w3(dw, 7552, 2, P), w3(dw, 7808, 2, P), dw(8064, 32)
        oh = late[:, 0:2048].rearrange("p (s q w n) -> p s q w n", s=2, q=4, w=2)
        UT = late[:, :].rearrange("p (s k n) -> p s k n", s=2, k=KT)
        MIX = HA

        def rows_of(w):
            return w.rearrange("(k p) n -> p k n", p=P)

        w_ada = rows_of(a["w_ada"][0])
        w_in = rows_of(a["w_in"][0])
        w_pa = rows_of(a["w_proj_a"][0])
        w_pb = rows_of(a["w_proj_b"][0])
        w_out = rows_of(a["w_out"][0])
        w_in2 = rows_of(a["w_in_2"][0])
        w_out2 = rows_of(a["w_out_2"][0])
        w_q = rows_of(a["peer_w_query_2"][0].rearrange("d h k -> d (h k)"))
        p_u = a["peer_u_2"][0].rearrange("(c e p) d -> c p e d", e=2, p=P)
        p_v = a["peer_v_2"][0].rearrange("(c e p) d -> c p e d", e=2, p=P)

        block = ctx.enter_context(nc.Block())

        @block.sync
        def _(sp):
            tiles = Count(tile_done, "sp tiles")
            tiles.n = 12

            def load(slot, pieces, makes, prev, width=512):
                if prev is not None:
                    sp.wait_ge(tile_done, tiles.value(-prev))
                dst = ring[slot][:, 0:KT * width].rearrange("p (k c) -> p k c", c=width)
                at = 0
                for src, off, n in pieces:
                    sp.dma_start(dst[:, :, at:at + n], src[:, :, ds(off, n)]).then_inc(landed[slot], 16)
                    at += n
                tiles.up(makes)

            load(0, [(w_ada, 0, 512)], 1, None)
            load(1, [(w_ada, 512, 512)], 1, None)
            with rounds(sp, 5, (tiles, 2)) as i:
                load(0, [(w_ada, 1024 + i * 1024, 512)], 1, 1)
                load(1, [(w_ada, 1536 + i * 1024, 512)], 1, 1)
            sp.dma_start(vbias, a["b_in"][0][OFF_V:OFF_V + VW].rearrange("(o n) -> o n", o=1)).then_inc(vbias_in, 16)
            sp.wait_ge(tile_evac, SETUP + ADA)
            sp.dma_start(mod_rows, mod_row.rearrange("o (r c) -> o r c", c=128)).then_inc(mod_moved, 16)

            def conv_chunks(j, prev):
                load(0, [(w_in, OFF_U + j * 256, 256), (w_in, OFF_C + j * 256, 256)], 4, prev)
                load(1, [(w_in, OFF_B + j * 256, 256), (w_in, OFF_ZB + j * 256, 256)], 4, 4)

            conv_chunks(0, 1)
            with rounds(sp, 7, (tiles, 8)) as j:
                conv_chunks(j + 1, 4)
            with rounds(sp, 8, (tiles, 8)) as h:
                load(0, [(w_in, h * 128, 128), (w_in, OFF_K + h * 128, 128),
                         (w_in, OFF_V + h * 256, 256)], 4, 4)
                load(1, [(w_in, OFF_O + h * 256, 256), (w_in, OFF_Z + h * 256, 256)], 4, 4)
            with rounds(sp, 8, (tiles, 8)) as j:
                load(0, [(w_in, OFF_GA + j * 256, 256), (w_pa, j * 256, 256)], 4, 4)
                load(1, [(w_in, OFF_GB + j * 256, 256), (w_pb, j * 256, 256)], 4, 4)
            with rounds(sp, 2, (tiles, 8)) as j:
                load(0, [(w_out, j * 1024, 512)], 4, 4)
                load(1, [(w_out, j * 1024 + 512, 512)], 4, 4)
            with rounds(sp, 4, (tiles, 8)) as i:
                for s in range(2):
                    load(s, [(w_in2, i * 256 + (off + s * 128), 128) for off in (0, OFF2_F, OFF2_I, OFF2_G)], 4, 4)

            def delta_chunks(g, prev):
                load(0, [(w_in2, OFF2_BQ + g * 128, 128), (w_in2, OFF2_BK + g * 128, 128),
                         (w_in2, OFF2_BV + g * 256, 128)], 3, prev, 384)
                load(1, [(w_in2, OFF2_BV + g * 256 + 128, 128),
                         (w_in2, OFF2_BZ + g * 256, 256)], 3, 3, 384)

            delta_chunks(0, 4)
            with rounds(sp, GROUPS - 1, (tiles, 6)) as g:
                delta_chunks(g + 1, 3)

            def out2_chunks(j, prev):
                load(0, [(w_out2, j * 1024, 512)], 4, prev)
                load(1, [(w_out2, j * 1024 + 512, 512)], 4, 4)

            out2_chunks(0, 3)
            out2_chunks(1, 4)

            load(0, [(w_q, 0, 256)], 2, 4, 256)
            sp.wait_ge(normed, 4)
            sp.dma_start(keys_rows, a["peer_sub_keys_2"][0].rearrange("s h n k -> n (s h) k")).then_inc(keys_in, 16)
            tiles.n += 4
            load(1, [(w_q, 256, 256)], 2, 6, 256)
            with rounds(sp, 3, (tiles, 4)) as i:
                load(0, [(w_q, (i + 1) * 512, 256)], 2, 2, 256)
                load(1, [(w_q, (i + 1) * 512 + 256, 256)], 2, 2, 256)
            sp.dma_start(xkeep, XT).then_inc(kept, 16)

            turned = Count(turn_done, "sp turned")

            def load_u(c, s, first):
                if not first:
                    sp.wait_ge(turn_done, turned.value(-2 * 4))
                sp.dma_start(peer_ring[s], p_u[ds(c, 1)].rearrange("o p e d -> p (o e) d")).then_inc(landed[s], 16)
                turned.up(8)
            sp.wait_ge(tile_done, tiles.value())
            load_u(0, 0, True)
            load_u(1, 1, True)
            with rounds(sp, 31, (turned, 16)) as i:
                load_u(2 * i + 2, 0, False)
                load_u(2 * i + 3, 1, False)
            yc = Count(y_done, "sp y")

            def load_v(c, s, first):
                if first:
                    sp.wait_ge(turn_done, turned.value(-8 * (1 - s)))
                else:
                    sp.wait_ge(y_done, yc.value(-1))
                sp.dma_start(peer_ring[s], p_v[ds(c, 1)].rearrange("o p e d -> p (o e) d")).then_inc(landed[s], 16)
                yc.up(1)
            load_v(0, 0, True)
            load_v(1, 1, True)
            with rounds(sp, 31, (yc, 2)) as i:
                load_v(2 * i + 2, 0, False)
                load_v(2 * i + 3, 1, False)
            sp.wait_ge(y_done, yc.value())
            sp.wait_ge(kept, 16)
            sp.dma_start(XT, xkeep).then_inc(x_back, 16)
            for c in range(TT):
                sp.wait_ge(tile_evac, FINAL_TILES + 4 * (c + 1))
                sp.dma_start(out[0][c * P:(c + 1) * P, :], xout[:, c, :]).then_inc(out_done, 16)
            sp.wait_ge(out_done, 16 * TT)

        @block.tensor
        def _(pe):
            tiles = Count(tile_done, "pe tiles")
            land = [Count(landed[0], "pe slot 0"), Count(landed[1], "pe slot 1")]

            def free_bank(lag=4):
                if isinstance(tiles.lead, int) and tiles.n < lag:
                    return
                pe.wait_ge(tile_evac, tiles.value(1 - lag))

            def arrive(slot, pieces):
                pe.wait_ge(landed[slot], land[slot].up(16 * pieces))

            def chunk(slot, width=512):
                return ring[slot][:, 0:KT * width].rearrange("p (k c) -> p k c", c=width)

            def feature_tile(bank, w, c0, moving, lag=4):
                free_bank(lag)
                for k in range(KT):
                    mm = nc.tensor.matmul(banks[bank][:, 0:T], w[:, k, c0:c0 + P], moving[:, k, :],
                                          start=(k == 0), stop=(k == KT - 1))
                mm.then_inc(tile_done, 1)
                tiles.up()

            def turn(bank, at, src):
                return nc.tensor.transpose(banks[bank][0:src.shape[1], at:at + src.shape[0]], src,
                                           ident[0:src.shape[0], 0:src.shape[0]])

            def mean_square(n):
                pe.wait_ge(squares, 4 * n)
                for k in range(KT):
                    mm = nc.tensor.matmul(banks[5][:, 0:T], ones[:, :], HB2[:, k, :],
                                          start=(k == 0), stop=(k == KT - 1))
                mm.then_inc(ss_ready, 1)

            pe.wait_ge(consts, 1)
            pe.wait_ge(x_in, 16)
            for m in range(8):
                free_bank()
                for q in range(4):
                    k, c = 2 * m + q // 2, q % 2
                    mm = turn(m % 4, q * P, xrow[:, c, k * P:(k + 1) * P])
                mm.then_inc(tile_done, 1)
                tiles.up()
            pe.wait_ge(params_in, 16 * N_PARAMS)
            for m, rows in enumerate(PACK_ROWS):
                free_bank()
                turn(m, 0, pack[0:rows, m, :]).then_inc(tile_done, 1)
                tiles.up()

            pe.wait_ge(c_ready, 1)
            with rounds(pe, 6, (tiles, 2), (land[0], 16), (land[1], 16)) as i:
                for s in range(2):
                    arrive(s, 1)
                    w = chunk(s)
                    free_bank(2)
                    for k in range(ADA_DVE, KT):
                        nc.tensor.matmul(banks[s][0:1, :], cact[:, k:k + 1], w[:, k, :],
                                         start=(k == ADA_DVE), stop=False)
                    pe.wait_ge(ada_part, 2 * i + (s + 1))
                    nc.tensor.matmul(banks[s][0:1, :], ones[:, 0:1], ada_acc[s],
                                     start=False, stop=True).then_inc(tile_done, 1)
                    tiles.up()
            mean_square(1)
            pe.wait_ge(mod_moved, 16)
            nc.tensor.transpose(banks[4][:, 0:48], mod_rows, ident[0:48, 0:48]).then_inc(mod_turned, 1)

            pe.wait_ge(shifted, 1)
            for g in range(2):
                for k in range(KT):
                    mm = nc.tensor.matmul(banks[4 + g][0:8, 0:T], wg[:, k, 8 * g:8 * g + 8], hT[:, k, :],
                                          start=(k == 0), stop=(k == KT - 1))
                mm.then_inc(gates_mm, 1)
            pe.wait_ge(tile_evac, tiles.value())

            with rounds(pe, 8, (tiles, 8), (land[0], 32), (land[1], 32)) as j:
                for s in range(2):
                    arrive(s, 2)
                    for m in range(4):
                        feature_tile(m, chunk(s), m * P, hT)

            pe.wait_ge(gates_rows, 1)
            for c in range(TT):
                mm = turn(6, c * 8, g8[:, 5, c * P:(c + 1) * P])
            mm.then_inc(gates_tp, 1)
            pe.wait_ge(vbias_in, 16)
            pe.wait_ge(gates_done, 1)
            with rounds(pe, 8, (tiles, 8), (land[0], 48), (land[1], 32)) as h:
                arrive(0, 3)
                w = chunk(0)
                for m in range(2):
                    feature_tile(m, w, m * P, hT)
                for c in range(TT):
                    free_bank()
                    for k in range(KT):
                        nc.tensor.matmul(banks[2 + c][:, 0:T], hT[:, k, c * P:(c + 1) * P],
                                         w[:, k, 256:512], start=(k == 0), stop=False)
                    mm = nc.tensor.matmul(banks[2 + c][:, 0:T], ones[0:1, :], vbias[:, ds(h * 256, 256)],
                                          start=False, stop=True)
                    mm.then_inc(tile_done, 1)
                    tiles.up()
                pe.wait_ge(tile_evac, tiles.value(-2))
                pe.wait_ge(mlstm_done, 1 + h)
                nc.tensor.matmul(banks[4][:, 0:T], mqk[:, 1, 0:P], mqk[:, 0, :], start=True, stop=True)
                nc.tensor.matmul(banks[4][:, T:T + P], mqk[:, 1, P:T], mqk[:, 0, P:T], start=True, stop=True)
                for n in range(2):
                    mm = nc.tensor.matmul(banks[6 + n][:, 0:T], ones[0:8, :], spread[:, n, ds(h, 1), :].rearrange("p o t -> p (o t)"),
                                          start=True, stop=True)
                mm.then_inc(scores_ready, 1)
                arrive(1, 2)
                for m in range(2):
                    feature_tile(m, chunk(1), m * P, hT)
                pe.wait_ge(att_ready, h + 1)
                pe.wait_ge(tile_evac, tiles.value(-2))
                for n in range(2):
                    o = banks[5][:, n * T:(n + 1) * T]
                    nc.tensor.matmul(o, mv[:, 0, n * P:(n + 1) * P], mS[:, 0:T], start=True, stop=False)
                    nc.tensor.matmul(o[:, P:T], mv[:, 1, n * P:(n + 1) * P], mS[:, T:T + P],
                                     start=False, stop=True)
                nc.tensor.matmul(banks[6][:, 0:T], ones[:, :], mS[:, 0:T], start=True, stop=False)
                nc.tensor.matmul(banks[6][:, P:T], ones[:, :], mS[:, T:T + P],
                                 start=False, stop=True).then_inc(num_ready, 1)
                for m in range(2, 4):
                    feature_tile(m, chunk(1), m * P, hT)
                pe.wait_ge(hsq_ready, h + 1)
                for n in range(2):
                    mm = nc.tensor.matmul(banks[7][:, 0:T], ones[:, :], msq[:, n, :],
                                          start=(n == 0), stop=(n == 1))
                mm.then_inc(hss_ready, 1)

            pe.wait_ge(mlstm_done, 1 + 8)
            pe.wait_ge(conv_done, 1 + 8)
            with rounds(pe, 8, (tiles, 8), (land[0], 32), (land[1], 32)) as j:
                for s, branch in enumerate((HA, HB)):
                    arrive(s, 2)
                    for m in range(4):
                        feature_tile(m, chunk(s), m * P, hT if m < 2 else branch)

            def out_projection(moving):
                with rounds(pe, 2, (tiles, 8), (land[0], 16), (land[1], 16)):
                    for s in range(2):
                        arrive(s, 1)
                        for m in range(4):
                            feature_tile(m, chunk(s), m * P, moving)

            pe.wait_ge(merge_done, 1 + 8)
            out_projection(MG)
            mean_square(2)
            mean_square(3)

            pe.wait_ge(normed, 3)
            with rounds(pe, 4, (tiles, 8), (land[0], 64), (land[1], 64)) as i:
                for s in range(2):
                    head = 2 * i + s
                    arrive(s, 4)
                    w = chunk(s)
                    feature_tile(0, w, 0, hT)
                    feature_tile(1, w, P, hT)
                    free_bank()
                    for c in range(TT):
                        for k in range(KT):
                            mm = nc.tensor.matmul(banks[2][:, c * P:(c + 1) * P], hT[:, k, c * P:(c + 1) * P],
                                                  w[:, k, T:T + P], start=(k == 0), stop=(k == KT - 1))
                    mm.then_inc(tile_done, 1)
                    tiles.up()
                    feature_tile(3, w, 3 * P, hT)
                    pe.wait_ge(x_levels, head + 1)
                    for l in range(9):
                        b = banks[4 + l % 4]
                        if l >= 4:
                            pe.wait_ge(gram_taken, head * 9 + l - 3)
                        if l == 0:
                            mm = nc.tensor.matmul(b[:, 0:P], hX[:, 7, 0:P], hX[:, 7, P:T], start=True, stop=True)
                        else:
                            x, y = (hX[:, l - 1, :], hX[:, l - 1, :]) if l < 8 else (hk, hq)
                            for c in range(TT):
                                mm = nc.tensor.matmul(b[:, c * P:(c + 1) * P], x[:, c * P:(c + 1) * P],
                                                      y[:, c * P:(c + 1) * P], start=True, stop=True)
                        mm.then_inc(gram_done, 1)
                    pe.wait_ge(gram_taken, head * 9 + 9)
                    pe.wait_ge(tile_evac, tiles.value(-1))
                    nc.tensor.matmul(banks[5][:, 0:T], hv[:, 0, :], hatt[:, 0:2, :].rearrange("p a t -> p (a t)"), start=True, stop=False)
                    nc.tensor.matmul(banks[5][:, P:T], hv[:, 1, :], hatt[:, 2, :],
                                     start=False, stop=True).then_inc(o_ready, 1)
                    pe.wait_ge(osq_ready, head + 1)
                    nc.tensor.matmul(banks[6][:, 0:T], ones[:, :], hsq, start=True, stop=True).then_inc(oss_ready, 1)

            pe.wait_ge(hgrn_done, 1 + 8)
            for g in range(2):
                for k in range(KT):
                    mm = nc.tensor.matmul(banks[4 + g][0:8, 0:T], wg2[:, k, 8 * g:8 * g + 8], hT[:, k, :],
                                          start=(k == 0), stop=(k == KT - 1))
                mm.then_inc(gates_mm, 1)
            pe.wait_ge(gates_rows, 2)
            for r, row in enumerate((4, 0)):
                for c in range(TT):
                    mm = turn(6, (r * TT + c) * 8, g8[:, row, c * P:(c + 1) * P])
            mm.then_inc(gates_tp, 1)
            pe.wait_ge(gates_done, 2)

            with rounds(pe, GROUPS, (tiles, 6), (land[0], 48), (land[1], 32)) as g:
                arrive(0, 3)
                for m in range(3):
                    feature_tile(m, chunk(0, 384), m * P, hT, lag=2)
                arrive(1, 2)
                for m in range(3):
                    feature_tile((3 + m) % 4, chunk(1, 384), m * P, hT, lag=2)
                pe.wait_ge(qk_sq, g + 1)
                for n in range(2):
                    mm = nc.tensor.matmul(banks[4][:, n * T:(n + 1) * T], ones[:, :], dsq[:, n, :], start=True, stop=True)
                mm.then_inc(qk_ss, 1)
                for n in range(2):
                    for c in range(TT):
                        mm = turn(5, (n * TT + c) * P, dc[:, 2 + n, c * P:(c + 1) * P])
                mm.then_inc(v_turned, 1)
                pe.wait_ge(qk_unit, g + 1)
                for n in range(2):
                    b, y = banks[6 + n], dqk[:, 1 - n, :]
                    nc.tensor.matmul(b[:, 0:T], dqk[:, 1, 0:P], y, start=True, stop=True)
                    mm = nc.tensor.matmul(b[:, T:T + P], dqk[:, 1, P:T], y[:, P:T], start=True, stop=True)
                mm.then_inc(kk_ready, 1)
                pe.wait_ge(bv_ready, g + 1)
                for n in range(2):
                    for r in range(2):
                        mm = nc.tensor.matmul(banks[4 + n][:, r * T:(r + 1) * T], ones[0:8, :],
                                              spread[:, r, ds(2 * g + n, 1), :].rearrange("p o t -> p (o t)"), start=True, stop=True)
                mm.then_inc(bc_ready, 1)
                for l in range(7):
                    step = g * 7 + l
                    pe.wait_ge(lv_mask, step + 1)
                    for q in range(4):
                        mm = nc.tensor.matmul(banks[4][:, q * P:(q + 1) * P], dC[:, q, :], dD[:, q, :], start=True, stop=True)
                    mm.then_inc(lv_cd, 1)
                    pe.wait_ge(lv_cd_copied, step + 1)
                    for q in range(4):
                        nc.tensor.matmul(banks[5][:, q * P:(q + 1) * P], dD[:, 4 + q, :], dcd[:, q, :], start=True, stop=True)
                    for q in range(4):
                        mm = nc.tensor.matmul(banks[6][:, q * P:(q + 1) * P], dcd[:, q, :], dD[:, 4 + q, :], start=True, stop=True)
                    mm.then_inc(lv_dd, 1)
                pe.wait_ge(lv_new, g + 1)
                for n in range(2):
                    mm = nc.tensor.matmul(banks[4][:, n * P:(n + 1) * P], dD[:, 4 + 2 * n, :], dbv[:, 2 * n, :], start=True, stop=True)
                mm.then_inc(u1_mm, 1)
                pe.wait_ge(u1_copied, g + 1)
                for n in range(2):
                    mm = nc.tensor.matmul(banks[5][:, n * P:(n + 1) * P], dM[:, 3 * n + 1, :], du[:, 2 * n, :], start=True, stop=True)
                mm.then_inc(r2_mm, 1)
                pe.wait_ge(r2_ready, g + 1)
                for n in range(2):
                    mm = nc.tensor.matmul(banks[6][:, n * P:(n + 1) * P], dD[:, 5 + 2 * n, :], dr2[:, n, :], start=True, stop=True)
                mm.then_inc(u2_mm, 1)
                pe.wait_ge(u2_copied, g + 1)
                for n in range(2):
                    o = banks[7][:, n * T:(n + 1) * T]
                    nc.tensor.matmul(o, du[:, 2 * n, :], dA[:, 3 * n:3 * n + 2, :].rearrange("p a t -> p (a t)"), start=True, stop=False)
                    mm = nc.tensor.matmul(o[:, P:T], du[:, 2 * n + 1, :], dA[:, 3 * n + 2, :], start=False, stop=True)
                mm.then_inc(o_ready, 1)
                pe.wait_ge(osq_ready, 8 + g + 1)
                for n in range(2):
                    mm = nc.tensor.matmul(banks[4][:, n * T:(n + 1) * T], ones[:, :], dosq[:, n, :], start=True, stop=True)
                mm.then_inc(oss_ready, 1)

            pe.wait_ge(delta_done, 1 + GROUPS)
            pe.wait_ge(tile_evac, tiles.value())
            out_projection(MIX)
            mean_square(4)

            pe.wait_ge(keys_in, 16)
            for m in range(4):
                free_bank()
                for q in range(4):
                    mm = turn(m, q * P, keys_rows[:, 4 * m + q, :])
                mm.then_inc(tile_done, 1)
                tiles.up()
            pe.wait_ge(normed, 4)
            with rounds(pe, 4, (tiles, 4), (land[0], 16), (land[1], 16)) as i:
                for s in range(2):
                    arrive(s, 1)
                    for m in range(2):
                        feature_tile(2 * s + m, chunk(s, 256), m * P, hT)
                    pe.wait_ge(tile_evac, tiles.value())
                    pe.wait_ge(keyscore_copied, 1 + 2 * i + s)
                    for c in range(TT):
                        for half in range(2):
                            mm = nc.tensor.matmul(banks[4 + s][:, (2 * c + half) * P:(2 * c + half + 1) * P],
                                                  eq_h[:, s, half, c * P:(c + 1) * P],
                                                  ekey[:, ds(2 * i + (s + 8 * half), 1), :].rearrange("p o n -> p (o n)"),
                                                  start=True, stop=True)
                    mm.then_inc(keyscore, 1)

            pe.wait_ge(slots_ready, 1)
            for c in range(TT):
                free_bank()
                for r, src in enumerate((e12[:, 0, c, :], e12[:, 1, c, :], eexp[:, c, :])):
                    mm = turn(c, r * P, src)
                mm.then_inc(tile_done, 1)
                tiles.up()

            def gate_products(i, first):
                for s in range(2):
                    n = 2 * i + s
                    pe.wait_ge(onehot, n + 1)
                    if not first:
                        pe.wait_ge(gmat_out, n - 1)
                    for q in range(4):
                        mm = nc.tensor.matmul(banks[4 + s][:, q * P:(q + 1) * P], oh[:, s, q, 1, :], oh[:, s, q, 0, :],
                                              start=True, stop=True)
                    mm.then_inc(gmat, 1)

            gate_products(0, True)
            with rounds(pe, T // 8 - 1) as i:
                gate_products(i + 1, False)
            pe.wait_ge(gmat_out, T // 4)

            def turn_bank(e, u, m, first):
                if not first:
                    pe.wait_ge(*(turn_out_act, 2 * e - 1 + m // 2) if m % 2 == 0 else (turn_out_dve, 2 * e - 1 + m // 2))
                for q in range(4):
                    mm = turn(m, q * P, peer_ring[u // 2][:, u % 2, (4 * m + q) * P:(4 * m + q + 1) * P])
                mm.then_inc(turn_done, 1)

            def hidden(i, first):
                arrive(0, 1)
                for m in range(4):
                    turn_bank(4 * i, 0, m, first)
                for u in range(4):
                    e = 4 * i + u
                    if u == 1:
                        arrive(1, 1)
                    if not (first and u < 2):
                        pe.wait_ge(gelu_done, e - 1)
                    for m in range(4):
                        pe.wait_ge(turn_out_act if m % 2 == 0 else turn_out_dve, 2 * e + m // 2 + 1)
                        for k in range(4 * m, 4 * m + 4):
                            mm = nc.tensor.matmul(banks[4 + u % 2][:, 0:T], UT[:, u % 2, k, :], hT[:, k, :],
                                                  start=(k == 0), stop=(k == KT - 1))
                        if m == 3:
                            mm.then_inc(hid_done, 1)
                        if u < 3:
                            turn_bank(e + 1, u + 1, m, False)

            hidden(0, True)
            with rounds(pe, N_KEYS // 4 - 1, (land[0], 16), (land[1], 16)) as i:
                hidden(i + 1, False)

            pe.wait_ge(zero_done, 1)
            pe.wait_ge(wmul, N_KEYS)
            for b in range(8):
                nc.tensor.matmul(banks[b][:, :], late[:, 512:640], late[:, 0:512], start=True, stop=False, skip_group_check=True)
            with rounds(pe, N_KEYS // 4, (land[0], 16), (land[1], 16)) as i:
                for s in range(2):
                    arrive(s, 1)
                    for e in range(2):
                        for k in range(KT):
                            mm = nc.tensor.matmul(banks[k // 2][:, (k % 2) * T:(k % 2 + 1) * T],
                                                  peer_ring[s][:, e, k * P:(k + 1) * P],
                                                  G[:, ds(4 * i + (2 * s + e), 1), :].rearrange("p o t -> p (o t)"),
                                                  start=False, stop=False, skip_group_check=True)
                    mm.then_inc(y_done, 1)

            mean_square(5)
            pe.wait_ge(normed, 5)
            for n in range(8):
                free_bank()
                for q in range(4):
                    mm = turn(n % 4, q * P, hT[:, 4 * (n % 4) + q, (n // 4) * P:(n // 4 + 1) * P])
                mm.then_inc(tile_done, 1)
                tiles.up()

        @block.scalar
        def _(act):
            tiles = Count(tile_evac, "act tiles")
            steps = Count(act_step, "act steps")

            def evac(dst, src, func=ACT.Copy, bias=None, scale=None):
                act.wait_ge(tile_done, tiles.up())
                kw = {}
                if bias is not None:
                    kw["bias"] = bias
                if scale is not None:
                    kw["scale"] = scale
                nc.scalar.activation(dst, src, func, **kw).then_inc(tile_evac, 1)

            def link(ins):
                ins.then_inc(act_step, 1)
                act.wait_ge(act_step, steps.up())

            def squares_of(src):
                for q in range(4):
                    nc.scalar.activation(HB2[:, 4 * q:4 * q + 4, :], src[:, 4 * q:4 * q + 4, :], ACT.Square).then_inc(squares, 1)

            def root(n):
                act.wait_ge(ss_ready, n)
                nc.scalar.activation(rms_t[:, 0, :], banks[5][:, 0:T], ACT.Sqrt, bias=eps_col[:, :],
                                     scale=1.0 / D).then_inc(rms_ready, 1)

            def pcol(at, n=1):
                return par[:, ds(at, n)]

            def rows128(src, dst):
                act.dma_start(dst, src).then_inc(params_in, 16)

            def r(ap):
                return ap.rearrange("(r c) -> r c", c=128)

            act.dma_start(xrow[:, :, :], a["x"][0].rearrange("(c p) d -> p c d", p=P)).then_inc(x_in, 16)
            b = a["b_in"][0]
            rows128(r(b[0:OFF_I]), pack[0:64, 0, :])
            rows128(r(a["norm1_w"][0]), pack[64:80, 0, :])
            rows128(r(a["headnorm_w"][0]), pack[80:96, 0, :])
            rows128(r(a["normf_w"]), pack[96:112, 0, :])
            rows128(r(a["attn_norm_g_2"][0]), pack[112:128, 0, :])
            rows128(r(b[OFF_U:IN_1]), pack[0:96, 1, :])
            rows128(r(a["ffn_norm_g_2"][0]), pack[96:112, 1, :])
            rows128(r(a["final_norm_g_2"]), pack[112:128, 1, :])
            rows128(a["conv_w"][0].rearrange("j (r c) -> (j r) c", c=128), pack[0:48, 2, :])
            rows128(r(a["b_ada"][0]), pack[48:96, 2, :])
            rows128(r(a["c"][0]), pack[96:112, 2, :])
            rows128(a["hgrn_norm_g_2"], pack[112:113, 2, :])
            rows128(a["gdn_norm_g_2"], pack[113:114, 2, :])
            rows128(a["gdn_conv_w_2"][0].rearrange("j (r c) -> (j r) c", c=128), pack[0:64, 3, :])
            rows128(a["hgrn_lb_logits_2"].rearrange("l h c -> (l h) c"), pack[64:80, 3, :])
            col = lambda v: v.rearrange("(h o) -> h o", o=1)
            with nc.allow_non_contiguous_dma("a few words"):
                rows128(col(b[OFF_I:OFF_I + 8]), gbias[:, 0:1])
                rows128(col(b[OFF_I + 8:OFF_I + 16]), gbias[:, 1:2])
                rows128(col(a["gdn_A_log_2"][0]), gbias[:, 2:3])
                rows128(col(a["gdn_dt_bias_2"][0]), gbias[:, 3:4])
                rows128(w_in[:, :, OFF_I:OFF_I + 16], wg[:, :, :])
                rows128(w_in2[:, :, OFF2_BB:OFF2_BB + 16], wg2[:, :, :])


            act.wait_ge(consts, 1)
            for m in range(8):
                evac(XT[:, 2 * m:2 * m + 2, :], banks[m % 4].rearrange("p (k t) -> p k t", t=T))
            for m, rows in enumerate(PACK_ROWS):
                evac(par[:, 128 * m:128 * m + rows], banks[m][:, 0:rows])
            act.wait_ge(tile_evac, tiles.value())
            nc.scalar.activation(cact[:, :], par[:, PK_C:PK_C + KT], ACT.Silu).then_inc(c_ready, 1)
            link(nc.scalar.activation(lbc[:, 0:2, :], par[:, PK_LB:PK_LB + 16].rearrange("p (l h) -> p l h", l=2), ACT.Exp))
            squares_of(XT)
            with rounds(act, 6, (tiles, 2)) as i:
                for s in range(2):
                    evac(mod_row[:, ds(1024 * i + 512 * s, 512)], banks[s][0:1, :])
            root(1)

            act.wait_ge(normed, 1)
            act.wait_ge(mod_ready, 1)
            for k in range(KT):
                ins = nc.scalar.activation(hT[:, k, :], hT[:, k, :], ACT.Identity, bias=mod[:, k:k + 1])
            ins.then_inc(shifted, 1)

            def soft(n):
                act.wait_ge(gates_abs, n)
                link(nc.scalar.activation(g8[:, 2, :], g8[:, 2, :], ACT.Exp, scale=-1.0))
                nc.scalar.activation(g8[:, 2, :], g8[:, 2, :], ACT.Ln, bias=1.0).then_inc(gates_log, 1)

            soft(1)
            with rounds(act, 8, (tiles, 8)) as j:
                act.wait_ge(conv_done, 1 + j)
                for m in range(8):
                    base = (PK_REST_B, PK_REST_B + 32, PK_REST_B + 16, PK_REST_B + 48)[m // 2]
                    evac(cv[:, m, :], banks[m % 4][:, 0:T], ACT.Identity if m < 6 else ACT.Silu,
                         bias=pcol(base + m % 2 + 2 * j))

            with rounds(act, 8, (tiles, 8)) as h:
                act.wait_ge(mlstm_done, 1 + h)
                evac(mqk[:, 0, :], banks[0][:, 0:T], ACT.Identity, bias=pcol(h + PK_QKVOZ_B))
                evac(mqk[:, 1, :], banks[1][:, 0:T], ACT.Identity, bias=pcol(h + (PK_QKVOZ_B + 8)))
                for c in range(TT):
                    evac(mv[:, c, :], banks[2 + c][:, 0:T])
                act.wait_ge(expo_ready, h + 1)
                nc.scalar.activation(mE, mE, ACT.Exp).then_inc(exp_done, 1)
                nc.scalar.activation(mfloor, banks[7][:, 0:T], ACT.Exp).then_inc(floor_done, 1)
                for m in range(2):
                    evac(mo[:, m, :], banks[m][:, 0:T], ACT.Sigmoid, bias=pcol(2 * h + (PK_QKVOZ_B + 32 + m)))
                act.wait_ge(h_ready, h + 1)
                nc.scalar.activation(msq, mh, ACT.Square).then_inc(hsq_ready, 1)
                for m in range(2):
                    evac(mz[:, m, :], banks[2 + m][:, 0:T], ACT.Silu, bias=pcol(2 * h + (PK_QKVOZ_B + 48 + m)))
                act.wait_ge(hss_ready, h + 1)
                nc.scalar.activation(mden[:, 1, :], banks[7][:, 0:T], ACT.Sqrt, bias=eps_col[:, :],
                                     scale=1.0 / 256).then_inc(hrms_ready, 1)

            with rounds(act, 8, (tiles, 8)) as j:
                act.wait_ge(merge_done, 1 + j)
                for s in range(2):
                    for m in range(2):
                        evac(sg[:, 2 * s + m, :], banks[m][:, 0:T], ACT.Sigmoid,
                             bias=pcol(2 * j + (PK_REST_B + 64 + 16 * s + m)))
                    for m in range(2):
                        evac(yy[:, 2 * s + m, :], banks[2 + m][:, 0:T])

            def residual(turns, gate):
                with rounds(act, 2, (tiles, 8)) as i:
                    act.wait_ge(resid_done, 1 + turns + i)
                    for m in range(8):
                        evac(upd[:, m, :], banks[m % 4][:, 0:T],
                             scale=mod[:, ds(8 * i + (32 + m), 1)] if gate else None)

            act.wait_ge(merge_done, 1 + 8)
            residual(0, True)
            act.wait_ge(resid_done, 1 + 2)
            squares_of(XT)
            root(2)
            act.wait_ge(normed, 2)
            squares_of(XT)
            root(3)

            with rounds(act, 4, (tiles, 8)) as i:
                for s in range(2):
                    head = 2 * i + s
                    act.wait_ge(hgrn_done, 1 + head)
                    evac(hq, banks[0][:, 0:T])
                    act.wait_ge(tile_done, tiles.value(1))
                    nc.scalar.activation(hneg, banks[1][:, 0:T], ACT.Sigmoid, scale=-1.0).then_inc(decay_in, 1)
                    evac(hsig, banks[1][:, 0:T], ACT.Sigmoid)
                    act.wait_ge(tile_evac, tiles.value())
                    nc.scalar.activation(hlf, hsig, ACT.Ln, bias=lbc[:, 2, ds(head, 1)], scale=lbc[:, 3, ds(head, 1)]).then_inc(decay_in, 1)
                    evac(hv[:, :, :], banks[2][:, 0:T].rearrange("p (c v) -> p c v", v=P))
                    act.wait_ge(decay_exp, head + 1)
                    nc.scalar.activation(hE, hE, ACT.Exp).then_inc(decayed, 1)
                    evac(hz, banks[3][:, 0:T], ACT.Silu)
                    act.wait_ge(o_ready, head + 1)
                    nc.scalar.activation(hsq, banks[5][:, 0:T], ACT.Square).then_inc(osq_ready, 1)
                    act.wait_ge(oss_ready, head + 1)
                    nc.scalar.activation(hon, banks[6][:, 0:T], ACT.Sqrt, bias=eps_col[:, :],
                                         scale=1.0 / P).then_inc(orms_ready, 1)

            act.wait_ge(gates_mm, 4)
            nc.scalar.activation(g8[:, 0, :], banks[4][0:8, 0:T], ACT.Sigmoid).then_inc(decay_in, 1)
            nc.scalar.activation(gbias[:, 4:5], gbias[:, 2:3], ACT.Exp).then_inc(decay_in, 1)
            soft(2)

            with rounds(act, GROUPS, (tiles, 6)) as g:
                act.wait_ge(delta_done, 1 + g)
                for m in range(4):
                    evac(draw[:, m, 3:T + 3], banks[m][:, 0:T])
                for m in range(2):
                    evac(dz[:, m, :], banks[m][:, 0:T], ACT.Silu)
                act.wait_ge(conv_in, g + 1)
                nc.scalar.activation(dc, dy, ACT.Silu).then_inc(silu_done, 1)
                act.wait_ge(silu_done, g + 1)
                nc.scalar.activation(dsq, dc[:, 0:2, :], ACT.Square).then_inc(qk_sq, 1)
                act.wait_ge(qk_ss, g + 1)
                nc.scalar.activation(drt, banks[4].rearrange("p (k t) -> p k t", t=T), ACT.Sqrt,
                                     bias=eps_col[:, :]).then_inc(qk_rms, 1)
                act.wait_ge(v_turned, g + 1)
                for n in range(2):
                    for c in range(TT):
                        ins = nc.scalar.activation(dbv[:, n * TT + c, :], banks[5][:, (n * TT + c) * P:(n * TT + c + 1) * P],
                                                   ACT.Copy, scale=colT[:, 2, c, ds(2 * g + n, 1)])
                ins.then_inc(bv_ready, 1)
                act.wait_ge(dex_ready, g + 1)
                nc.scalar.activation(dW, dW, ACT.Exp).then_inc(dex_done, 1)
                for l in range(7):
                    act.wait_ge(lv_cd, g * 7 + l + 1)
                    nc.scalar.activation(dcd, banks[4].rearrange("p (q t) -> p q t", t=P), ACT.Copy).then_inc(lv_cd_copied, 1)
                act.wait_ge(u1_mm, g + 1)
                nc.scalar.activation(du[:, 0:4:2, :], banks[4][:, 0:T].rearrange("p (q t) -> p q t", t=P), ACT.Copy).then_inc(u1_copied, 1)
                act.wait_ge(u2_mm, g + 1)
                nc.scalar.activation(du[:, 1:4:2, :], banks[6][:, 0:T].rearrange("p (q t) -> p q t", t=P), ACT.Copy).then_inc(u2_copied, 1)
                act.wait_ge(o_ready, 8 + g + 1)
                nc.scalar.activation(dosq, banks[7].rearrange("p (q t) -> p q t", t=T), ACT.Square).then_inc(osq_ready, 1)
                act.wait_ge(oss_ready, 8 + g + 1)
                nc.scalar.activation(don, banks[4].rearrange("p (q t) -> p q t", t=T), ACT.Sqrt, bias=eps_col[:, :],
                                     scale=1.0 / P).then_inc(orms_ready, 1)

            act.wait_ge(delta_done, 1 + GROUPS)
            residual(2, False)
            act.wait_ge(resid_done, 1 + 4)
            squares_of(XT)
            root(4)

            act.wait_ge(normed, 4)
            for m in range(4):
                evac(ekey[:, 4 * m:4 * m + 4, :], banks[m].rearrange("p (q n) -> p q n", n=P))
            with rounds(act, 4, (tiles, 4)) as i:
                for s in range(2):
                    for m in range(2):
                        evac(eq_h[:, s, m, :], banks[2 * s + m][:, 0:T])
                    act.wait_ge(keyscore, 2 * i + s + 1)
                    act.wait_ge(picked, 1 + 2 * i)
                    nc.scalar.activation(esc[:, s, :, :, :], banks[4 + s].rearrange("p (c a n) -> p c a n", c=2, a=2),
                                         ACT.Copy).then_inc(keyscore_copied, 1)
            act.wait_ge(best_in, 1)
            nc.scalar.activation(eexp, ebest, ACT.Exp).then_inc(best_exp, 1)
            for c in range(TT):
                evac(slt[:, :, c * P:(c + 1) * P], banks[c][:, 0:3 * P].rearrange("p (r t) -> p r t", t=P))

            act.wait_ge(kept, 16)
            with rounds(act, T // 8) as i:
                for s in range(2):
                    act.wait_ge(gmat, 2 * i + s + 1)
                    nc.scalar.activation(G[:, :, ds(8 * i + 4 * s, 4)], banks[4 + s].rearrange("p (q e) -> p e q", e=P),
                                         ACT.Copy).then_inc(gmat_out, 1)

            def take_turned(e, u, m, first):
                act.wait_ge(turn_done, 4 * e + m + 1)
                if not first and m == 0:
                    act.wait_ge(hid_done, e - 1)
                nc.scalar.activation(UT[:, u % 2, 4 * m:4 * m + 4, :], banks[m].rearrange("p (q n) -> p q n", n=P),
                                     ACT.Copy).then_inc(turn_out_act, 1)

            def gelus(i, first):
                for m in (0, 2):
                    take_turned(4 * i, 0, m, first)
                for u in range(4):
                    e = 4 * i + u
                    if u < 3:
                        for m in (0, 2):
                            take_turned(e + 1, u + 1, m, first and u == 0)
                    act.wait_ge(hid_done, e + 1)
                    if not (first and u < 2):
                        act.wait_ge(wmul, e - 1)
                    nc.scalar.activation(gact[:, u % 2, :], banks[4 + u % 2][:, 0:T], ACT.Gelu).then_inc(gelu_done, 1)

            act.wait_ge(onehot, T // 4)
            act.wait_ge(gmat, T // 4)
            gelus(0, True)
            with rounds(act, N_KEYS // 4 - 1) as i:
                gelus(i + 1, False)

            act.wait_ge(y_added, 1)
            squares_of(XT)
            root(5)
            act.wait_ge(normed, 5)
            for n in range(8):
                evac(xout[:, n // 4, (n % 4) * 512:(n % 4 + 1) * 512], banks[n % 4][:, :])

        @block.vector
        def _(dve):
            v = nc.vector
            steps = Count(dve_step, "dve steps")
            tiles = Count(tile_evac, "dve tiles")

            def link(ins):
                ins.then_inc(dve_step, 1)
                dve.wait_ge(dve_step, steps.up())

            carried = [0]

            def carry():
                carried[0] += 1
                v.memset(carrier[:, carried[0] % 64:carried[0] % 64 + 1], 0.0)

            def pcol(at, n=1):
                return par[:, ds(at, n)]

            def norm(n, dst, wcol):
                dve.wait_ge(rms_ready, n)
                link(v.reciprocal(rms_t[:, 1, :], rms_t[:, 0, :]))
                for k in range(KT):
                    ins = v.scalar_tensor_tensor(out=dst[:, k, :], in0=XT[:, k, :], scalar=wcol[:, k:k + 1],
                                                 in1=rms_t[:, 1, :], op0=ALU.mult, op1=ALU.mult)
                ins.then_inc(normed, 1)

            for n, free in enumerate((conv_done, mlstm_done, merge_done, resid_done, hgrn_done, delta_done,
                                      keyscore_copied, picked)):
                v.memset(w1s[:, n:n + 1], 0.0).then_inc(free, 1)
            dve.wait_ge(c_ready, 1)
            land = [Count(landed[0], "dve slot 0"), Count(landed[1], "dve slot 1")]
            with rounds(dve, 6, (steps, 2 * ADA_DVE - 2), (land[0], 16), (land[1], 16)) as i:
                for n in range(2):
                    dve.wait_ge(landed[n], land[n].up(16))
                    w = ring[n][:, 0:KT * 512].rearrange("p (k c) -> p k c", c=512)
                    ins = v.tensor_scalar(ada_acc[n], w[:, 0, :], cact[:, 0:1], None, ALU.mult)
                    for k in range(1, ADA_DVE):
                        link(ins)
                        ins = v.scalar_tensor_tensor(out=ada_acc[n], in0=w[:, k, :], scalar=cact[:, k:k + 1],
                                                     in1=ada_acc[n], op0=ALU.mult, op1=ALU.add)
                    ins.then_inc(ada_part, 1)
            dve.wait_ge(mod_turned, 1)
            v.memset(cu, 0.0).then_inc(pads_done, 1)
            tiles.n = SETUP + ADA
            dve.wait_ge(act_step, 1)
            link(v.tensor_tensor(lbc[:, 2, :], lbc[:, 0, :], lbc[:, 1, :], ALU.add))
            link(v.reciprocal(lbc[:, 3, :], lbc[:, 2, :]))
            link(v.tensor_tensor(lbc[:, 2, :], lbc[:, 0, :], lbc[:, 3, :], ALU.mult))
            link(v.tensor_scalar(lbc[:, 3, :], lbc[:, 2, :], -1.0, 1.0, ALU.mult, ALU.add))
            link(v.tensor_tensor(mod[:, :], banks[4][:, 0:48], par[:, PK_BADA:PK_BADA + 48], ALU.add))
            v.scalar_tensor_tensor(out=w1s[:, :], in0=mod[:, 16:32], scalar=1.0, in1=par[:, PK_NORM1:PK_NORM1 + KT],
                                   op0=ALU.add, op1=ALU.mult).then_inc(mod_ready, 1)
            dve.wait_ge(mod_ready, 1)
            norm(1, hT, w1s)

            I, F_, AB, LF, F, A, MX, Z = (g8[:, n, :] for n in range(8))
            link(v.memset(Z, 0.0))
            dve.wait_ge(gates_mm, 2)
            v.tensor_scalar(I, banks[4][0:8, 0:T], gbias[:, 0:1], None, ALU.add)
            link(v.tensor_scalar(F_, banks[5][0:8, 0:T], gbias[:, 1:2], None, ALU.add))
            v.scalar_tensor_tensor(out=AB, in0=F_, scalar=-1.0, in1=F_, op0=ALU.mult, op1=ALU.max).then_inc(gates_abs, 1)
            dve.wait_ge(gates_log, 1)
            link(v.scalar_tensor_tensor(out=LF, in0=F_, scalar=0.0, in1=AB, op0=ALU.min, op1=ALU.subtract))
            link(v.tensor_tensor_scan(F, LF, Z, 0.0, ALU.add, ALU.add))
            link(v.tensor_tensor(A, I, F, ALU.subtract))
            v.tensor_tensor_scan(MX, A, A, 0.0, ALU.max, ALU.max).then_inc(gates_rows, 1)
            dve.wait_ge(gates_rows, 1)
            link(v.tensor_scalar(AB, MX, -1.0, None, ALU.mult))
            link(v.tensor_tensor(LF, AB, F, ALU.subtract))

            def spread_rows(n, row):
                link(v.tensor_tensor(spread[:, n, :, :], b3(row, 8),
                                     ident[0:8, 0:8].unsqueeze(2).broadcast_to([8, 8, T]), ALU.mult))

            spread_rows(0, AB)
            spread_rows(1, LF)

            dve.wait_ge(pads_done, 1)
            with rounds(dve, 8, (steps, 7), (tiles, 8)) as j:
                dve.wait_ge(tile_evac, tiles.value(4))
                link(v.tensor_tensor(cu[:, :, 2:T + 2], cv[:, 0:2, :], cv[:, 2:4, :], ALU.mult))
                for tap in (2, 1, 0):
                    for n in range(2):
                        wc = pcol(2 * j + (PK_CONV + tap * 16 + n))
                        if tap == 2:
                            ins = v.tensor_scalar(cy[:, n, :], cu[:, n, 2:T + 2], wc, None, ALU.mult)
                        else:
                            ins = v.scalar_tensor_tensor(out=cy[:, n, :], in0=cu[:, n, tap:tap + T], scalar=wc,
                                                         in1=cy[:, n, :], op0=ALU.mult, op1=ALU.add)
                        if n == 1:
                            link(ins)
                dve.wait_ge(tile_evac, tiles.value(8))
                link(v.tensor_tensor(cy, cy, cv[:, 4:6, :], ALU.mult))
                link(v.tensor_tensor(cy, cy, cv[:, 6:8, :], ALU.mult))
                link(v.tensor_copy(HB[:, ds(2 * j, 2), :], cy))
                ins = v.memset(cy[:, 0, 0:1], 0.0)
                ins.then_inc(conv_done, 1)
                tiles.up(8)

            dve.wait_ge(gates_tp, 1)
            v.tensor_copy(colT[:, 0, :, :], banks[6][:, 0:16].rearrange("p (c h) -> p c h", h=8)).then_inc(gates_done, 1)

            with rounds(dve, 8, (steps, 7), (tiles, 8)) as h:
                dve.wait_ge(scores_ready, h + 1)
                v.tensor_scalar(mE[:, 0:T], banks[6][:, 0:T], colT[:, 0, 0, ds(h, 1)], 0.0, ALU.add, ALU.min)
                v.tensor_scalar(mE[:, T:T + P], banks[6][:, P:T], colT[:, 0, 1, ds(h, 1)], 0.0, ALU.add,
                                ALU.min).then_inc(expo_ready, 1)
                dve.wait_ge(causal_done, h + 1)
                v.scalar_tensor_tensor(out=mS, in0=banks[4][:, 0:384], scalar=float(128 ** -0.5), in1=mE,
                                       op0=ALU.mult, op1=ALU.mult).then_inc(att_ready, 1)
                dve.wait_ge(num_ready, h + 1)
                dve.wait_ge(floor_done, h + 1)
                link(v.tensor_tensor(mden[:, 0, :], banks[6][:, 0:T], mfloor, ALU.max))
                link(v.scalar_tensor_tensor(out=mden[:, 0, :], in0=banks[6][:, 0:T], scalar=-1.0, in1=mden[:, 0, :],
                                            op0=ALU.mult, op1=ALU.max))
                link(v.reciprocal(mden[:, 0, :], mden[:, 0, :]))
                link(v.tensor_tensor(mh, banks[5].rearrange("p (n t) -> p n t", t=T), b3(mden[:, 0, :], 2), ALU.mult))
                dve.wait_ge(tile_evac, tiles.value(6))
                v.tensor_tensor(mh, mh, mo, ALU.mult).then_inc(h_ready, 1)
                dve.wait_ge(h_ready, h + 1)
                dve.wait_ge(hrms_ready, h + 1)
                link(v.reciprocal(mden[:, 1, :], mden[:, 1, :]))
                for n in range(2):
                    ins = v.scalar_tensor_tensor(out=mh[:, n, :], in0=mh[:, n, :], scalar=pcol(2 * h + (PK_HEADN + n)),
                                                 in1=mden[:, 1, :], op0=ALU.mult, op1=ALU.mult)
                link(ins)
                dve.wait_ge(tile_evac, tiles.value(8))
                link(v.tensor_tensor(mh, mh, mz, ALU.mult))
                v.tensor_copy(HA[:, ds(2 * h, 2), :], mh).then_inc(mlstm_done, 1)
                tiles.up(8)

            with rounds(dve, 8, (steps, 1), (tiles, 8)) as j:
                tiles.up(8)
                dve.wait_ge(tile_evac, tiles.value())
                link(v.tensor_tensor(prod, sg, yy, ALU.mult))
                v.tensor_tensor(MG[:, ds(2 * j, 2), :], prod[:, 0:2, :], prod[:, 2:4, :], ALU.add).then_inc(merge_done, 1)

            def residual():
                with rounds(dve, 2, (tiles, 8)) as i:
                    for s in range(2):
                        tiles.up(4)
                        dve.wait_ge(tile_evac, tiles.value())
                        part = XT[:, ds(8 * i + 4 * s, 4), :]
                        ins = v.tensor_tensor(part, part, upd[:, 4 * s:4 * s + 4, :], ALU.add)
                    ins.then_inc(resid_done, 1)

            residual()
            norm(2, XT, par[:, PK_NORMF:PK_NORMF + KT])
            norm(3, hT, par[:, PK_ATTN:PK_ATTN + KT])

            link(v.memset(zrow, 0.0))
            link(v.memset(hatt, 0.0))
            dve.wait_ge(masks_done, 1)
            with rounds(dve, 4, (steps, 10), (tiles, 8)) as i:
                for s in range(2):
                    head = 2 * i + s
                    dve.wait_ge(decay_in, 2 * head + 2)
                    v.tensor_scalar(hk, hneg, lbc[:, 3, ds(head, 1)], None, ALU.mult)
                    link(v.tensor_tensor_scan(hb, hlf, zrow, 0.0, ALU.add, ALU.add))
                    for l, half in enumerate(LEVELS + [128]):
                        bb = hb.rearrange("p (n s t) -> p n s t", s=2, t=half)
                        ee = hE[:, l, :].rearrange("p (n s t) -> p n s t", s=2, t=half)
                        nb = T // (2 * half)
                        ref = bb[:, :, 0, half - 1:half].broadcast_to([P, nb, half])
                        v.tensor_tensor(ee[:, :, 1, :], bb[:, :, 1, :], ref, ALU.subtract)
                        ins = v.tensor_tensor(ee[:, :, 0, :], ref, bb[:, :, 0, :], ALU.subtract)
                    ins.then_inc(decay_exp, 1)
                    dve.wait_ge(decayed, head + 1)
                    dve.wait_ge(dve_step, steps.value())
                    for l, half in enumerate(LEVELS + [128]):
                        qq, kk, ee, xx = (y.rearrange("p (n s t) -> p n s t", s=2, t=half)
                                          for y in (hq, hk, hE[:, l, :], hX[:, l, :]))
                        v.tensor_tensor(xx[:, :, 1, :], qq[:, :, 1, :], ee[:, :, 1, :], ALU.mult)
                        ins = v.tensor_tensor(xx[:, :, 0, :], kk[:, :, 0, :], ee[:, :, 0, :], ALU.mult)
                    ins.then_inc(x_levels, 1)
                    for l in range(9):
                        dve.wait_ge(gram_done, head * 9 + l + 1)
                        dve.wait_ge(gram_taken, head * 9 + l)
                        if l:
                            carry()
                        b = banks[4 + l % 4]
                        if l == 0:
                            ins = v.tensor_copy(hatt[:, 1, :], b[:, 0:P])
                        else:
                            mask = masks[:, l - 1, :] if l < 8 else ident[:, :]
                            ins = v.copy_predicated(hatt[:, 0:3:2, :], b3(mask, 2).bitcast(U32),
                                                    b[:, 0:T].rearrange("p (c t) -> p c t", t=P))
                        ins.then_inc(gram_taken, 1)
                    dve.wait_ge(orms_ready, head + 1)
                    link(v.reciprocal(hsig, hon))
                    link(v.scalar_tensor_tensor(out=hneg, in0=banks[5][:, 0:T], scalar=par[:, PK_HGN:PK_HGN + 1],
                                                in1=hsig, op0=ALU.mult, op1=ALU.mult))
                    tiles.up(4)
                    dve.wait_ge(tile_evac, tiles.value())
                    link(v.tensor_tensor(hneg, hneg, hz, ALU.mult))
                    link(v.tensor_copy(MIX[:, ds(head, 1), :].rearrange("p o t -> p (o t)"), hneg))
                    v.memset(hb[:, 0:1], 0.0).then_inc(hgrn_done, 1)

            link(v.memset(Z, 0.0))
            link(v.memset(draw, 0.0))
            dve.wait_ge(gates_mm, 4)
            link(v.tensor_scalar(F_, banks[5][0:8, 0:T], gbias[:, 3:4], None, ALU.add))
            v.scalar_tensor_tensor(out=AB, in0=F_, scalar=-1.0, in1=F_, op0=ALU.mult, op1=ALU.max).then_inc(gates_abs, 1)
            dve.wait_ge(gates_log, 2)
            link(v.scalar_tensor_tensor(out=LF, in0=F_, scalar=0.0, in1=AB, op0=ALU.max, op1=ALU.add))
            dve.wait_ge(decay_in, 18)
            link(v.tensor_scalar(LF, LF, gbias[:, 4:5], -1.0, ALU.mult, ALU.mult))
            v.tensor_tensor_scan(F, LF, Z, 0.0, ALU.add, ALU.add).then_inc(gates_rows, 1)
            dve.wait_ge(gates_rows, 2)
            spread_rows(0, F)
            spread_rows(1, I)
            dve.wait_ge(gates_tp, 2)
            v.tensor_copy(colT[:, 1:3, :, :], banks[6][:, 0:32].rearrange("p (r c h) -> p r c h", r=2, h=8)).then_inc(gates_done, 1)

            with rounds(dve, GROUPS, (steps, 8), (tiles, 6)) as g:
                tiles.up(6)
                dve.wait_ge(tile_evac, tiles.value())
                for tap in range(TAPS):
                    for m, c0 in enumerate((g, 4 + g, 8 + 2 * g, 9 + 2 * g)):
                        wc = pcol(c0 + (PK_GCONV + 16 * tap))
                        if tap == 0:
                            ins = v.tensor_scalar(dy[:, m, :], draw[:, m, 0:T], wc, None, ALU.mult)
                        else:
                            ins = v.scalar_tensor_tensor(out=dy[:, m, :], in0=draw[:, m, tap:tap + T], scalar=wc,
                                                         in1=dy[:, m, :], op0=ALU.mult, op1=ALU.add)
                    if tap < TAPS - 1:
                        link(ins)
                ins.then_inc(conv_in, 1)
                dve.wait_ge(qk_rms, g + 1)
                link(v.reciprocal(drt, drt))
                v.scalar_tensor_tensor(out=dqk[:, 0, :], in0=dc[:, 0, :], scalar=float(128 ** -0.5), in1=drt[:, 0, :],
                                       op0=ALU.mult, op1=ALU.mult)
                v.tensor_tensor(dqk[:, 1, :], dc[:, 1, :], drt[:, 1, :], ALU.mult).then_inc(qk_unit, 1)
                dve.wait_ge(bc_ready, g + 1)
                for n in range(2):
                    for c in range(TT):
                        dst = dW[:, 3 * n:3 * n + 2, :].rearrange("p a t -> p (a t)") if c == 0 else dW[:, 3 * n + 2, :]
                        ins = v.tensor_scalar(dst, banks[4 + n][:, c * P:T], colT[:, 1, c, ds(2 * g + n, 1)], 0.0,
                                              ALU.subtract, ALU.min)
                ins.then_inc(dex_ready, 1)
                v.tensor_copy(dD, b3(ident[:, :], 8))
                dve.wait_ge(dmask_done, g + 1)
                for n in range(2):
                    w = dW[:, 3 * n:3 * n + 3, :]
                    v.tensor_tensor(dA[:, 3 * n:3 * n + 3, :], banks[7][:, 0:384].rearrange("p (a t) -> p a t", t=P), w, ALU.mult)
                    ins = v.tensor_tensor(dM[:, 3 * n:3 * n + 3, :], banks[6][:, 0:384].rearrange("p (a t) -> p a t", t=P), w, ALU.mult)
                link(ins)
                for n in range(2):
                    w = dM[:, 3 * n:3 * n + 2, :]
                    v.tensor_tensor(w, w, banks[4 + n][:, T:2 * T].rearrange("p (a t) -> p a t", t=P), ALU.mult)
                    w = dM[:, 3 * n + 2, :]
                    ins = v.tensor_tensor(w, w, banks[4 + n][:, T + P:2 * T], ALU.mult)
                link(ins)
                for l in range(7):
                    step = g * 7 + l
                    if l:
                        dve.wait_ge(lv_dd, step)
                    for n in range(2):
                        ins = v.tensor_tensor(dC[:, 2 * n:2 * n + 2, :], dM[:, 3 * n:3 * n + 3:2, :], b3(masks[:, l, :], 2), ALU.mult)
                    if l:
                        v.tensor_tensor(dD[:, 0:4, :], dD[:, 0:4, :], banks[5].rearrange("p (q t) -> p q t", t=P), ALU.subtract)
                        ins = v.tensor_tensor(dD[:, 4:8, :], dD[:, 4:8, :], banks[6].rearrange("p (q t) -> p q t", t=P), ALU.subtract)
                    ins.then_inc(lv_mask, 1)
                dve.wait_ge(lv_dd, g * 7 + 7)
                v.tensor_tensor(dD[:, 4:8, :], dD[:, 4:8, :], banks[6].rearrange("p (q t) -> p q t", t=P), ALU.subtract).then_inc(lv_new, 1)
                dve.wait_ge(r2_mm, g + 1)
                v.tensor_tensor(dr2, dbv[:, 1:4:2, :], banks[5][:, 0:T].rearrange("p (q t) -> p q t", t=P), ALU.subtract).then_inc(r2_ready, 1)
                dve.wait_ge(orms_ready, 8 + g + 1)
                link(v.reciprocal(drt, don))
                link(v.scalar_tensor_tensor(out=dy[:, 0:2, :], in0=banks[7].rearrange("p (q t) -> p q t", t=T),
                                            scalar=par[:, PK_GDN:PK_GDN + 1], in1=drt, op0=ALU.mult, op1=ALU.mult))
                v.tensor_tensor(MIX[:, ds(8 + 2 * g, 2), :], dy[:, 0:2, :], dz, ALU.mult).then_inc(delta_done, 1)

            residual()
            norm(4, hT, par[:, PK_FFN:PK_FFN + KT])

            def top16(vals, idx, src, spare):
                carry()
                link(v.max(vals[:, 0:8], src))
                carry()
                v.max_index(idx[:, 0:8], vals[:, 0:8], src)
                link(v.match_replace(spare, vals[:, 0:8], src, -3.0e38))
                carry()
                link(v.max(vals[:, 8:16], spare))
                carry()
                return v.max_index(idx[:, 8:16], vals[:, 8:16], spare)

            with rounds(dve, 4, (steps, 54)) as i:
                for s in range(2):
                    head = 2 * i + s
                    dve.wait_ge(keyscore_copied, 1 + head + 1)
                    for c in range(TT):
                        for half in range(2):
                            ins = top16(ev[:, c, half, :], ei[:, c, half, :], esc[:, s, c, half, :], esc2[:, c, half, :])
                    link(ins)
                    link(v.tensor_copy(eif, ei))
                    for c in range(TT):
                        ins = v.tensor_tensor(ecand[:, c, :].rearrange("p (i j) -> p i j", j=TOPK),
                                              ev[:, c, 0, :].unsqueeze(2).broadcast_to([P, TOPK, TOPK]),
                                              b3(ev[:, c, 1, :], TOPK), ALU.add)
                    link(ins)
                    for c in range(TT):
                        ins = top16(ebv[:, c, :], ebp[:, c, :], ecand[:, c, :], ecand2[:, c, :])
                    link(ins)
                    v.tensor_scalar(ehl[:, 0, :, :], ebp, 4, None, ALU.logical_shift_right)
                    link(v.tensor_scalar(ehl[:, 1, :, :], ebp, 15, None, ALU.bitwise_and))
                    link(v.tensor_copy(ehf, ehl))
                    for q in range(2):
                        ins = v.tensor_tensor(eeq[:, q, :, :, :], ehf[:, q, :, :].unsqueeze(3).broadcast_to([P, 2, TOPK, TOPK]),
                                              iota[:, 0:TOPK].unsqueeze(1).unsqueeze(1).broadcast_to([P, 2, TOPK, TOPK]), ALU.is_equal)
                    link(ins)
                    for q in range(2):
                        ins = v.tensor_tensor(eeq[:, q, :, :, :], eeq[:, q, :, :, :],
                                              eif[:, :, q, :].unsqueeze(2).broadcast_to([P, 2, TOPK, TOPK]), ALU.mult)
                    link(ins)
                    for q in range(2):
                        v.tensor_reduce(e12[:, q, :, ds(head * TOPK, TOPK)], eeq[:, q, :, :, :], AX.X, ALU.add)
                    link(v.tensor_tensor(ebest[:, :, ds(head * TOPK, TOPK)], ebv, ebv[:, :, 0:1].broadcast_to([P, 2, TOPK]), ALU.subtract))
                    v.memset(esum[:, 0:1], 0.0).then_inc(picked, 1)
            dve.wait_ge(picked, 1 + 8)
            v.memset(esum[:, 1:2], 0.0).then_inc(best_in, 1)
            dve.wait_ge(best_exp, 1)
            es = esum[:, 0:16].rearrange("p (c h) -> p c h", h=8)
            ex = eexp.rearrange("p c (h k) -> p c h k", k=TOPK)
            link(v.tensor_reduce(es, ex, AX.X, ALU.add))
            link(v.reciprocal(es, es))
            v.tensor_tensor(ex, ex, es.unsqueeze(3).broadcast_to([P, 2, 8, TOPK]), ALU.mult).then_inc(slots_ready, 1)

            tiles.n = FINAL_TILES
            dve.wait_ge(tile_evac, tiles.value())

            def onehots(i, first):
                for s in range(2):
                    n = 2 * i + s
                    if not first:
                        dve.wait_ge(gmat, n - 1)
                    for q in range(4):
                        t = 8 * i + (4 * s + q)
                        v.tensor_scalar(oh[:, s, q, 0, :], iota[:, :], slt[:, 0, ds(t, 1)], slt[:, 2, ds(t, 1)],
                                        ALU.is_equal, ALU.mult)
                        ins = v.tensor_scalar(oh[:, s, q, 1, :], iota[:, :], slt[:, 1, ds(t, 1)], None, ALU.is_equal)
                    ins.then_inc(onehot, 1)

            onehots(0, True)
            with rounds(dve, T // 8 - 1) as i:
                onehots(i + 1, False)

            def take_turned(e, u, m, first):
                dve.wait_ge(turn_done, 4 * e + m + 1)
                if not first and m == 1:
                    dve.wait_ge(hid_done, e - 1)
                v.tensor_copy(UT[:, u % 2, 4 * m:4 * m + 4, :], banks[m].rearrange("p (q n) -> p q n", n=P)).then_inc(turn_out_dve, 1)

            def weigh(i, first):
                for m in (1, 3):
                    take_turned(4 * i, 0, m, first)
                for u in range(4):
                    e = 4 * i + u
                    if u < 3:
                        for m in (1, 3):
                            take_turned(e + 1, u + 1, m, first and u == 0)
                    dve.wait_ge(gelu_done, e + 1)
                    g = G[:, ds(e, 1), :].rearrange("p o t -> p (o t)")
                    v.tensor_tensor(g, g, gact[:, u % 2, :], ALU.mult).then_inc(wmul, 1)

            dve.wait_ge(gmat_out, T // 4)
            weigh(0, True)
            with rounds(dve, N_KEYS // 4 - 1) as i:
                weigh(i + 1, False)
            dve.wait_ge(hid_done, N_KEYS)
            v.memset(late[:, 0:640], 0.0).then_inc(zero_done, 1)

            dve.wait_ge(y_done, N_KEYS // 2)
            dve.wait_ge(x_back, 16)
            for b in range(8):
                part = XT[:, 2 * b:2 * b + 2, :]
                ins = v.tensor_tensor(part, part, banks[b].rearrange("p (k t) -> p k t", t=T), ALU.add)
            ins.then_inc(y_added, 1)
            dve.wait_ge(y_added, 1)
            norm(5, hT, par[:, PK_FINAL:PK_FINAL + KT])

        @block.gpsimd
        def _(pool):
            steps = Count(pool_step, "pool steps")

            def link(ins):
                ins.then_inc(pool_step, 1)
                pool.wait_ge(pool_step, steps.up())

            nc.gpsimd.memset(ones[:, :], 1.0)
            nc.gpsimd.memset(eps_col[:, :], EPS)
            link(nc.gpsimd.memset(ident[:, :], 0.0))
            nc.gpsimd.iota(iota[:, :], [[1, P]], base=0, channel_multiplier=0, allow_small_or_imprecise_dtypes=True)
            nc.gpsimd.affine_select(out=ident[:, :], in_=ident[:, :], compare_op=ALU.not_equal, fill=1.0, base=0,
                                    pattern=[[-1, P]], channel_multiplier=1).then_inc(consts, 1)
            link(nc.gpsimd.memset(masks, 1.0))
            for l, half in enumerate(LEVELS):
                nb = P // (2 * half)
                m = masks[:, l, :]
                for sign, base in ((1, 0), (-1, half - 1)):
                    link(nc.gpsimd.affine_select(out=m, in_=m, compare_op=ALU.is_ge, fill=0.0, base=base,
                                                 pattern=[[-sign * 2 * half, nb], [0, 2], [0, half]],
                                                 channel_multiplier=sign))
                ins = nc.gpsimd.affine_select(out=m, in_=m, compare_op=ALU.is_gt, fill=0.0, base=0,
                                              pattern=[[0, nb], [1, 2], [0, half]], channel_multiplier=0)
                link(ins)
            link(nc.gpsimd.memset(causal_mask, 1.0))
            nc.gpsimd.affine_select(out=causal_mask, in_=causal_mask, compare_op=ALU.is_ge, fill=0.0, base=0,
                                    pattern=[[1, P]], channel_multiplier=-1).then_inc(masks_done, 1)
            pool.wait_ge(masks_done, 1)

            def causal(view):
                return nc.gpsimd.tensor_tensor(view, view, b3(causal_mask, 2), ALU.mult)

            with rounds(pool, 8) as h:
                pool.wait_ge(exp_done, h + 1)
                causal(mE.rearrange("p (a t) -> p a t", t=P)[:, 0:3:2, :]).then_inc(causal_done, 1)
            with rounds(pool, GROUPS) as g:
                pool.wait_ge(dex_done, g + 1)
                for n in range(2):
                    ins = causal(dW[:, 3 * n:3 * n + 3:2, :])
                ins.then_inc(dmask_done, 1)


_INS = ['x', 'c', 'norm1_w', 'w_ada', 'b_ada', 'w_in', 'b_in', 'conv_w', 'headnorm_w', 'w_proj_a', 'w_proj_b',
        'w_out', 'normf_w', 'attn_norm_g_2', 'w_in_2', 'hgrn_lb_logits_2', 'hgrn_norm_g_2', 'gdn_conv_w_2',
        'gdn_A_log_2', 'gdn_dt_bias_2', 'gdn_norm_g_2', 'w_out_2', 'ffn_norm_g_2', 'peer_w_query_2',
        'peer_sub_keys_2', 'peer_u_2', 'peer_v_2', 'final_norm_g_2']


def kernel(**inputs):
    import numpy as _np
    import concourse.bacc as _bacc
    from concourse import mybir as _mybir
    from concourse.bass_utils import run_bass_kernel_spmd as _run

    nc = _bacc.Bacc("TRN2", target_bir_lowering=False, num_devices=1)
    arrays, aps = {}, {}
    for name in _INS:
        v = _np.ascontiguousarray(inputs[name])
        arrays[f"in_{name}_dram"] = v
        aps[name] = nc.dram_tensor(f"in_{name}_dram", v.shape, _mybir.dt.from_np(v.dtype), kind="ExternalInput").ap()
    out = nc.dram_tensor("out_dram", (1, T, D), F32, kind="ExternalOutput").ap()
    build(nc, aps, out)
    r = _run(nc, [arrays], core_ids=[0])
    return r.results[0]["out_dram"]
```

```python
from contextlib import ExitStack, contextmanager

import concourse.bass as bass
from concourse import mybir

ALU = mybir.AluOpType
ACT = mybir.ActivationFunctionType
AX = mybir.AxisListType
F32 = mybir.dt.float32
F32R = mybir.dt.float32r
U32 = mybir.dt.uint32
ds = bass.ds

P = 128
T = 256
TT = T // P
D = 2048
KT = D // P
EPS = 1e-6
HEADS = 8
QKW = HEADS * 128
VW = 2048
OFF_K, OFF_V, OFF_O, OFF_Z = QKW, 2 * QKW, 2 * QKW + VW, 2 * QKW + 2 * VW
OFF_I = 2 * QKW + 3 * VW
OFF_U = OFF_I + 2 * HEADS
OFF_B, OFF_C, OFF_ZB, OFF_GA, OFF_GB = (OFF_U + n * D for n in range(1, 6))
IN_1 = OFF_GB + D
OFF2_F, OFF2_I, OFF2_G = 1024, 2048, 3072
OFF2_BQ, OFF2_BK, OFF2_BV, OFF2_BZ = 4096, 4608, 5120, 6144
OFF2_BB = 7168
GROUPS = 4
TAPS = 4
N_KEYS = 128
TOPK = 16
LEVELS = [1, 2, 4, 8, 16, 32, 64]

PK_QKVOZ_B, PK_NORM1, PK_HEADN, PK_NORMF, PK_ATTN = 0, 64, 80, 96, 112
PK_REST_B, PK_FFN, PK_FINAL = 128, 128 + 96, 128 + 112
PK_CONV, PK_BADA, PK_C, PK_HGN, PK_GDN = 256, 256 + 48, 256 + 96, 256 + 112, 256 + 113
PK_GCONV, PK_LB = 384, 384 + 64
PACK_ROWS = [128, 128, 114, 80]

N_PARAMS = 21
SLOT = 8192
ADA_DVE = 6
U_CHUNKS = N_KEYS // 4
PEER_SLOT = 4096


class Count:

    def __init__(self, sem, name=""):
        self.sem, self.n, self.lead, self.name = sem, 0, 0, name

    def value(self, more=0):
        return self.lead + (self.n + more)

    def up(self, k=1):
        self.n += k
        return self.value()


@contextmanager
def rounds(eng, count, *counts):
    with eng.Fori(0, count) as i:
        before = [c.n for c, _ in counts]
        for c, per in counts:
            c.lead = i * per
        yield i
        for (c, per), b in zip(counts, before):
            assert c.n - b == per, (c.name, c.n - b, per)
    for c, per in counts:
        c.lead = 0
        c.n += (count - 1) * per


def build(nc, a, out, stop=99):
    ctx = ExitStack()
    with ctx:
        def sb(name, shape, dt=F32):
            return ctx.enter_context(nc.sbuf_tensor(name, shape, dt))

        def sem(name):
            return ctx.enter_context(nc.semaphore(name))

        def top():
            return -(-nc.sbuf_base // 32) * 32

        arena_at = top()
        arena = sb("arena", [P, 45056])
        late_at = top()
        late = sb("late", [P, 4096])
        ident = sb("ident", [P, P])
        ones = sb("ones", [P, P])
        iota = sb("iota", [P, P])
        par = sb("par", [P, 512])
        eps_col = sb("eps_col", [P, 1])
        cact = sb("cact", [P, KT])
        mod = sb("mod", [P, 48])
        w1s = sb("w1s", [P, KT])
        lbc = sb("lbc", [P, 4, HEADS])
        rms_t = sb("rms_t", [P, 2, T])
        slt_at = top()
        slt = sb("slt", [P, 3, T])
        carrier = sb("carrier", [P, 64])
        gact_at = top()
        gact = sb("gact", [P, TT, 512])

        def halves(name, at, k, n):
            return nc.alloc_sbuf_tensor_at(name, [P, k, n], F32R, offset=at)

        h_hi = halves("h_hi", late_at, KT, T)
        h_lo = halves("h_lo", arena_at + 10 * 4096 * 4, KT, T)
        u_hi = halves("u_hi", arena_at + 4096 * 4, 4, 512)
        u_lo = halves("u_lo", arena_at + 6144 * 4, 4, 512)
        v_hi = halves("v_hi", arena_at + 10 * 4096 * 4, 2, D)
        v_lo = halves("v_lo", late_at, 2, D)
        w_hi = halves("w_hi", gact_at, 2, T)
        w_lo = halves("w_lo", slt_at, 2, T)

        def slab(n):
            return arena[:, n * 4096:(n + 1) * 4096].rearrange("p (k t) -> p k t", t=T)

        ring = [arena[:, s * SLOT:(s + 1) * SLOT] for s in range(2)]
        peer_ring = [arena[:, s * PEER_SLOT:(s + 1) * PEER_SLOT].rearrange("p (c d) -> p c d", d=D)
                     for s in range(2)]
        u_ring = [arena[:, s * 2048:(s + 1) * 2048].rearrange("p (e d) -> p e d", d=512) for s in range(2)]
        keys_rows = arena[:, 9 * 4096:9 * 4096 + 2048].rearrange("p (s n) -> p s n", n=P)
        G = arena[:, 2 * 4096:10 * 4096].rearrange("p (e t) -> p e t", t=T)
        XT, HA, HB, MG = slab(4), slab(5), slab(6), slab(7)
        HB2 = HB
        WK, WK2 = slab(8), slab(9)
        hT = slab(10)
        wk = arena[:, 8 * 4096:10 * 4096]

        ada_acc = [wk[:, 512 + n * 512:1024 + n * 512] for n in range(2)]
        mod_rows = wk[0:48, 1536:1664]
        mod_row = wk[0:1, 2048:2048 + 3 * D]
        dw0 = 6 * 4096

        def dw(at, n):
            return arena[:, dw0 + at:dw0 + at + n]

        def words(at, n):
            return wk[:, at:at + n]

        xrow = arena[:, 5 * 4096:6 * 4096].rearrange("p (c d) -> p c d", d=D)
        vbias = arena[0:1, 7 * 4096:7 * 4096 + VW]
        spread = arena[0:8, 9 * 4096:10 * 4096].rearrange("p (a h t) -> p a h t", a=2, t=T)
        xout = arena[:, 6 * 4096:7 * 4096].rearrange("p (c d) -> p c d", d=D)
        pack = words(0, 512).rearrange("p (k c) -> p k c", c=128)
        causal_mask = late[:, 896:1024]
        masks = late[:, 0:896].rearrange("p (l t) -> p l t", t=P)
        wg = late[:, 1024:1280].rearrange("p (k c) -> p k c", c=16)
        wg2 = late[:, 1280:1536].rearrange("p (k c) -> p k c", c=16)
        gbias = late[0:8, 1536:1544]
        colT = late[:, 1552:1600].rearrange("p (a c h) -> p a c h", a=3, c=TT)
        g8 = late[0:8, 1664:1664 + 8 * T].rearrange("p (a t) -> p a t", t=T)

        banks = [ctx.enter_context(nc.psum_tensor(f"bank{n}", [P, 512], F32)) for n in range(8)]
        xkeep = nc.dram_tensor("xkeep", [P, KT, T], F32, kind="Internal").ap()

        landed = [sem("slot0_landed"), sem("slot1_landed")]
        params_in = sem("params_in")
        x_in = sem("x_in")
        keys_in = sem("keys_in")
        vbias_in = sem("vbias_in")
        kept = sem("kept")
        x_back = sem("x_back")
        out_done = sem("out_done")
        consts = sem("consts")
        masks_done = sem("masks_done")
        tile_done = sem("tile_done")
        tile_evac = sem("tile_evac")
        act_step = sem("act_step")
        dve_step = sem("dve_step")
        pool_step = sem("pool_step")
        pads_done = sem("pads_done")
        c_ready = sem("c_ready")
        ada_part = sem("ada_part")
        mod_moved = sem("mod_moved")
        mod_turned = sem("mod_turned")
        mod_ready = sem("mod_ready")
        squares = sem("squares")
        ss_ready = sem("ss_ready")
        rms_ready = sem("rms_ready")
        normed = sem("normed")
        shifted = sem("shifted")
        conv_done = sem("conv_done")
        gates_mm = sem("gates_mm")
        gates_abs = sem("gates_abs")
        gates_log = sem("gates_log")
        gates_rows = sem("gates_rows")
        gates_tp = sem("gates_tp")
        gates_done = sem("gates_done")
        scores_ready = sem("scores_ready")
        expo_ready = sem("expo_ready")
        exp_done = sem("exp_done")
        floor_done = sem("floor_done")
        causal_done = sem("causal_done")
        att_ready = sem("att_ready")
        num_ready = sem("num_ready")
        h_ready = sem("h_ready")
        hsq_ready = sem("hsq_ready")
        hss_ready = sem("hss_ready")
        hrms_ready = sem("hrms_ready")
        mlstm_done = sem("mlstm_done")
        merge_done = sem("merge_done")
        resid_done = sem("resid_done")
        decay_in = sem("decay_in")
        decay_exp = sem("decay_exp")
        x_levels = sem("x_levels")
        decayed = sem("decayed")
        gram_done = sem("gram_done")
        gram_taken = sem("gram_taken")
        att_clear = sem("att_clear")
        o_ready = sem("o_ready")
        osq_ready = sem("osq_ready")
        oss_ready = sem("oss_ready")
        orms_ready = sem("orms_ready")
        hgrn_done = sem("hgrn_done")
        conv_in = sem("conv_in")
        silu_done = sem("silu_done")
        qk_sq = sem("qk_sq")
        qk_ss = sem("qk_ss")
        qk_rms = sem("qk_rms")
        qk_unit = sem("qk_unit")
        v_turned = sem("v_turned")
        bv_ready = sem("bv_ready")
        kk_ready = sem("kk_ready")
        bc_ready = sem("bc_ready")
        dex_ready = sem("dex_ready")
        dex_done = sem("dex_done")
        dmask_done = sem("dmask_done")
        mt_ready = sem("mt_ready")
        lv_mask = sem("lv_mask")
        lv_cd = sem("lv_cd")
        lv_cd_copied = sem("lv_cd_copied")
        lv_dd = sem("lv_dd")
        lv_new = sem("lv_new")
        u1_mm = sem("u1_mm")
        u1_copied = sem("u1_copied")
        r2_mm = sem("r2_mm")
        r2_ready = sem("r2_ready")
        u2_mm = sem("u2_mm")
        u2_copied = sem("u2_copied")
        delta_done = sem("delta_done")
        keyscore = sem("keyscore")
        keyscore_copied = sem("keyscore_copied")
        picked = sem("picked")
        best_in = sem("best_in")
        best_exp = sem("best_exp")
        slots_ready = sem("slots_ready")
        onehot = sem("onehot")
        gmat = sem("gmat")
        gmat_out = sem("gmat_out")
        turn_done = sem("turn_done")
        h_rounded = sem("h_rounded")
        h_split = sem("h_split")
        u_rounded = sem("u_rounded")
        u_split = sem("u_split")
        u_used = sem("u_used")
        act_turned = sem("act_turned")
        gelu_done = sem("gelu_done")
        wmul = sem("wmul")
        v_landed = [sem("v_slot0_landed"), sem("v_slot1_landed")]
        hi_ready = sem("hi_ready")
        lo_ready = sem("lo_ready")
        y_rows_act = sem("y_rows_act")
        y_rows_dve = sem("y_rows_dve")
        y_turned = sem("y_turned")
        y_done = sem("y_done")
        y_added = sem("y_added")

        SETUP, ADA = 12, 12
        FINAL_TILES = SETUP + ADA + 3 * 64 + 16 + 32 + 24 + 16 + 4 + 16 + 2

        def b3(ap, n):
            return ap.unsqueeze(1).broadcast_to([ap.shape[0], n, ap.shape[1]])

        def w3(f, at, k, t=T):
            return f(at, k * t).rearrange("p (k t) -> p k t", t=t)

        upd = w3(words, 0, 8)
        sg, yy, prod = w3(words, 0, 4), w3(words, 1024, 4), w3(words, 2048, 4)
        cv, cu, cy = w3(words, 0, 8), w3(words, 2048, 2, T + 2), w3(words, 2564, 2)
        mqk, mv, mo, mz = (w3(words, n * 512, 2) for n in range(4))
        mE, mS, mfloor = words(2048, 384), words(2432, 384), words(2816, T)
        mden, mh = w3(words, 3072, 2), w3(words, 3584, 2)
        msq = arena[:, 7 * 4096 + 2048:7 * 4096 + 2560].rearrange("p (k t) -> p k t", t=T)
        hq, hv, hz = dw(0, T), w3(dw, T, 2, P), dw(512, T)
        hsig, hneg, hlf, hk, hb = (dw(768 + n * T, T) for n in range(5))
        hE, hX = w3(dw, 2048, 8), w3(dw, 4096, 8)
        hatt = w3(dw, 6144, 3, P)
        zrow, hsq, hon = dw(6528, T), dw(6784, T), dw(7040, T)
        draw, dy, dc = w3(dw, 0, 4, T + 3), w3(dw, 1036, 4), w3(dw, 2060, 4)
        dsq, drt, dqk = w3(dw, 3084, 2), w3(dw, 3596, 2), w3(dw, 4108, 2)
        dz = gact[:, 0, :].rearrange("p (n t) -> p n t", t=T)
        dbv = w3(dw, 5132, 4, P)
        dW, dA, dM = w3(dw, 6028, 6, P), w3(dw, 6796, 6, P), w3(dw, 7564, 6, P)
        dC, dD, dcd = w3(dw, 8332, 4, P), w3(dw, 8844, 8, P), w3(dw, 9868, 4, P)
        du, dr2 = w3(dw, 10380, 4, P), w3(dw, 10892, 2, P)
        don, dosq = w3(dw, 11148, 2), w3(dw, 11660, 2)
        eq_h = dw(0, 1024).rearrange("p (a s t) -> p a s t", a=2, s=2)
        ekey = w3(dw, 1024, 16, P)
        esc = dw(3072, 1024).rearrange("p (a c s n) -> p a c s n", a=2, c=2, s=2)
        esc2 = dw(4096, 512).rearrange("p (c s n) -> p c s n", c=2, s=2)
        ev = dw(4608, 64).rearrange("p (c s k) -> p c s k", c=2, s=2)
        ei = dw(4672, 64).bitcast(U32).rearrange("p (c s k) -> p c s k", c=2, s=2)
        eif = dw(4736, 64).rearrange("p (c s k) -> p c s k", c=2, s=2)
        ecand, ecand2 = w3(dw, 4800, 2), w3(dw, 5312, 2)
        ebv, ebp = w3(dw, 5824, 2, 16), dw(5856, 32).bitcast(U32).rearrange("p (c k) -> p c k", k=16)
        ehl = dw(5888, 64).bitcast(U32).rearrange("p (s c k) -> p s c k", s=2, k=16)
        ehf = dw(5952, 64).rearrange("p (s c k) -> p s c k", s=2, k=16)
        eeq = dw(6016, 1024).rearrange("p (s c k j) -> p s c k j", s=2, c=2, k=16)
        e12 = dw(7040, 512).rearrange("p (s c n) -> p s c n", s=2, n=P)
        ebest, eexp, esum = w3(dw, 7552, 2, P), w3(dw, 7808, 2, P), dw(8064, 32)
        oh = late[:, 0:2048].rearrange("p (s q w n) -> p s q w n", s=2, q=4, w=2)
        MIX = HA

        def rows_of(w):
            return w.rearrange("(k p) n -> p k n", p=P)

        w_ada = rows_of(a["w_ada"][0])
        w_in = rows_of(a["w_in"][0])
        w_pa = rows_of(a["w_proj_a"][0])
        w_pb = rows_of(a["w_proj_b"][0])
        w_out = rows_of(a["w_out"][0])
        w_in2 = rows_of(a["w_in_2"][0])
        w_out2 = rows_of(a["w_out_2"][0])
        w_q = rows_of(a["peer_w_query_2"][0].rearrange("d h k -> d (h k)"))
        p_u = a["peer_u_2"][0].rearrange("(c e p) d -> c p e d", e=4, p=P)
        p_v = a["peer_v_2"][0].rearrange("(c e p) d -> c p e d", e=2, p=P)

        block = ctx.enter_context(nc.Block())

        @block.sync
        def _(sp):
            tiles = Count(tile_done, "sp tiles")
            tiles.n = 12

            def load(slot, pieces, makes, prev, width=512):
                if prev is not None:
                    sp.wait_ge(tile_done, tiles.value(-prev))
                dst = ring[slot][:, 0:KT * width].rearrange("p (k c) -> p k c", c=width)
                at = 0
                for src, off, n in pieces:
                    sp.dma_start(dst[:, :, at:at + n], src[:, :, ds(off, n)]).then_inc(landed[slot], 16)
                    at += n
                tiles.up(makes)

            load(0, [(w_ada, 0, 512)], 1, None)
            load(1, [(w_ada, 512, 512)], 1, None)
            with rounds(sp, 5, (tiles, 2)) as i:
                load(0, [(w_ada, 1024 + i * 1024, 512)], 1, 1)
                load(1, [(w_ada, 1536 + i * 1024, 512)], 1, 1)
            sp.dma_start(vbias, a["b_in"][0][OFF_V:OFF_V + VW].rearrange("(o n) -> o n", o=1)).then_inc(vbias_in, 16)
            sp.wait_ge(tile_evac, SETUP + ADA)
            sp.dma_start(mod_rows, mod_row.rearrange("o (r c) -> o r c", c=128)).then_inc(mod_moved, 16)

            def conv_chunks(j, prev):
                load(0, [(w_in, OFF_U + j * 256, 256), (w_in, OFF_C + j * 256, 256)], 4, prev)
                load(1, [(w_in, OFF_B + j * 256, 256), (w_in, OFF_ZB + j * 256, 256)], 4, 4)

            conv_chunks(0, 1)
            with rounds(sp, 7, (tiles, 8)) as j:
                conv_chunks(j + 1, 4)
            with rounds(sp, 8, (tiles, 8)) as h:
                load(0, [(w_in, h * 128, 128), (w_in, OFF_K + h * 128, 128),
                         (w_in, OFF_V + h * 256, 256)], 4, 4)
                load(1, [(w_in, OFF_O + h * 256, 256), (w_in, OFF_Z + h * 256, 256)], 4, 4)
            with rounds(sp, 8, (tiles, 8)) as j:
                load(0, [(w_in, OFF_GA + j * 256, 256), (w_pa, j * 256, 256)], 4, 4)
                load(1, [(w_in, OFF_GB + j * 256, 256), (w_pb, j * 256, 256)], 4, 4)
            with rounds(sp, 2, (tiles, 8)) as j:
                load(0, [(w_out, j * 1024, 512)], 4, 4)
                load(1, [(w_out, j * 1024 + 512, 512)], 4, 4)
            with rounds(sp, 4, (tiles, 8)) as i:
                for s in range(2):
                    load(s, [(w_in2, i * 256 + (off + s * 128), 128) for off in (0, OFF2_F, OFF2_I, OFF2_G)], 4, 4)

            def delta_chunks(g, prev):
                load(0, [(w_in2, OFF2_BQ + g * 128, 128), (w_in2, OFF2_BK + g * 128, 128),
                         (w_in2, OFF2_BV + g * 256, 128)], 3, prev, 384)
                load(1, [(w_in2, OFF2_BV + g * 256 + 128, 128),
                         (w_in2, OFF2_BZ + g * 256, 256)], 3, 3, 384)

            delta_chunks(0, 4)
            with rounds(sp, GROUPS - 1, (tiles, 6)) as g:
                delta_chunks(g + 1, 3)

            def out2_chunks(j, prev):
                load(0, [(w_out2, j * 1024, 512)], 4, prev)
                load(1, [(w_out2, j * 1024 + 512, 512)], 4, 4)

            out2_chunks(0, 3)
            out2_chunks(1, 4)

            load(0, [(w_q, 0, 256)], 2, 4, 256)
            sp.wait_ge(normed, 4)
            sp.dma_start(keys_rows, a["peer_sub_keys_2"][0].rearrange("s h n k -> n (s h) k")).then_inc(keys_in, 16)
            tiles.n += 4
            load(1, [(w_q, 256, 256)], 2, 6, 256)
            with rounds(sp, 3, (tiles, 4)) as i:
                load(0, [(w_q, (i + 1) * 512, 256)], 2, 2, 256)
                load(1, [(w_q, (i + 1) * 512 + 256, 256)], 2, 2, 256)
            sp.dma_start(xkeep, XT).then_inc(kept, 16)

            def load_u(i, q):
                sp.dma_start(u_ring[q % 2], p_u[ds(i, 1), :, :, q * 512:(q + 1) * 512].rearrange("o p e d -> p (o e) d")).then_inc(landed[q % 2], 16)

            sp.wait_ge(tile_done, tiles.value())
            load_u(0, 0)
            load_u(0, 1)
            for q in range(2, 4):
                sp.wait_ge(turn_done, 4 * (q - 1))
                load_u(0, q)
            with rounds(sp, U_CHUNKS - 1) as i:
                for q in range(4):
                    sp.wait_ge(turn_done, 16 * i + (4 * (q + 3)))
                    load_u(i + 1, q)

            def load_v(c, s):
                sp.dma_start(peer_ring[s], p_v[ds(c, 1)].rearrange("o p e d -> p (o e) d")).then_inc(v_landed[s], 16)

            sp.wait_ge(turn_done, 16 * U_CHUNKS)
            load_v(0, 0)
            sp.wait_ge(u_used, 16 * U_CHUNKS)
            load_v(1, 1)
            with rounds(sp, 31) as i:
                for s in range(2):
                    sp.wait_ge(lo_ready, 4 * i + (2 * s + 2))
                    load_v(2 * i + (s + 2), s)
            sp.wait_ge(lo_ready, N_KEYS)
            sp.wait_ge(kept, 16)
            sp.dma_start(XT, xkeep).then_inc(x_back, 16)
            for c in range(TT):
                sp.wait_ge(tile_evac, FINAL_TILES + 4 * (c + 1))
                sp.dma_start(out[0][c * P:(c + 1) * P, :], xout[:, c, :]).then_inc(out_done, 16)
            sp.wait_ge(out_done, 16 * TT)

        @block.tensor
        def _(pe):
            tiles = Count(tile_done, "pe tiles")
            land = [Count(landed[0], "pe slot 0"), Count(landed[1], "pe slot 1")]

            def free_bank(lag=4):
                if isinstance(tiles.lead, int) and tiles.n < lag:
                    return
                pe.wait_ge(tile_evac, tiles.value(1 - lag))

            def arrive(slot, pieces):
                pe.wait_ge(landed[slot], land[slot].up(16 * pieces))

            def chunk(slot, width=512):
                return ring[slot][:, 0:KT * width].rearrange("p (k c) -> p k c", c=width)

            def feature_tile(bank, w, c0, moving, lag=4):
                free_bank(lag)
                for k in range(KT):
                    mm = nc.tensor.matmul(banks[bank][:, 0:T], w[:, k, c0:c0 + P], moving[:, k, :],
                                          start=(k == 0), stop=(k == KT - 1))
                mm.then_inc(tile_done, 1)
                tiles.up()

            def turn(bank, at, src):
                return nc.tensor.transpose(banks[bank][0:src.shape[1], at:at + src.shape[0]], src,
                                           ident[0:src.shape[0], 0:src.shape[0]])

            def mean_square(n):
                pe.wait_ge(squares, 4 * n)
                for k in range(KT):
                    mm = nc.tensor.matmul(banks[5][:, 0:T], ones[:, :], HB2[:, k, :],
                                          start=(k == 0), stop=(k == KT - 1))
                mm.then_inc(ss_ready, 1)

            pe.wait_ge(consts, 1)
            pe.wait_ge(x_in, 16)
            for m in range(8):
                free_bank()
                for q in range(4):
                    k, c = 2 * m + q // 2, q % 2
                    mm = turn(m % 4, q * P, xrow[:, c, k * P:(k + 1) * P])
                mm.then_inc(tile_done, 1)
                tiles.up()
            pe.wait_ge(params_in, 16 * N_PARAMS)
            for m, rows in enumerate(PACK_ROWS):
                free_bank()
                turn(m, 0, pack[0:rows, m, :]).then_inc(tile_done, 1)
                tiles.up()

            pe.wait_ge(c_ready, 1)
            with rounds(pe, 6, (tiles, 2), (land[0], 16), (land[1], 16)) as i:
                for s in range(2):
                    arrive(s, 1)
                    w = chunk(s)
                    free_bank(2)
                    for k in range(ADA_DVE, KT):
                        nc.tensor.matmul(banks[s][0:1, :], cact[:, k:k + 1], w[:, k, :],
                                         start=(k == ADA_DVE), stop=False)
                    pe.wait_ge(ada_part, 2 * i + (s + 1))
                    nc.tensor.matmul(banks[s][0:1, :], ones[:, 0:1], ada_acc[s],
                                     start=False, stop=True).then_inc(tile_done, 1)
                    tiles.up()
            mean_square(1)
            pe.wait_ge(mod_moved, 16)
            nc.tensor.transpose(banks[4][:, 0:48], mod_rows, ident[0:48, 0:48]).then_inc(mod_turned, 1)

            pe.wait_ge(shifted, 1)
            for g in range(2):
                for k in range(KT):
                    mm = nc.tensor.matmul(banks[4 + g][0:8, 0:T], wg[:, k, 8 * g:8 * g + 8], hT[:, k, :],
                                          start=(k == 0), stop=(k == KT - 1))
                mm.then_inc(gates_mm, 1)
            pe.wait_ge(tile_evac, tiles.value())

            with rounds(pe, 8, (tiles, 8), (land[0], 32), (land[1], 32)) as j:
                for s in range(2):
                    arrive(s, 2)
                    for m in range(4):
                        feature_tile(m, chunk(s), m * P, hT)

            pe.wait_ge(gates_rows, 1)
            for c in range(TT):
                mm = turn(6, c * 8, g8[:, 5, c * P:(c + 1) * P])
            mm.then_inc(gates_tp, 1)
            pe.wait_ge(vbias_in, 16)
            pe.wait_ge(gates_done, 1)
            with rounds(pe, 8, (tiles, 8), (land[0], 48), (land[1], 32)) as h:
                arrive(0, 3)
                w = chunk(0)
                for m in range(2):
                    feature_tile(m, w, m * P, hT)
                for c in range(TT):
                    free_bank()
                    for k in range(KT):
                        nc.tensor.matmul(banks[2 + c][:, 0:T], hT[:, k, c * P:(c + 1) * P],
                                         w[:, k, 256:512], start=(k == 0), stop=False)
                    mm = nc.tensor.matmul(banks[2 + c][:, 0:T], ones[0:1, :], vbias[:, ds(h * 256, 256)],
                                          start=False, stop=True)
                    mm.then_inc(tile_done, 1)
                    tiles.up()
                pe.wait_ge(tile_evac, tiles.value(-2))
                pe.wait_ge(mlstm_done, 1 + h)
                nc.tensor.matmul(banks[4][:, 0:T], mqk[:, 1, 0:P], mqk[:, 0, :], start=True, stop=True)
                nc.tensor.matmul(banks[4][:, T:T + P], mqk[:, 1, P:T], mqk[:, 0, P:T], start=True, stop=True)
                for n in range(2):
                    mm = nc.tensor.matmul(banks[6 + n][:, 0:T], ones[0:8, :], spread[:, n, ds(h, 1), :].rearrange("p o t -> p (o t)"),
                                          start=True, stop=True)
                mm.then_inc(scores_ready, 1)
                arrive(1, 2)
                for m in range(2):
                    feature_tile(m, chunk(1), m * P, hT)
                pe.wait_ge(att_ready, h + 1)
                pe.wait_ge(tile_evac, tiles.value(-2))
                for n in range(2):
                    o = banks[5][:, n * T:(n + 1) * T]
                    nc.tensor.matmul(o, mv[:, 0, n * P:(n + 1) * P], mS[:, 0:T], start=True, stop=False)
                    nc.tensor.matmul(o[:, P:T], mv[:, 1, n * P:(n + 1) * P], mS[:, T:T + P],
                                     start=False, stop=True)
                nc.tensor.matmul(banks[6][:, 0:T], ones[:, :], mS[:, 0:T], start=True, stop=False)
                nc.tensor.matmul(banks[6][:, P:T], ones[:, :], mS[:, T:T + P],
                                 start=False, stop=True).then_inc(num_ready, 1)
                for m in range(2, 4):
                    feature_tile(m, chunk(1), m * P, hT)
                pe.wait_ge(hsq_ready, h + 1)
                for n in range(2):
                    mm = nc.tensor.matmul(banks[7][:, 0:T], ones[:, :], msq[:, n, :],
                                          start=(n == 0), stop=(n == 1))
                mm.then_inc(hss_ready, 1)

            pe.wait_ge(mlstm_done, 1 + 8)
            pe.wait_ge(conv_done, 1 + 8)
            with rounds(pe, 8, (tiles, 8), (land[0], 32), (land[1], 32)) as j:
                for s, branch in enumerate((HA, HB)):
                    arrive(s, 2)
                    for m in range(4):
                        feature_tile(m, chunk(s), m * P, hT if m < 2 else branch)

            def out_projection(moving):
                with rounds(pe, 2, (tiles, 8), (land[0], 16), (land[1], 16)):
                    for s in range(2):
                        arrive(s, 1)
                        for m in range(4):
                            feature_tile(m, chunk(s), m * P, moving)

            pe.wait_ge(merge_done, 1 + 8)
            out_projection(MG)
            mean_square(2)
            mean_square(3)

            pe.wait_ge(normed, 3)
            with rounds(pe, 4, (tiles, 8), (land[0], 64), (land[1], 64)) as i:
                for s in range(2):
                    head = 2 * i + s
                    arrive(s, 4)
                    w = chunk(s)
                    feature_tile(0, w, 0, hT)
                    feature_tile(1, w, P, hT)
                    free_bank()
                    for c in range(TT):
                        for k in range(KT):
                            mm = nc.tensor.matmul(banks[2][:, c * P:(c + 1) * P], hT[:, k, c * P:(c + 1) * P],
                                                  w[:, k, T:T + P], start=(k == 0), stop=(k == KT - 1))
                    mm.then_inc(tile_done, 1)
                    tiles.up()
                    feature_tile(3, w, 3 * P, hT)
                    pe.wait_ge(x_levels, head + 1)
                    for l in range(9):
                        b = banks[4 + l % 4]
                        if l >= 4:
                            pe.wait_ge(gram_taken, head * 9 + l - 3)
                        if l == 0:
                            mm = nc.tensor.matmul(b[:, 0:P], hX[:, 7, 0:P], hX[:, 7, P:T], start=True, stop=True)
                        else:
                            x, y = (hX[:, l - 1, :], hX[:, l - 1, :]) if l < 8 else (hk, hq)
                            for c in range(TT):
                                mm = nc.tensor.matmul(b[:, c * P:(c + 1) * P], x[:, c * P:(c + 1) * P],
                                                      y[:, c * P:(c + 1) * P], start=True, stop=True)
                        mm.then_inc(gram_done, 1)
                    pe.wait_ge(gram_taken, head * 9 + 9)
                    pe.wait_ge(tile_evac, tiles.value(-1))
                    nc.tensor.matmul(banks[5][:, 0:T], hv[:, 0, :], hatt[:, 0:2, :].rearrange("p a t -> p (a t)"), start=True, stop=False)
                    nc.tensor.matmul(banks[5][:, P:T], hv[:, 1, :], hatt[:, 2, :],
                                     start=False, stop=True).then_inc(o_ready, 1)
                    pe.wait_ge(osq_ready, head + 1)
                    nc.tensor.matmul(banks[6][:, 0:T], ones[:, :], hsq, start=True, stop=True).then_inc(oss_ready, 1)

            pe.wait_ge(hgrn_done, 1 + 8)
            for g in range(2):
                for k in range(KT):
                    mm = nc.tensor.matmul(banks[4 + g][0:8, 0:T], wg2[:, k, 8 * g:8 * g + 8], hT[:, k, :],
                                          start=(k == 0), stop=(k == KT - 1))
                mm.then_inc(gates_mm, 1)

            def delta_tiles(x0, n):
                for x in range(x0, x0 + n):
                    m, k = divmod(x, KT)
                    if x % 48 == 0:
                        arrive(m // 3, 3 if m == 0 else 2)
                    if k == 0:
                        free_bank((4, 4, 2, 2, 6, 6)[m])
                    w = chunk(m // 3, 384)
                    c0 = m % 3 * P
                    mm = nc.tensor.matmul(banks[(0, 1, 0, 1, 2, 3)[m]][:, 0:T], w[:, k, c0:c0 + P], hT[:, k, :],
                                          start=(k == 0), stop=(k == KT - 1))
                    if k == KT - 1:
                        mm.then_inc(tile_done, 1)
                        tiles.up()

            delta_tiles(0, 96)
            pe.wait_ge(gates_rows, 2)
            for r, row in enumerate((4, 0)):
                for c in range(TT):
                    mm = turn(6, (r * TT + c) * 8, g8[:, row, c * P:(c + 1) * P])
            mm.then_inc(gates_tp, 1)
            pe.wait_ge(gates_done, 2)

            def delta(g, last=False):
                def meanwhile(x0, n):
                    if not last:
                        delta_tiles(x0, n)

                pe.wait_ge(qk_sq, g + 1)
                pe.wait_ge(orms_ready, 8 + g)
                for n in range(2):
                    mm = nc.tensor.matmul(banks[4][:, n * T:(n + 1) * T], ones[:, :], dsq[:, n, :], start=True, stop=True)
                mm.then_inc(qk_ss, 1)
                for n in range(2):
                    for c in range(TT):
                        mm = turn(5, (n * TT + c) * P, dc[:, 2 + n, c * P:(c + 1) * P])
                mm.then_inc(v_turned, 1)
                meanwhile(0, 20)
                pe.wait_ge(qk_unit, g + 1)
                for n in range(2):
                    b, y = banks[6 + n], dqk[:, 1 - n, :]
                    nc.tensor.matmul(b[:, 0:T], dqk[:, 1, 0:P], y, start=True, stop=True)
                    mm = nc.tensor.matmul(b[:, T:T + P], dqk[:, 1, P:T], y[:, P:T], start=True, stop=True)
                mm.then_inc(kk_ready, 1)
                pe.wait_ge(bv_ready, g + 1)
                for n in range(2):
                    for r in range(2):
                        mm = nc.tensor.matmul(banks[4 + n][:, r * T:(r + 1) * T], ones[0:8, :],
                                              spread[:, r, ds(2 * g + n, 1), :].rearrange("p o t -> p (o t)"), start=True, stop=True)
                mm.then_inc(bc_ready, 1)
                meanwhile(20, 18)
                pe.wait_ge(lv_mask, g * 7 + 1)
                for q in range(4):
                    mm = turn(5, q * P, dC[:, q, :])
                mm.then_inc(lv_dd, 1)
                meanwhile(38, 5)
                for l in range(1, 7):
                    pe.wait_ge(lv_mask, g * 7 + (l + 1))
                    for q in range(4):
                        mm = nc.tensor.matmul(banks[4][:, q * P:(q + 1) * P], dC[:, q, :], dD[:, q, :], start=True, stop=True)
                    mm.then_inc(lv_cd, 1)
                    meanwhile(36 + 7 * l, 2)
                    pe.wait_ge(lv_cd_copied, g * 6 + l)
                    if l < 6:
                        for q in range(4):
                            nc.tensor.matmul(banks[5][:, q * P:(q + 1) * P], dD[:, 4 + q, :], dcd[:, q, :], start=True, stop=True)
                    for q in range(4):
                        mm = nc.tensor.matmul(banks[6][:, q * P:(q + 1) * P], dcd[:, q, :], dD[:, 4 + q, :], start=True, stop=True)
                    mm.then_inc(lv_dd, 1)
                    meanwhile(38 + 7 * l, 5)
                pe.wait_ge(lv_new, g + 1)
                for n in range(2):
                    mm = nc.tensor.matmul(banks[4][:, n * P:(n + 1) * P], dD[:, 4 + 2 * n, :], dbv[:, 2 * n, :], start=True, stop=True)
                mm.then_inc(u1_mm, 1)
                meanwhile(85, 3)
                pe.wait_ge(u1_copied, g + 1)
                for n in range(2):
                    mm = nc.tensor.matmul(banks[5][:, n * P:(n + 1) * P], dM[:, 3 * n + 1, :], du[:, 2 * n, :], start=True, stop=True)
                mm.then_inc(r2_mm, 1)
                meanwhile(88, 2)
                pe.wait_ge(r2_ready, g + 1)
                for n in range(2):
                    mm = nc.tensor.matmul(banks[6][:, n * P:(n + 1) * P], dD[:, 5 + 2 * n, :], dr2[:, n, :], start=True, stop=True)
                mm.then_inc(u2_mm, 1)
                meanwhile(90, 2)
                pe.wait_ge(u2_copied, g + 1)
                for n in range(2):
                    o = banks[7][:, n * T:(n + 1) * T]
                    nc.tensor.matmul(o, du[:, 2 * n, :], dA[:, 3 * n:3 * n + 2, :].rearrange("p a t -> p (a t)"), start=True, stop=False)
                    mm = nc.tensor.matmul(o[:, P:T], du[:, 2 * n + 1, :], dA[:, 3 * n + 2, :], start=False, stop=True)
                mm.then_inc(o_ready, 1)
                meanwhile(92, 4)
                pe.wait_ge(osq_ready, 8 + g + 1)
                for n in range(2):
                    mm = nc.tensor.matmul(banks[4][:, n * T:(n + 1) * T], ones[:, :], dosq[:, n, :], start=True, stop=True)
                mm.then_inc(oss_ready, 1)

            with rounds(pe, GROUPS - 1, (tiles, 6), (land[0], 48), (land[1], 32)) as g:
                delta(g)
            delta(GROUPS - 1, last=True)

            pe.wait_ge(delta_done, 1 + GROUPS)
            pe.wait_ge(tile_evac, tiles.value())
            out_projection(MIX)
            mean_square(4)

            pe.wait_ge(keys_in, 16)
            for m in range(4):
                free_bank()
                for q in range(4):
                    mm = turn(m, q * P, keys_rows[:, 4 * m + q, :])
                mm.then_inc(tile_done, 1)
                tiles.up()
            pe.wait_ge(normed, 4)
            with rounds(pe, 4, (tiles, 4), (land[0], 16), (land[1], 16)) as i:
                for s in range(2):
                    arrive(s, 1)
                    for m in range(2):
                        feature_tile(2 * s + m, chunk(s, 256), m * P, hT)
                    pe.wait_ge(tile_evac, tiles.value())
                    pe.wait_ge(keyscore_copied, 1 + 2 * i + s)
                    for c in range(TT):
                        for half in range(2):
                            mm = nc.tensor.matmul(banks[4 + s][:, (2 * c + half) * P:(2 * c + half + 1) * P],
                                                  eq_h[:, s, half, c * P:(c + 1) * P],
                                                  ekey[:, ds(2 * i + (s + 8 * half), 1), :].rearrange("p o n -> p (o n)"),
                                                  start=True, stop=True)
                    mm.then_inc(keyscore, 1)

            pe.wait_ge(slots_ready, 1)
            for c in range(TT):
                free_bank()
                for r, src in enumerate((e12[:, 0, c, :], e12[:, 1, c, :], eexp[:, c, :])):
                    mm = turn(c, r * P, src)
                mm.then_inc(tile_done, 1)
                tiles.up()

            def gate_products(i, first):
                for s in range(2):
                    n = 2 * i + s
                    pe.wait_ge(onehot, n + 1)
                    if not first:
                        pe.wait_ge(gmat_out, n - 1)
                    for q in range(4):
                        mm = nc.tensor.matmul(banks[4 + s][:, q * P:(q + 1) * P], oh[:, s, q, 1, :], oh[:, s, q, 0, :],
                                              start=True, stop=True)
                    mm.then_inc(gmat, 1)

            gate_products(0, True)
            with rounds(pe, T // 8 - 1) as i:
                gate_products(i + 1, False)
            pe.wait_ge(gmat_out, T // 4)

            def turn_u(j, k, first=False):
                if k % 4 == 0:
                    arrive(k // 4 % 2, 1)
                if not first:
                    pe.wait_ge(u_split, j - 3)
                for e in range(4):
                    mm = turn(k % 4, e * P, u_ring[k // 4 % 2][:, e, (k % 4) * P:(k % 4 + 1) * P])
                mm.then_inc(turn_done, 1)

            def turn_activated(b):
                for e in range(4):
                    for c in range(TT):
                        mm = turn(b + e // 2, (e % 2) * T + c * P, gact[:, c, e * P:(e + 1) * P])
                mm.then_inc(act_turned, 1)

            def hidden(n, b, first=False, last=False):
                for k in range(KT):
                    j = 16 * n + k
                    if not (last and k + 3 >= KT):
                        turn_u(j + 3, (k + 3) % KT, first and k == 0)
                    if first and k % 4 == 0:
                        pe.wait_ge(h_split, k // 4 + 1)
                    if not first and k == 0:
                        pe.wait_ge(wmul, 1 + 2 * n - 2)
                    pe.wait_ge(u_split, j + 1)
                    for c in range(TT):
                        for h, u in ((h_hi, u_hi), (h_hi, u_lo), (h_lo, u_hi)):
                            mm = nc.tensor.matmul(banks[b + c][:, :], h[:, k, c * P:(c + 1) * P], u[:, k % 4, :],
                                                  start=(k == 0 and h is h_hi and u is u_hi),
                                                  stop=(k == KT - 1 and h is h_lo))
                    mm.then_inc(u_used, 1)
                    if not first and k == 7:
                        pe.wait_ge(gelu_done, 2 * n)
                        turn_activated(10 - b)

            for k in range(3):
                turn_u(k, k, True)
            hidden(0, 4, first=True)
            with rounds(pe, U_CHUNKS // 2 - 1, (land[0], 64), (land[1], 64)) as i:
                hidden(2 * i + 1, 6)
                hidden(2 * i + 2, 4)
            hidden(U_CHUNKS - 1, 6, last=True)
            pe.wait_ge(gelu_done, 2 * U_CHUNKS)
            turn_activated(6)

            def outputs(i, first):
                for u in range(4):
                    pe.wait_ge(lo_ready, 4 * i + (u + 1))
                    for c in range(TT):
                        for w, v, opens in ((w_hi, v_hi, first and u == 0), (w_hi, v_lo, False), (w_lo, v_hi, False)):
                            for b in range(4):
                                mm = nc.tensor.matmul(banks[4 * c + b][:, :], w[:, u % 2, c * P:(c + 1) * P],
                                                      v[:, u % 2, b * 512:(b + 1) * 512],
                                                      start=opens, stop=False, skip_group_check=True)
                    mm.then_inc(y_done, 1)

            outputs(0, True)
            with rounds(pe, N_KEYS // 4 - 1) as i:
                outputs(i + 1, False)
            pe.wait_ge(y_rows_act, 4)
            pe.wait_ge(y_rows_dve, 4)
            for m in range(8):
                for q in range(4):
                    mm = turn(m, q * P, xrow[:, q % 2, (2 * m + q // 2) * P:(2 * m + q // 2 + 1) * P])
                mm.then_inc(y_turned, 1)

            mean_square(5)
            pe.wait_ge(normed, 5)
            for n in range(8):
                free_bank()
                for q in range(4):
                    mm = turn(n % 4, q * P, hT[:, 4 * (n % 4) + q, (n // 4) * P:(n // 4 + 1) * P])
                mm.then_inc(tile_done, 1)
                tiles.up()

        @block.scalar
        def _(act):
            tiles = Count(tile_evac, "act tiles")
            steps = Count(act_step, "act steps")

            def evac(dst, src, func=ACT.Copy, bias=None, scale=None):
                act.wait_ge(tile_done, tiles.up())
                kw = {}
                if bias is not None:
                    kw["bias"] = bias
                if scale is not None:
                    kw["scale"] = scale
                nc.scalar.activation(dst, src, func, **kw).then_inc(tile_evac, 1)

            def link(ins):
                ins.then_inc(act_step, 1)
                act.wait_ge(act_step, steps.up())

            def squares_of(src):
                for q in range(4):
                    nc.scalar.activation(HB2[:, 4 * q:4 * q + 4, :], src[:, 4 * q:4 * q + 4, :], ACT.Square).then_inc(squares, 1)

            def root(n):
                act.wait_ge(ss_ready, n)
                nc.scalar.activation(rms_t[:, 0, :], banks[5][:, 0:T], ACT.Sqrt, bias=eps_col[:, :],
                                     scale=1.0 / D).then_inc(rms_ready, 1)

            def pcol(at, n=1):
                return par[:, ds(at, n)]

            def rows128(src, dst):
                act.dma_start(dst, src).then_inc(params_in, 16)

            def r(ap):
                return ap.rearrange("(r c) -> r c", c=128)

            act.dma_start(xrow[:, :, :], a["x"][0].rearrange("(c p) d -> p c d", p=P)).then_inc(x_in, 16)
            b = a["b_in"][0]
            rows128(r(b[0:OFF_I]), pack[0:64, 0, :])
            rows128(r(a["norm1_w"][0]), pack[64:80, 0, :])
            rows128(r(a["headnorm_w"][0]), pack[80:96, 0, :])
            rows128(r(a["normf_w"]), pack[96:112, 0, :])
            rows128(r(a["attn_norm_g_2"][0]), pack[112:128, 0, :])
            rows128(r(b[OFF_U:IN_1]), pack[0:96, 1, :])
            rows128(r(a["ffn_norm_g_2"][0]), pack[96:112, 1, :])
            rows128(r(a["final_norm_g_2"]), pack[112:128, 1, :])
            rows128(a["conv_w"][0].rearrange("j (r c) -> (j r) c", c=128), pack[0:48, 2, :])
            rows128(r(a["b_ada"][0]), pack[48:96, 2, :])
            rows128(r(a["c"][0]), pack[96:112, 2, :])
            rows128(a["hgrn_norm_g_2"], pack[112:113, 2, :])
            rows128(a["gdn_norm_g_2"], pack[113:114, 2, :])
            rows128(a["gdn_conv_w_2"][0].rearrange("j (r c) -> (j r) c", c=128), pack[0:64, 3, :])
            rows128(a["hgrn_lb_logits_2"].rearrange("l h c -> (l h) c"), pack[64:80, 3, :])
            col = lambda v: v.rearrange("(h o) -> h o", o=1)
            with nc.allow_non_contiguous_dma("a few words"):
                rows128(col(b[OFF_I:OFF_I + 8]), gbias[:, 0:1])
                rows128(col(b[OFF_I + 8:OFF_I + 16]), gbias[:, 1:2])
                rows128(col(a["gdn_A_log_2"][0]), gbias[:, 2:3])
                rows128(col(a["gdn_dt_bias_2"][0]), gbias[:, 3:4])
                rows128(w_in[:, :, OFF_I:OFF_I + 16], wg[:, :, :])
                rows128(w_in2[:, :, OFF2_BB:OFF2_BB + 16], wg2[:, :, :])


            act.wait_ge(consts, 1)
            for m in range(8):
                evac(XT[:, 2 * m:2 * m + 2, :], banks[m % 4].rearrange("p (k t) -> p k t", t=T))
            for m, rows in enumerate(PACK_ROWS):
                evac(par[:, 128 * m:128 * m + rows], banks[m][:, 0:rows])
            act.wait_ge(tile_evac, tiles.value())
            nc.scalar.activation(cact[:, :], par[:, PK_C:PK_C + KT], ACT.Silu).then_inc(c_ready, 1)
            link(nc.scalar.activation(lbc[:, 0:2, :], par[:, PK_LB:PK_LB + 16].rearrange("p (l h) -> p l h", l=2), ACT.Exp))
            squares_of(XT)
            with rounds(act, 6, (tiles, 2)) as i:
                for s in range(2):
                    evac(mod_row[:, ds(1024 * i + 512 * s, 512)], banks[s][0:1, :])
            root(1)

            act.wait_ge(normed, 1)
            act.wait_ge(mod_ready, 1)
            for k in range(KT):
                ins = nc.scalar.activation(hT[:, k, :], hT[:, k, :], ACT.Identity, bias=mod[:, k:k + 1])
            ins.then_inc(shifted, 1)

            def soft(n):
                act.wait_ge(gates_abs, n)
                link(nc.scalar.activation(g8[:, 2, :], g8[:, 2, :], ACT.Exp, scale=-1.0))
                nc.scalar.activation(g8[:, 2, :], g8[:, 2, :], ACT.Ln, bias=1.0).then_inc(gates_log, 1)

            soft(1)
            with rounds(act, 8, (tiles, 8)) as j:
                act.wait_ge(conv_done, 1 + j)
                for m in range(8):
                    base = (PK_REST_B, PK_REST_B + 32, PK_REST_B + 16, PK_REST_B + 48)[m // 2]
                    evac(cv[:, m, :], banks[m % 4][:, 0:T], ACT.Identity if m < 6 else ACT.Silu,
                         bias=pcol(base + m % 2 + 2 * j))

            with rounds(act, 8, (tiles, 8)) as h:
                act.wait_ge(mlstm_done, 1 + h)
                evac(mqk[:, 0, :], banks[0][:, 0:T], ACT.Identity, bias=pcol(h + PK_QKVOZ_B))
                evac(mqk[:, 1, :], banks[1][:, 0:T], ACT.Identity, bias=pcol(h + (PK_QKVOZ_B + 8)))
                for c in range(TT):
                    evac(mv[:, c, :], banks[2 + c][:, 0:T])
                act.wait_ge(expo_ready, h + 1)
                nc.scalar.activation(mE, mE, ACT.Exp).then_inc(exp_done, 1)
                nc.scalar.activation(mfloor, banks[7][:, 0:T], ACT.Exp).then_inc(floor_done, 1)
                for m in range(2):
                    evac(mo[:, m, :], banks[m][:, 0:T], ACT.Sigmoid, bias=pcol(2 * h + (PK_QKVOZ_B + 32 + m)))
                act.wait_ge(h_ready, h + 1)
                nc.scalar.activation(msq, mh, ACT.Square).then_inc(hsq_ready, 1)
                for m in range(2):
                    evac(mz[:, m, :], banks[2 + m][:, 0:T], ACT.Silu, bias=pcol(2 * h + (PK_QKVOZ_B + 48 + m)))
                act.wait_ge(hss_ready, h + 1)
                nc.scalar.activation(mden[:, 1, :], banks[7][:, 0:T], ACT.Sqrt, bias=eps_col[:, :],
                                     scale=1.0 / 256).then_inc(hrms_ready, 1)

            with rounds(act, 8, (tiles, 8)) as j:
                act.wait_ge(merge_done, 1 + j)
                for s in range(2):
                    for m in range(2):
                        evac(sg[:, 2 * s + m, :], banks[m][:, 0:T], ACT.Sigmoid,
                             bias=pcol(2 * j + (PK_REST_B + 64 + 16 * s + m)))
                    for m in range(2):
                        evac(yy[:, 2 * s + m, :], banks[2 + m][:, 0:T])

            def residual(turns, gate):
                with rounds(act, 2, (tiles, 8)) as i:
                    act.wait_ge(resid_done, 1 + turns + i)
                    for m in range(8):
                        evac(upd[:, m, :], banks[m % 4][:, 0:T],
                             scale=mod[:, ds(8 * i + (32 + m), 1)] if gate else None)

            act.wait_ge(merge_done, 1 + 8)
            residual(0, True)
            act.wait_ge(resid_done, 1 + 2)
            squares_of(XT)
            root(2)
            act.wait_ge(normed, 2)
            squares_of(XT)
            root(3)

            with rounds(act, 4, (tiles, 8)) as i:
                for s in range(2):
                    head = 2 * i + s
                    act.wait_ge(hgrn_done, 1 + head)
                    evac(hq, banks[0][:, 0:T])
                    act.wait_ge(tile_done, tiles.value(1))
                    nc.scalar.activation(hneg, banks[1][:, 0:T], ACT.Sigmoid, scale=-1.0).then_inc(decay_in, 1)
                    evac(hsig, banks[1][:, 0:T], ACT.Sigmoid)
                    act.wait_ge(tile_evac, tiles.value())
                    nc.scalar.activation(hlf, hsig, ACT.Ln, bias=lbc[:, 2, ds(head, 1)], scale=lbc[:, 3, ds(head, 1)]).then_inc(decay_in, 1)
                    evac(hv[:, :, :], banks[2][:, 0:T].rearrange("p (c v) -> p c v", v=P))
                    act.wait_ge(decay_exp, head + 1)
                    nc.scalar.activation(hE, hE, ACT.Exp).then_inc(decayed, 1)
                    evac(hz, banks[3][:, 0:T], ACT.Silu)
                    act.wait_ge(o_ready, head + 1)
                    nc.scalar.activation(hsq, banks[5][:, 0:T], ACT.Square).then_inc(osq_ready, 1)
                    act.wait_ge(oss_ready, head + 1)
                    nc.scalar.activation(hon, banks[6][:, 0:T], ACT.Sqrt, bias=eps_col[:, :],
                                         scale=1.0 / P).then_inc(orms_ready, 1)

            act.wait_ge(gates_mm, 4)
            nc.scalar.activation(g8[:, 0, :], banks[4][0:8, 0:T], ACT.Sigmoid).then_inc(decay_in, 1)
            nc.scalar.activation(gbias[:, 4:5], gbias[:, 2:3], ACT.Exp).then_inc(decay_in, 1)
            soft(2)

            def take_qkv(m):
                evac(draw[:, m, 3:T + 3], banks[m % 2][:, 0:T])

            def silus(g):
                act.wait_ge(conv_in, g + 1)
                nc.scalar.activation(dc, dy, ACT.Silu).then_inc(silu_done, 1)
                act.wait_ge(silu_done, g + 1)
                nc.scalar.activation(dsq, dc[:, 0:2, :], ACT.Square).then_inc(qk_sq, 1)

            for m in range(4):
                take_qkv(m)
            silus(0)

            def delta(g, last=False):
                act.wait_ge(qk_ss, g + 1)
                nc.scalar.activation(drt, banks[4].rearrange("p (k t) -> p k t", t=T), ACT.Sqrt,
                                     bias=eps_col[:, :]).then_inc(qk_rms, 1)
                act.wait_ge(v_turned, g + 1)
                for n in range(2):
                    for c in range(TT):
                        ins = nc.scalar.activation(dbv[:, n * TT + c, :], banks[5][:, (n * TT + c) * P:(n * TT + c + 1) * P],
                                                   ACT.Copy, scale=colT[:, 2, c, ds(2 * g + n, 1)])
                ins.then_inc(bv_ready, 1)
                act.wait_ge(delta_done, 1 + g)
                for m in range(2):
                    evac(dz[:, m, :], banks[2 + m][:, 0:T], ACT.Silu)
                if not last:
                    act.wait_ge(conv_in, g + 1)
                    take_qkv(0)
                act.wait_ge(dex_ready, g + 1)
                nc.scalar.activation(dW, dW, ACT.Exp).then_inc(dex_done, 1)
                if not last:
                    take_qkv(1)
                for l in range(1, 7):
                    act.wait_ge(lv_cd, g * 6 + l)
                    nc.scalar.activation(dcd, banks[4].rearrange("p (q t) -> p q t", t=P), ACT.Copy).then_inc(lv_cd_copied, 1)
                    if not last and l in (2, 4):
                        take_qkv(1 + l // 2)
                if not last:
                    silus(g + 1)
                act.wait_ge(u1_mm, g + 1)
                nc.scalar.activation(du[:, 0:4:2, :], banks[4][:, 0:T].rearrange("p (q t) -> p q t", t=P), ACT.Copy).then_inc(u1_copied, 1)
                act.wait_ge(u2_mm, g + 1)
                nc.scalar.activation(du[:, 1:4:2, :], banks[6][:, 0:T].rearrange("p (q t) -> p q t", t=P), ACT.Copy).then_inc(u2_copied, 1)
                act.wait_ge(o_ready, 8 + g + 1)
                nc.scalar.activation(dosq, banks[7].rearrange("p (q t) -> p q t", t=T), ACT.Square).then_inc(osq_ready, 1)
                act.wait_ge(oss_ready, 8 + g + 1)
                nc.scalar.activation(don, banks[4].rearrange("p (q t) -> p q t", t=T), ACT.Sqrt, bias=eps_col[:, :],
                                     scale=1.0 / P).then_inc(orms_ready, 1)

            with rounds(act, GROUPS - 1, (tiles, 6)) as g:
                delta(g)
            delta(GROUPS - 1, last=True)

            act.wait_ge(delta_done, 1 + GROUPS)
            residual(2, False)
            act.wait_ge(resid_done, 1 + 4)
            squares_of(XT)
            root(4)

            act.wait_ge(normed, 4)
            for m in range(4):
                evac(ekey[:, 4 * m:4 * m + 4, :], banks[m].rearrange("p (q n) -> p q n", n=P))
            with rounds(act, 4, (tiles, 4)) as i:
                for s in range(2):
                    for m in range(2):
                        evac(eq_h[:, s, m, :], banks[2 * s + m][:, 0:T])
                    act.wait_ge(keyscore, 2 * i + s + 1)
                    act.wait_ge(picked, 1 + 2 * i)
                    nc.scalar.activation(esc[:, s, :, :, :], banks[4 + s].rearrange("p (c a n) -> p c a n", c=2, a=2),
                                         ACT.Copy).then_inc(keyscore_copied, 1)
            act.wait_ge(best_in, 1)
            nc.scalar.activation(eexp, ebest, ACT.Exp).then_inc(best_exp, 1)
            for c in range(TT):
                evac(slt[:, :, c * P:(c + 1) * P], banks[c][:, 0:3 * P].rearrange("p (r t) -> p r t", t=P))

            act.wait_ge(kept, 16)
            with rounds(act, T // 8) as i:
                for s in range(2):
                    act.wait_ge(gmat, 2 * i + s + 1)
                    nc.scalar.activation(G[:, :, ds(8 * i + 4 * s, 4)], banks[4 + s].rearrange("p (q e) -> p e q", e=P),
                                         ACT.Copy).then_inc(gmat_out, 1)

            act.wait_ge(onehot, T // 4)
            act.wait_ge(gmat, T // 4)
            for q in range(4):
                nc.scalar.activation(h_hi[:, 4 * q:4 * q + 4, :], hT[:, 4 * q:4 * q + 4, :], ACT.Copy).then_inc(h_rounded, 1)

            def gelu(n, b, c):
                if c == 0:
                    act.wait_ge(u_used, 16 * n + 16)
                nc.scalar.activation(gact[:, c, :], banks[b + c][:, :], ACT.Gelu).then_inc(gelu_done, 1)

            def round_u(n, b, first=False):
                for k in range(KT):
                    j = 16 * n + k
                    act.wait_ge(turn_done, j + 1)
                    if not (first and k < 4):
                        act.wait_ge(u_used, j - 3)
                    nc.scalar.activation(u_hi[:, k % 4, :], banks[k % 4][:, :], ACT.Copy).then_inc(u_rounded, 1)
                    if not first and k in (3, 4):
                        gelu(n - 1, b, k - 3)

            round_u(0, 6, True)
            round_u(1, 4)
            with rounds(act, U_CHUNKS // 2 - 1) as i:
                act.wait_ge(act_turned, 2 * i + 1)
                round_u(2 * i + 2, 6)
                act.wait_ge(act_turned, 2 * i + 2)
                round_u(2 * i + 3, 4)
            act.wait_ge(act_turned, U_CHUNKS - 1)
            gelu(U_CHUNKS - 1, 6, 0)
            gelu(U_CHUNKS - 1, 6, 1)

            act.wait_ge(act_turned, U_CHUNKS)
            act.wait_ge(wmul, 1 + 2 * U_CHUNKS)

            def round_halves(i, first):
                for u in range(4):
                    if u % 2 == 0:
                        act.wait_ge(v_landed[u // 2], 16 * i + 16)
                    if not (first and u < 2):
                        act.wait_ge(y_done, 4 * i + (u - 1))
                    nc.scalar.activation(v_hi[:, u % 2, :], peer_ring[u // 2][:, u % 2, :], ACT.Copy)
                    nc.scalar.activation(w_hi[:, u % 2, :], G[:, ds(4 * i + u, 1), :].rearrange("p o t -> p (o t)"),
                                         ACT.Copy).then_inc(hi_ready, 1)

            round_halves(0, True)
            with rounds(act, N_KEYS // 4 - 1) as i:
                round_halves(i + 1, False)
            act.wait_ge(y_done, N_KEYS)
            act.wait_ge(lo_ready, N_KEYS)
            for b in range(4):
                nc.scalar.activation(xrow[:, 0, b * 512:(b + 1) * 512], banks[b][:, :], ACT.Copy).then_inc(y_rows_act, 1)

            act.wait_ge(y_added, 1)
            squares_of(XT)
            root(5)
            act.wait_ge(normed, 5)
            for n in range(8):
                evac(xout[:, n // 4, (n % 4) * 512:(n % 4 + 1) * 512], banks[n % 4][:, :])

        @block.vector
        def _(dve):
            v = nc.vector
            steps = Count(dve_step, "dve steps")
            tiles = Count(tile_evac, "dve tiles")

            def link(ins):
                ins.then_inc(dve_step, 1)
                dve.wait_ge(dve_step, steps.up())

            carried = [0]

            def carry():
                carried[0] += 1
                v.memset(carrier[:, carried[0] % 64:carried[0] % 64 + 1], 0.0)

            def pcol(at, n=1):
                return par[:, ds(at, n)]

            def norm(n, dst, wcol):
                dve.wait_ge(rms_ready, n)
                link(v.reciprocal(rms_t[:, 1, :], rms_t[:, 0, :]))
                for k in range(KT):
                    ins = v.scalar_tensor_tensor(out=dst[:, k, :], in0=XT[:, k, :], scalar=wcol[:, k:k + 1],
                                                 in1=rms_t[:, 1, :], op0=ALU.mult, op1=ALU.mult)
                ins.then_inc(normed, 1)

            for n, free in enumerate((conv_done, mlstm_done, merge_done, resid_done, hgrn_done, delta_done,
                                      keyscore_copied, picked, wmul)):
                v.memset(w1s[:, n:n + 1], 0.0).then_inc(free, 1)
            dve.wait_ge(c_ready, 1)
            land = [Count(landed[0], "dve slot 0"), Count(landed[1], "dve slot 1")]
            with rounds(dve, 6, (steps, 2 * ADA_DVE - 2), (land[0], 16), (land[1], 16)) as i:
                for n in range(2):
                    dve.wait_ge(landed[n], land[n].up(16))
                    w = ring[n][:, 0:KT * 512].rearrange("p (k c) -> p k c", c=512)
                    ins = v.tensor_scalar(ada_acc[n], w[:, 0, :], cact[:, 0:1], None, ALU.mult)
                    for k in range(1, ADA_DVE):
                        link(ins)
                        ins = v.scalar_tensor_tensor(out=ada_acc[n], in0=w[:, k, :], scalar=cact[:, k:k + 1],
                                                     in1=ada_acc[n], op0=ALU.mult, op1=ALU.add)
                    ins.then_inc(ada_part, 1)
            dve.wait_ge(mod_turned, 1)
            v.memset(cu, 0.0).then_inc(pads_done, 1)
            tiles.n = SETUP + ADA
            dve.wait_ge(act_step, 1)
            link(v.tensor_tensor(lbc[:, 2, :], lbc[:, 0, :], lbc[:, 1, :], ALU.add))
            link(v.reciprocal(lbc[:, 3, :], lbc[:, 2, :]))
            link(v.tensor_tensor(lbc[:, 2, :], lbc[:, 0, :], lbc[:, 3, :], ALU.mult))
            link(v.tensor_scalar(lbc[:, 3, :], lbc[:, 2, :], -1.0, 1.0, ALU.mult, ALU.add))
            link(v.tensor_tensor(mod[:, :], banks[4][:, 0:48], par[:, PK_BADA:PK_BADA + 48], ALU.add))
            v.scalar_tensor_tensor(out=w1s[:, :], in0=mod[:, 16:32], scalar=1.0, in1=par[:, PK_NORM1:PK_NORM1 + KT],
                                   op0=ALU.add, op1=ALU.mult).then_inc(mod_ready, 1)
            dve.wait_ge(mod_ready, 1)
            norm(1, hT, w1s)

            I, F_, AB, LF, F, A, MX, Z = (g8[:, n, :] for n in range(8))
            link(v.memset(Z, 0.0))
            dve.wait_ge(gates_mm, 2)
            v.tensor_scalar(I, banks[4][0:8, 0:T], gbias[:, 0:1], None, ALU.add)
            link(v.tensor_scalar(F_, banks[5][0:8, 0:T], gbias[:, 1:2], None, ALU.add))
            v.scalar_tensor_tensor(out=AB, in0=F_, scalar=-1.0, in1=F_, op0=ALU.mult, op1=ALU.max).then_inc(gates_abs, 1)
            dve.wait_ge(gates_log, 1)
            link(v.scalar_tensor_tensor(out=LF, in0=F_, scalar=0.0, in1=AB, op0=ALU.min, op1=ALU.subtract))
            link(v.tensor_tensor_scan(F, LF, Z, 0.0, ALU.add, ALU.add))
            link(v.tensor_tensor(A, I, F, ALU.subtract))
            v.tensor_tensor_scan(MX, A, A, 0.0, ALU.max, ALU.max).then_inc(gates_rows, 1)
            dve.wait_ge(gates_rows, 1)
            link(v.tensor_scalar(AB, MX, -1.0, None, ALU.mult))
            link(v.tensor_tensor(LF, AB, F, ALU.subtract))

            def spread_rows(n, row):
                link(v.tensor_tensor(spread[:, n, :, :], b3(row, 8),
                                     ident[0:8, 0:8].unsqueeze(2).broadcast_to([8, 8, T]), ALU.mult))

            spread_rows(0, AB)
            spread_rows(1, LF)

            dve.wait_ge(pads_done, 1)
            with rounds(dve, 8, (steps, 7), (tiles, 8)) as j:
                dve.wait_ge(tile_evac, tiles.value(4))
                link(v.tensor_tensor(cu[:, :, 2:T + 2], cv[:, 0:2, :], cv[:, 2:4, :], ALU.mult))
                for tap in (2, 1, 0):
                    for n in range(2):
                        wc = pcol(2 * j + (PK_CONV + tap * 16 + n))
                        if tap == 2:
                            ins = v.tensor_scalar(cy[:, n, :], cu[:, n, 2:T + 2], wc, None, ALU.mult)
                        else:
                            ins = v.scalar_tensor_tensor(out=cy[:, n, :], in0=cu[:, n, tap:tap + T], scalar=wc,
                                                         in1=cy[:, n, :], op0=ALU.mult, op1=ALU.add)
                        if n == 1:
                            link(ins)
                dve.wait_ge(tile_evac, tiles.value(8))
                link(v.tensor_tensor(cy, cy, cv[:, 4:6, :], ALU.mult))
                link(v.tensor_tensor(cy, cy, cv[:, 6:8, :], ALU.mult))
                link(v.tensor_copy(HB[:, ds(2 * j, 2), :], cy))
                ins = v.memset(cy[:, 0, 0:1], 0.0)
                ins.then_inc(conv_done, 1)
                tiles.up(8)

            dve.wait_ge(gates_tp, 1)
            v.tensor_copy(colT[:, 0, :, :], banks[6][:, 0:16].rearrange("p (c h) -> p c h", h=8)).then_inc(gates_done, 1)

            with rounds(dve, 8, (steps, 7), (tiles, 8)) as h:
                dve.wait_ge(scores_ready, h + 1)
                v.tensor_scalar(mE[:, 0:T], banks[6][:, 0:T], colT[:, 0, 0, ds(h, 1)], 0.0, ALU.add, ALU.min)
                v.tensor_scalar(mE[:, T:T + P], banks[6][:, P:T], colT[:, 0, 1, ds(h, 1)], 0.0, ALU.add,
                                ALU.min).then_inc(expo_ready, 1)
                dve.wait_ge(causal_done, h + 1)
                v.scalar_tensor_tensor(out=mS, in0=banks[4][:, 0:384], scalar=float(128 ** -0.5), in1=mE,
                                       op0=ALU.mult, op1=ALU.mult).then_inc(att_ready, 1)
                dve.wait_ge(num_ready, h + 1)
                dve.wait_ge(floor_done, h + 1)
                link(v.tensor_tensor(mden[:, 0, :], banks[6][:, 0:T], mfloor, ALU.max))
                link(v.scalar_tensor_tensor(out=mden[:, 0, :], in0=banks[6][:, 0:T], scalar=-1.0, in1=mden[:, 0, :],
                                            op0=ALU.mult, op1=ALU.max))
                link(v.reciprocal(mden[:, 0, :], mden[:, 0, :]))
                link(v.tensor_tensor(mh, banks[5].rearrange("p (n t) -> p n t", t=T), b3(mden[:, 0, :], 2), ALU.mult))
                dve.wait_ge(tile_evac, tiles.value(6))
                v.tensor_tensor(mh, mh, mo, ALU.mult).then_inc(h_ready, 1)
                dve.wait_ge(h_ready, h + 1)
                dve.wait_ge(hrms_ready, h + 1)
                link(v.reciprocal(mden[:, 1, :], mden[:, 1, :]))
                for n in range(2):
                    ins = v.scalar_tensor_tensor(out=mh[:, n, :], in0=mh[:, n, :], scalar=pcol(2 * h + (PK_HEADN + n)),
                                                 in1=mden[:, 1, :], op0=ALU.mult, op1=ALU.mult)
                link(ins)
                dve.wait_ge(tile_evac, tiles.value(8))
                link(v.tensor_tensor(mh, mh, mz, ALU.mult))
                v.tensor_copy(HA[:, ds(2 * h, 2), :], mh).then_inc(mlstm_done, 1)
                tiles.up(8)

            with rounds(dve, 8, (steps, 1), (tiles, 8)) as j:
                tiles.up(8)
                dve.wait_ge(tile_evac, tiles.value())
                link(v.tensor_tensor(prod, sg, yy, ALU.mult))
                v.tensor_tensor(MG[:, ds(2 * j, 2), :], prod[:, 0:2, :], prod[:, 2:4, :], ALU.add).then_inc(merge_done, 1)

            def residual():
                with rounds(dve, 2, (tiles, 8)) as i:
                    for s in range(2):
                        tiles.up(4)
                        dve.wait_ge(tile_evac, tiles.value())
                        part = XT[:, ds(8 * i + 4 * s, 4), :]
                        ins = v.tensor_tensor(part, part, upd[:, 4 * s:4 * s + 4, :], ALU.add)
                    ins.then_inc(resid_done, 1)

            residual()
            norm(2, XT, par[:, PK_NORMF:PK_NORMF + KT])
            norm(3, hT, par[:, PK_ATTN:PK_ATTN + KT])

            link(v.memset(zrow, 0.0))
            link(v.memset(hatt, 0.0))
            dve.wait_ge(masks_done, 1)
            with rounds(dve, 4, (steps, 10), (tiles, 8)) as i:
                for s in range(2):
                    head = 2 * i + s
                    dve.wait_ge(decay_in, 2 * head + 2)
                    v.tensor_scalar(hk, hneg, lbc[:, 3, ds(head, 1)], None, ALU.mult)
                    link(v.tensor_tensor_scan(hb, hlf, zrow, 0.0, ALU.add, ALU.add))
                    for l, half in enumerate(LEVELS + [128]):
                        bb = hb.rearrange("p (n s t) -> p n s t", s=2, t=half)
                        ee = hE[:, l, :].rearrange("p (n s t) -> p n s t", s=2, t=half)
                        nb = T // (2 * half)
                        ref = bb[:, :, 0, half - 1:half].broadcast_to([P, nb, half])
                        v.tensor_tensor(ee[:, :, 1, :], bb[:, :, 1, :], ref, ALU.subtract)
                        ins = v.tensor_tensor(ee[:, :, 0, :], ref, bb[:, :, 0, :], ALU.subtract)
                    ins.then_inc(decay_exp, 1)
                    dve.wait_ge(decayed, head + 1)
                    dve.wait_ge(dve_step, steps.value())
                    for l, half in enumerate(LEVELS + [128]):
                        qq, kk, ee, xx = (y.rearrange("p (n s t) -> p n s t", s=2, t=half)
                                          for y in (hq, hk, hE[:, l, :], hX[:, l, :]))
                        v.tensor_tensor(xx[:, :, 1, :], qq[:, :, 1, :], ee[:, :, 1, :], ALU.mult)
                        ins = v.tensor_tensor(xx[:, :, 0, :], kk[:, :, 0, :], ee[:, :, 0, :], ALU.mult)
                    ins.then_inc(x_levels, 1)
                    for l in range(9):
                        dve.wait_ge(gram_done, head * 9 + l + 1)
                        dve.wait_ge(gram_taken, head * 9 + l)
                        if l:
                            carry()
                        b = banks[4 + l % 4]
                        if l == 0:
                            ins = v.tensor_copy(hatt[:, 1, :], b[:, 0:P])
                        else:
                            mask = masks[:, l - 1, :] if l < 8 else ident[:, :]
                            ins = v.copy_predicated(hatt[:, 0:3:2, :], b3(mask, 2).bitcast(U32),
                                                    b[:, 0:T].rearrange("p (c t) -> p c t", t=P))
                        ins.then_inc(gram_taken, 1)
                    dve.wait_ge(orms_ready, head + 1)
                    link(v.reciprocal(hsig, hon))
                    link(v.scalar_tensor_tensor(out=hneg, in0=banks[5][:, 0:T], scalar=par[:, PK_HGN:PK_HGN + 1],
                                                in1=hsig, op0=ALU.mult, op1=ALU.mult))
                    tiles.up(4)
                    dve.wait_ge(tile_evac, tiles.value())
                    link(v.tensor_tensor(hneg, hneg, hz, ALU.mult))
                    link(v.tensor_copy(MIX[:, ds(head, 1), :].rearrange("p o t -> p (o t)"), hneg))
                    v.memset(hb[:, 0:1], 0.0).then_inc(hgrn_done, 1)

            link(v.memset(Z, 0.0))
            link(v.memset(draw, 0.0))
            dve.wait_ge(gates_mm, 4)
            link(v.tensor_scalar(F_, banks[5][0:8, 0:T], gbias[:, 3:4], None, ALU.add))
            v.scalar_tensor_tensor(out=AB, in0=F_, scalar=-1.0, in1=F_, op0=ALU.mult, op1=ALU.max).then_inc(gates_abs, 1)
            dve.wait_ge(gates_log, 2)
            link(v.scalar_tensor_tensor(out=LF, in0=F_, scalar=0.0, in1=AB, op0=ALU.max, op1=ALU.add))
            dve.wait_ge(decay_in, 18)
            link(v.tensor_scalar(LF, LF, gbias[:, 4:5], -1.0, ALU.mult, ALU.mult))
            v.tensor_tensor_scan(F, LF, Z, 0.0, ALU.add, ALU.add).then_inc(gates_rows, 1)
            dve.wait_ge(gates_rows, 2)
            spread_rows(0, F)
            spread_rows(1, I)
            dve.wait_ge(gates_tp, 2)
            v.tensor_copy(colT[:, 1:3, :, :], banks[6][:, 0:32].rearrange("p (r c h) -> p r c h", r=2, h=8)).then_inc(gates_done, 1)

            def conv_taps(g, pair, taps):
                for tap in taps:
                    for m in (2 * pair, 2 * pair + 1):
                        wc = pcol((g, 4 + g, 8 + 2 * g, 9 + 2 * g)[m] + (PK_GCONV + 16 * tap))
                        if tap == 0:
                            ins = v.tensor_scalar(dy[:, m, :], draw[:, m, 0:T], wc, None, ALU.mult)
                        else:
                            ins = v.scalar_tensor_tensor(out=dy[:, m, :], in0=draw[:, m, tap:tap + T], scalar=wc,
                                                         in1=dy[:, m, :], op0=ALU.mult, op1=ALU.add)
                    if tap < TAPS - 1:
                        link(ins)
                    elif pair == 1:
                        ins.then_inc(conv_in, 1)

            tiles.up(4)
            dve.wait_ge(tile_evac, tiles.value())
            for pair in range(2):
                conv_taps(0, pair, range(TAPS))

            def delta(g, last=False):
                dve.wait_ge(qk_rms, g + 1)
                link(v.reciprocal(drt, drt))
                v.scalar_tensor_tensor(out=dqk[:, 0, :], in0=dc[:, 0, :], scalar=float(128 ** -0.5), in1=drt[:, 0, :],
                                       op0=ALU.mult, op1=ALU.mult)
                v.tensor_tensor(dqk[:, 1, :], dc[:, 1, :], drt[:, 1, :], ALU.mult).then_inc(qk_unit, 1)
                dve.wait_ge(bc_ready, g + 1)
                for n in range(2):
                    for c in range(TT):
                        dst = dW[:, 3 * n:3 * n + 2, :].rearrange("p a t -> p (a t)") if c == 0 else dW[:, 3 * n + 2, :]
                        ins = v.tensor_scalar(dst, banks[4 + n][:, c * P:T], colT[:, 1, c, ds(2 * g + n, 1)], 0.0,
                                              ALU.subtract, ALU.min)
                ins.then_inc(dex_ready, 1)
                dve.wait_ge(dmask_done, g + 1)
                for n in range(2):
                    w = dW[:, 3 * n:3 * n + 3, :]
                    ins = v.tensor_tensor(dM[:, 3 * n:3 * n + 3, :], banks[6][:, 0:384].rearrange("p (a t) -> p a t", t=P), w, ALU.mult)
                link(ins)
                for n in range(2):
                    w = dM[:, 3 * n:3 * n + 2, :]
                    v.tensor_tensor(w, w, banks[4 + n][:, T:2 * T].rearrange("p (a t) -> p a t", t=P), ALU.mult)
                    w = dM[:, 3 * n + 2, :]
                    ins = v.tensor_tensor(w, w, banks[4 + n][:, T + P:2 * T], ALU.mult)
                link(ins)

                def cross(l):
                    for n in range(2):
                        ins = v.tensor_tensor(dC[:, 2 * n:2 * n + 2, :], dM[:, 3 * n:3 * n + 3:2, :], b3(masks[:, l, :], 2), ALU.mult)
                    return ins

                cross(0).then_inc(lv_mask, 1)
                for n in range(2):
                    w = dW[:, 3 * n:3 * n + 3, :]
                    v.tensor_tensor(dA[:, 3 * n:3 * n + 3, :], banks[7][:, 0:384].rearrange("p (a t) -> p a t", t=P), w, ALU.mult)
                dve.wait_ge(lv_mask, g * 7 + 1)
                v.tensor_tensor(dD[:, 4:8, :], b3(ident[:, :], 4), dC, ALU.subtract)
                dve.wait_ge(lv_dd, g * 7 + 1)
                link(v.tensor_tensor(dD[:, 0:4, :], b3(ident[:, :], 4), banks[5].rearrange("p (q t) -> p q t", t=P), ALU.subtract))
                cross(1).then_inc(lv_mask, 1)
                for l in range(2, 7):
                    dve.wait_ge(lv_dd, g * 7 + l)
                    v.tensor_tensor(dD[:, 0:4, :], dD[:, 0:4, :], banks[5].rearrange("p (q t) -> p q t", t=P), ALU.subtract)
                    v.tensor_tensor(dD[:, 4:8, :], dD[:, 4:8, :], banks[6].rearrange("p (q t) -> p q t", t=P), ALU.subtract)
                    cross(l).then_inc(lv_mask, 1)
                    if not last and l > 2:
                        if l in (3, 5):
                            dve.wait_ge(tile_evac, tiles.value(l + 1))
                        conv_taps(g + 1, (l - 3) // 2, ((2, 3) if l % 2 == 0 else (0, 1)))
                dve.wait_ge(lv_dd, g * 7 + 7)
                v.tensor_tensor(dD[:, 4:8, :], dD[:, 4:8, :], banks[6].rearrange("p (q t) -> p q t", t=P), ALU.subtract).then_inc(lv_new, 1)
                dve.wait_ge(r2_mm, g + 1)
                v.tensor_tensor(dr2, dbv[:, 1:4:2, :], banks[5][:, 0:T].rearrange("p (q t) -> p q t", t=P), ALU.subtract).then_inc(r2_ready, 1)
                dve.wait_ge(orms_ready, 8 + g + 1)
                link(v.reciprocal(don, don))
                link(v.scalar_tensor_tensor(out=dosq, in0=banks[7].rearrange("p (q t) -> p q t", t=T),
                                            scalar=par[:, PK_GDN:PK_GDN + 1], in1=don, op0=ALU.mult, op1=ALU.mult))
                v.tensor_tensor(MIX[:, ds(8 + 2 * g, 2), :], dosq, dz, ALU.mult).then_inc(delta_done, 1)
                tiles.up(2 if last else 6)

            with rounds(dve, GROUPS - 1, (steps, 3 + 1 + 2 + 6), (tiles, 6)) as g:
                delta(g)
            delta(GROUPS - 1, last=True)

            residual()
            norm(4, hT, par[:, PK_FFN:PK_FFN + KT])

            def top16(vals, idx, src, spare):
                carry()
                link(v.max(vals[:, 0:8], src))
                carry()
                v.max_index(idx[:, 0:8], vals[:, 0:8], src)
                link(v.match_replace(spare, vals[:, 0:8], src, -3.0e38))
                carry()
                link(v.max(vals[:, 8:16], spare))
                carry()
                return v.max_index(idx[:, 8:16], vals[:, 8:16], spare)

            with rounds(dve, 4, (steps, 54)) as i:
                for s in range(2):
                    head = 2 * i + s
                    dve.wait_ge(keyscore_copied, 1 + head + 1)
                    for c in range(TT):
                        for half in range(2):
                            ins = top16(ev[:, c, half, :], ei[:, c, half, :], esc[:, s, c, half, :], esc2[:, c, half, :])
                    link(ins)
                    link(v.tensor_copy(eif, ei))
                    for c in range(TT):
                        ins = v.tensor_tensor(ecand[:, c, :].rearrange("p (i j) -> p i j", j=TOPK),
                                              ev[:, c, 0, :].unsqueeze(2).broadcast_to([P, TOPK, TOPK]),
                                              b3(ev[:, c, 1, :], TOPK), ALU.add)
                    link(ins)
                    for c in range(TT):
                        ins = top16(ebv[:, c, :], ebp[:, c, :], ecand[:, c, :], ecand2[:, c, :])
                    link(ins)
                    v.tensor_scalar(ehl[:, 0, :, :], ebp, 4, None, ALU.logical_shift_right)
                    link(v.tensor_scalar(ehl[:, 1, :, :], ebp, 15, None, ALU.bitwise_and))
                    link(v.tensor_copy(ehf, ehl))
                    for q in range(2):
                        ins = v.tensor_tensor(eeq[:, q, :, :, :], ehf[:, q, :, :].unsqueeze(3).broadcast_to([P, 2, TOPK, TOPK]),
                                              iota[:, 0:TOPK].unsqueeze(1).unsqueeze(1).broadcast_to([P, 2, TOPK, TOPK]), ALU.is_equal)
                    link(ins)
                    for q in range(2):
                        ins = v.tensor_tensor(eeq[:, q, :, :, :], eeq[:, q, :, :, :],
                                              eif[:, :, q, :].unsqueeze(2).broadcast_to([P, 2, TOPK, TOPK]), ALU.mult)
                    link(ins)
                    for q in range(2):
                        v.tensor_reduce(e12[:, q, :, ds(head * TOPK, TOPK)], eeq[:, q, :, :, :], AX.X, ALU.add)
                    link(v.tensor_tensor(ebest[:, :, ds(head * TOPK, TOPK)], ebv, ebv[:, :, 0:1].broadcast_to([P, 2, TOPK]), ALU.subtract))
                    v.memset(esum[:, 0:1], 0.0).then_inc(picked, 1)
            dve.wait_ge(picked, 1 + 8)
            v.memset(esum[:, 1:2], 0.0).then_inc(best_in, 1)
            dve.wait_ge(best_exp, 1)
            es = esum[:, 0:16].rearrange("p (c h) -> p c h", h=8)
            ex = eexp.rearrange("p c (h k) -> p c h k", k=TOPK)
            link(v.tensor_reduce(es, ex, AX.X, ALU.add))
            link(v.reciprocal(es, es))
            v.tensor_tensor(ex, ex, es.unsqueeze(3).broadcast_to([P, 2, 8, TOPK]), ALU.mult).then_inc(slots_ready, 1)

            tiles.n = FINAL_TILES
            dve.wait_ge(tile_evac, tiles.value())

            def onehots(i, first):
                for s in range(2):
                    n = 2 * i + s
                    if not first:
                        dve.wait_ge(gmat, n - 1)
                    for q in range(4):
                        t = 8 * i + (4 * s + q)
                        v.tensor_scalar(oh[:, s, q, 0, :], iota[:, :], slt[:, 0, ds(t, 1)], slt[:, 2, ds(t, 1)],
                                        ALU.is_equal, ALU.mult)
                        ins = v.tensor_scalar(oh[:, s, q, 1, :], iota[:, :], slt[:, 1, ds(t, 1)], None, ALU.is_equal)
                    ins.then_inc(onehot, 1)

            onehots(0, True)
            with rounds(dve, T // 8 - 1) as i:
                onehots(i + 1, False)

            dve.wait_ge(gmat_out, T // 4)
            for q in range(4):
                dve.wait_ge(h_rounded, q + 1)
                v.tensor_tensor(h_lo[:, 4 * q:4 * q + 4, :], hT[:, 4 * q:4 * q + 4, :],
                                h_hi[:, 4 * q:4 * q + 4, :].bitcast(F32), ALU.subtract).then_inc(h_split, 1)

            def weigh(n, b, m):
                if m == 0:
                    dve.wait_ge(act_turned, n + 1)
                g = G[:, ds(4 * n + 2 * m, 2), :]
                v.tensor_tensor(g, g, banks[b + m].rearrange("p (e t) -> p e t", t=T), ALU.mult).then_inc(wmul, 1)

            def split_u(n, b, first=False):
                for k in range(KT):
                    dve.wait_ge(u_rounded, 16 * n + (k + 1))
                    v.tensor_tensor(u_lo[:, k % 4, :], banks[k % 4][:, :], u_hi[:, k % 4, :].bitcast(F32),
                                    ALU.subtract).then_inc(u_split, 1)
                    if not first and k in (11, 12):
                        weigh(n - 1, b, k - 11)

            split_u(0, 6, True)
            split_u(1, 4)
            with rounds(dve, U_CHUNKS // 2 - 1) as i:
                split_u(2 * i + 2, 6)
                split_u(2 * i + 3, 4)
            weigh(U_CHUNKS - 1, 6, 0)
            weigh(U_CHUNKS - 1, 6, 1)

            def leave_halves(i, first):
                for u in range(4):
                    dve.wait_ge(hi_ready, 4 * i + (u + 1))
                    v.tensor_tensor(v_lo[:, u % 2, :], peer_ring[u // 2][:, u % 2, :], v_hi[:, u % 2, :].bitcast(F32), ALU.subtract)
                    v.tensor_tensor(w_lo[:, u % 2, :], G[:, ds(4 * i + u, 1), :].rearrange("p o t -> p (o t)"),
                                    w_hi[:, u % 2, :].bitcast(F32), ALU.subtract).then_inc(lo_ready, 1)

            with rounds(dve, N_KEYS // 4) as i:
                leave_halves(i, False)
            dve.wait_ge(y_done, N_KEYS)
            dve.wait_ge(lo_ready, N_KEYS)
            for b in range(4):
                v.tensor_copy(xrow[:, 1, b * 512:(b + 1) * 512], banks[4 + b][:, :]).then_inc(y_rows_dve, 1)
            dve.wait_ge(x_back, 16)
            for b in range(8):
                dve.wait_ge(y_turned, b + 1)
                part = XT[:, 2 * b:2 * b + 2, :]
                ins = v.tensor_tensor(part, part, banks[b].rearrange("p (k t) -> p k t", t=T), ALU.add)
            ins.then_inc(y_added, 1)
            dve.wait_ge(y_added, 1)
            norm(5, hT, par[:, PK_FINAL:PK_FINAL + KT])

        @block.gpsimd
        def _(pool):
            steps = Count(pool_step, "pool steps")

            def link(ins):
                ins.then_inc(pool_step, 1)
                pool.wait_ge(pool_step, steps.up())

            nc.gpsimd.memset(ones[:, :], 1.0)
            nc.gpsimd.memset(eps_col[:, :], EPS)
            link(nc.gpsimd.memset(ident[:, :], 0.0))
            nc.gpsimd.iota(iota[:, :], [[1, P]], base=0, channel_multiplier=0, allow_small_or_imprecise_dtypes=True)
            nc.gpsimd.affine_select(out=ident[:, :], in_=ident[:, :], compare_op=ALU.not_equal, fill=1.0, base=0,
                                    pattern=[[-1, P]], channel_multiplier=1).then_inc(consts, 1)
            link(nc.gpsimd.memset(masks, 1.0))
            for l, half in enumerate(LEVELS):
                nb = P // (2 * half)
                m = masks[:, l, :]
                for sign, base in ((1, 0), (-1, half - 1)):
                    link(nc.gpsimd.affine_select(out=m, in_=m, compare_op=ALU.is_ge, fill=0.0, base=base,
                                                 pattern=[[-sign * 2 * half, nb], [0, 2], [0, half]],
                                                 channel_multiplier=sign))
                ins = nc.gpsimd.affine_select(out=m, in_=m, compare_op=ALU.is_gt, fill=0.0, base=0,
                                              pattern=[[0, nb], [1, 2], [0, half]], channel_multiplier=0)
                link(ins)
            link(nc.gpsimd.memset(causal_mask, 1.0))
            nc.gpsimd.affine_select(out=causal_mask, in_=causal_mask, compare_op=ALU.is_ge, fill=0.0, base=0,
                                    pattern=[[1, P]], channel_multiplier=-1).then_inc(masks_done, 1)
            pool.wait_ge(masks_done, 1)

            def causal(view):
                return nc.gpsimd.tensor_tensor(view, view, b3(causal_mask, 2), ALU.mult)

            with rounds(pool, 8) as h:
                pool.wait_ge(exp_done, h + 1)
                causal(mE.rearrange("p (a t) -> p a t", t=P)[:, 0:3:2, :]).then_inc(causal_done, 1)
            with rounds(pool, GROUPS) as g:
                pool.wait_ge(dex_done, g + 1)
                for n in range(2):
                    ins = causal(dW[:, 3 * n:3 * n + 3:2, :])
                ins.then_inc(dmask_done, 1)


_INS = ['x', 'c', 'norm1_w', 'w_ada', 'b_ada', 'w_in', 'b_in', 'conv_w', 'headnorm_w', 'w_proj_a', 'w_proj_b',
        'w_out', 'normf_w', 'attn_norm_g_2', 'w_in_2', 'hgrn_lb_logits_2', 'hgrn_norm_g_2', 'gdn_conv_w_2',
        'gdn_A_log_2', 'gdn_dt_bias_2', 'gdn_norm_g_2', 'w_out_2', 'ffn_norm_g_2', 'peer_w_query_2',
        'peer_sub_keys_2', 'peer_u_2', 'peer_v_2', 'final_norm_g_2']


def kernel(**inputs):
    import numpy as _np
    import concourse.bacc as _bacc
    from concourse import mybir as _mybir
    from concourse.bass_utils import run_bass_kernel_spmd as _run

    nc = _bacc.Bacc("TRN2", target_bir_lowering=False, num_devices=1)
    arrays, aps = {}, {}
    for name in _INS:
        v = _np.ascontiguousarray(inputs[name])
        arrays[f"in_{name}_dram"] = v
        aps[name] = nc.dram_tensor(f"in_{name}_dram", v.shape, _mybir.dt.from_np(v.dtype), kind="ExternalInput").ap()
    out = nc.dram_tensor("out_dram", (1, T, D), F32, kind="ExternalOutput").ap()
    build(nc, aps, out)
    r = _run(nc, [arrays], core_ids=[0])
    return r.results[0]["out_dram"]
```

```python
from contextlib import ExitStack, contextmanager

import concourse.bass as bass
from concourse import mybir

ALU = mybir.AluOpType
ACT = mybir.ActivationFunctionType
AX = mybir.AxisListType
F32 = mybir.dt.float32
F32R = mybir.dt.float32r
U32 = mybir.dt.uint32
ds = bass.ds

P = 128
T = 256
TT = T // P
D = 2048
KT = D // P
EPS = 1e-6
HEADS = 8
QKW = HEADS * 128
VW = 2048
OFF_K, OFF_V, OFF_O, OFF_Z = QKW, 2 * QKW, 2 * QKW + VW, 2 * QKW + 2 * VW
OFF_I = 2 * QKW + 3 * VW
OFF_U = OFF_I + 2 * HEADS
OFF_B, OFF_C, OFF_ZB, OFF_GA, OFF_GB = (OFF_U + n * D for n in range(1, 6))
IN_1 = OFF_GB + D
OFF2_F, OFF2_I, OFF2_G = 1024, 2048, 3072
OFF2_BQ, OFF2_BK, OFF2_BV, OFF2_BZ = 4096, 4608, 5120, 6144
OFF2_BB = 7168
GROUPS = 4
TAPS = 4
N_KEYS = 128
TOPK = 16
LEVELS = [1, 2, 4, 8, 16, 32, 64]

PK_QKVOZ_B, PK_NORM1, PK_HEADN, PK_NORMF, PK_ATTN = 0, 64, 80, 96, 112
PK_REST_B, PK_FFN, PK_FINAL = 128, 128 + 96, 128 + 112
PK_CONV, PK_BADA, PK_C, PK_HGN, PK_GDN = 256, 256 + 48, 256 + 96, 256 + 112, 256 + 113
PK_GCONV, PK_LB = 384, 384 + 64
PACK_ROWS = [128, 128, 114, 80]

N_PARAMS = 21
SLOT = 8192
ADA_DVE = 6
U_CHUNKS = N_KEYS // 4
PEER_SLOT = 4096


class Count:

    def __init__(self, sem, name=""):
        self.sem, self.n, self.lead, self.name = sem, 0, 0, name

    def value(self, more=0):
        return self.lead + (self.n + more)

    def up(self, k=1):
        self.n += k
        return self.value()


@contextmanager
def rounds(eng, count, *counts):
    with eng.Fori(0, count) as i:
        before = [c.n for c, _ in counts]
        for c, per in counts:
            c.lead = i * per
        yield i
        for (c, per), b in zip(counts, before):
            assert c.n - b == per, (c.name, c.n - b, per)
    for c, per in counts:
        c.lead = 0
        c.n += (count - 1) * per


def build(nc, a, out):
    ctx = ExitStack()
    with ctx:
        def sb(name, shape, dt=F32):
            return ctx.enter_context(nc.sbuf_tensor(name, shape, dt))

        def sem(name):
            return ctx.enter_context(nc.semaphore(name))

        def top():
            return -(-nc.sbuf_base // 32) * 32

        arena_at = top()
        arena = sb("arena", [P, 45056])
        late_at = top()
        late = sb("late", [P, 4096])
        ident = sb("ident", [P, P])
        ones = sb("ones", [P, P])
        iota = sb("iota", [P, P])
        par = sb("par", [P, 512])
        eps_col = sb("eps_col", [P, 1])
        cact = sb("cact", [P, KT])
        mod = sb("mod", [P, 48])
        w1s = sb("w1s", [P, KT])
        lbc = sb("lbc", [P, 4, HEADS])
        rms_t = sb("rms_t", [P, 2, T])
        slt_at = top()
        slt = sb("slt", [P, 3, T])
        carrier = sb("carrier", [P, 64])
        pool_carrier = sb("pool_carrier", [P, 4])
        gact_at = top()
        gact = sb("gact", [P, TT, 512])

        def halves(name, at, k, n):
            return nc.alloc_sbuf_tensor_at(name, [P, k, n], F32R, offset=at)

        h_hi = halves("h_hi", late_at, KT, T)
        h_lo = halves("h_lo", arena_at + 10 * 4096 * 4, KT, T)
        u_hi = halves("u_hi", arena_at + 4096 * 4, 4, 512)
        u_lo = halves("u_lo", arena_at + 6144 * 4, 4, 512)
        hc_hi = halves("hc_hi", arena_at + 5 * 4096 * 4, KT, T)
        hc_lo = halves("hc_lo", arena_at + 7 * 4096 * 4, KT, T)
        wc_hi = halves("wc_hi", arena_at + 2 * 4096 * 4, 8, 512)
        wc_lo = halves("wc_lo", arena_at + 3 * 4096 * 4, 8, 512)
        ho_hi = halves("ho_hi", arena_at + 10 * 4096 * 4, KT, T)
        ho_lo = halves("ho_lo", arena_at + 9 * 4096 * 4, KT, T)
        v_hi = halves("v_hi", arena_at + 10 * 4096 * 4, 2, D)
        v_lo = halves("v_lo", late_at, 2, D)
        w_hi = halves("w_hi", gact_at, 2, T)
        w_lo = halves("w_lo", slt_at, 2, T)

        def slab(n):
            return arena[:, n * 4096:(n + 1) * 4096].rearrange("p (k t) -> p k t", t=T)

        ring = [arena[:, s * SLOT:(s + 1) * SLOT] for s in range(2)]
        peer_ring = [arena[:, s * PEER_SLOT:(s + 1) * PEER_SLOT].rearrange("p (c d) -> p c d", d=D)
                     for s in range(2)]
        half_ring = [arena[:, s * 4096:(s + 1) * 4096].rearrange("p (k c) -> p k c", c=512) for s in range(2)]
        u_ring = [arena[:, s * 2048:(s + 1) * 2048].rearrange("p (e d) -> p e d", d=512) for s in range(2)]
        keys_rows = arena[:, 9 * 4096:9 * 4096 + 2048].rearrange("p (s n) -> p s n", n=P)
        G = arena[:, 2 * 4096:10 * 4096].rearrange("p (e t) -> p e t", t=T)
        XT, HA, HB, MG = slab(4), slab(5), slab(6), slab(7)
        HB2 = HB
        hT = slab(10)
        wk = arena[:, 8 * 4096:10 * 4096]

        ada_acc = [wk[:, 512 + n * 512:1024 + n * 512] for n in range(2)]
        mod_rows = wk[0:48, 1536:1664]
        mod_row = wk[0:1, 2048:2048 + 3 * D]
        dw0 = 6 * 4096

        def dw(at, n):
            return arena[:, dw0 + at:dw0 + at + n]

        def words(at, n):
            return wk[:, at:at + n]

        xrow = arena[:, 5 * 4096:6 * 4096].rearrange("p (c d) -> p c d", d=D)
        vbias = arena[0:1, 7 * 4096:7 * 4096 + VW]
        spread = arena[0:8, 9 * 4096:10 * 4096].rearrange("p (a h t) -> p a h t", a=2, t=T)
        xout = arena[:, 6 * 4096:7 * 4096].rearrange("p (c d) -> p c d", d=D)
        pack = words(0, 512).rearrange("p (k c) -> p k c", c=128)
        causal_mask = late[:, 896:1024]
        masks = late[:, 0:896].rearrange("p (l t) -> p l t", t=P)
        wg = late[:, 1024:1280].rearrange("p (k c) -> p k c", c=16)
        wg2 = late[:, 1280:1536].rearrange("p (k c) -> p k c", c=16)
        gbias = late[0:8, 1536:1544]
        colT = late[:, 1552:1600].rearrange("p (a c h) -> p a c h", a=3, c=TT)
        g8 = late[0:8, 1664:1664 + 8 * T].rearrange("p (a t) -> p a t", t=T)

        banks = [ctx.enter_context(nc.psum_tensor(f"bank{n}", [P, 512], F32)) for n in range(8)]

        def square_bank(n):
            return banks[0 if n == 5 else 5][:, 0:T]

        xkeep = nc.dram_tensor("xkeep", [P, KT, T], F32, kind="Internal").ap()

        landed = [sem("slot0_landed"), sem("slot1_landed")]
        params_in = sem("params_in")
        x_in = sem("x_in")
        keys_in = sem("keys_in")
        vbias_in = sem("vbias_in")
        kept = sem("kept")
        x_back = sem("x_back")
        out_done = sem("out_done")
        consts = sem("consts")
        masks_done = sem("masks_done")
        tile_done = sem("tile_done")
        tile_evac = sem("tile_evac")
        act_step = sem("act_step")
        dve_step = sem("dve_step")
        pool_step = sem("pool_step")
        pads_done = sem("pads_done")
        c_ready = sem("c_ready")
        ada_part = sem("ada_part")
        mod_moved = sem("mod_moved")
        mod_turned = sem("mod_turned")
        mod_ready = sem("mod_ready")
        squares = sem("squares")
        ss_ready = sem("ss_ready")
        rms_ready = sem("rms_ready")
        normed = sem("normed")
        norm_part = sem("norm_part")
        shifted = sem("shifted")
        conv_done = sem("conv_done")
        conv_mixed = sem("conv_mixed")
        hc_rounded = sem("hc_rounded")
        hc_split = sem("hc_split")
        wc_rounded = sem("wc_rounded")
        wc_split = sem("wc_split")
        wc_used = sem("wc_used")
        out_landed = [sem("out_half0_landed"), sem("out_half1_landed")]
        conv_rows = sem("conv_rows")
        gates_mm = sem("gates_mm")
        gates_abs = sem("gates_abs")
        gates_log = sem("gates_log")
        gates_rows = sem("gates_rows")
        gates_tp = sem("gates_tp")
        gates_done = sem("gates_done")
        scores_ready = sem("scores_ready")
        expo_ready = sem("expo_ready")
        exp_done = sem("exp_done")
        floor_done = sem("floor_done")
        causal_done = sem("causal_done")
        att_ready = sem("att_ready")
        num_ready = sem("num_ready")
        h_ready = sem("h_ready")
        hsq_ready = sem("hsq_ready")
        hss_ready = sem("hss_ready")
        hrms_ready = sem("hrms_ready")
        mlstm_done = sem("mlstm_done")
        merge_done = sem("merge_done")
        resid_done = sem("resid_done")
        decay_in = sem("decay_in")
        decay_exp = sem("decay_exp")
        x_levels = sem("x_levels")
        decayed = sem("decayed")
        gram_done = sem("gram_done")
        gram_taken = sem("gram_taken")
        o_ready = sem("o_ready")
        osq_ready = sem("osq_ready")
        oss_ready = sem("oss_ready")
        orms_ready = sem("orms_ready")
        hgrn_done = sem("hgrn_done")
        conv_in = sem("conv_in")
        silu_done = sem("silu_done")
        qk_sq = sem("qk_sq")
        qk_ss = sem("qk_ss")
        qk_rms = sem("qk_rms")
        qk_unit = sem("qk_unit")
        v_turned = sem("v_turned")
        bv_ready = sem("bv_ready")
        bc_ready = sem("bc_ready")
        dex_ready = sem("dex_ready")
        dex_done = sem("dex_done")
        dmask_done = sem("dmask_done")
        lv_mask = sem("lv_mask")
        lv_cd = sem("lv_cd")
        lv_cd_copied = sem("lv_cd_copied")
        lv_dd = sem("lv_dd")
        lv_new = sem("lv_new")
        u1_mm = sem("u1_mm")
        u1_copied = sem("u1_copied")
        r2_mm = sem("r2_mm")
        r2_ready = sem("r2_ready")
        u2_mm = sem("u2_mm")
        u2_copied = sem("u2_copied")
        delta_done = sem("delta_done")
        keyscore = sem("keyscore")
        keyscore_copied = sem("keyscore_copied")
        picked = sem("picked")
        best_in = sem("best_in")
        best_exp = sem("best_exp")
        slots_ready = sem("slots_ready")
        onehot = sem("onehot")
        gated_act = sem("gated_act")
        gated_pool = sem("gated_pool")
        gmat = sem("gmat")
        gmat_out = sem("gmat_out")
        turn_done = sem("turn_done")
        h_rounded = sem("h_rounded")
        h_split = sem("h_split")
        u_rounded = sem("u_rounded")
        u_split = sem("u_split")
        u_used = sem("u_used")
        act_turned = sem("act_turned")
        gelu_done = sem("gelu_done")
        wmul = sem("wmul")
        v_landed = [sem("v_slot0_landed"), sem("v_slot1_landed")]
        hi_ready = sem("hi_ready")
        lo_ready = sem("lo_ready")
        y_rows_act = sem("y_rows_act")
        y_rows_dve = sem("y_rows_dve")
        y_turned = sem("y_turned")
        y_done = sem("y_done")
        y_added = sem("y_added")

        SETUP, ADA = 12, 12
        FINAL_TILES = SETUP + ADA + 3 * 64 + 16 + 32 + 24 + 16 + 4 + 16 + 2

        def b3(ap, n):
            return ap.unsqueeze(1).broadcast_to([ap.shape[0], n, ap.shape[1]])

        def w3(f, at, k, t=T):
            return f(at, k * t).rearrange("p (k t) -> p k t", t=t)

        upd = w3(words, 0, 8)
        sg, yy, prod = w3(words, 0, 4), w3(words, 1024, 4), w3(words, 2048, 4)
        cv, cu, cy = w3(words, 0, 8), w3(words, 2048, 2, T + 2), w3(words, 2564, 2)
        mqk, mv, mo, mz = (w3(words, n * 512, 2) for n in range(4))
        mE, mS, mfloor = words(2048, 384), words(2432, 384), words(2816, T)
        mden, mh = w3(words, 3072, 2), w3(words, 3584, 2)
        msq = arena[:, 7 * 4096 + 2048:7 * 4096 + 2560].rearrange("p (k t) -> p k t", t=T)
        hq, hv, hz = dw(0, T), w3(dw, T, 2, P), dw(512, T)
        hsig, hneg, hlf, hk, hb = (dw(768 + n * T, T) for n in range(5))
        hE, hX = w3(dw, 2048, 8), w3(dw, 4096, 8)
        hatt = w3(dw, 6144, 3, P)
        zrow, hsq, hon = dw(6528, T), dw(6784, T), dw(7040, T)
        draw, dy, dc = w3(dw, 0, 4, T + 3), w3(dw, 1036, 4), w3(dw, 2060, 4)
        dsq, drt, dqk = w3(dw, 3084, 2), w3(dw, 3596, 2), w3(dw, 4108, 2)
        dz = gact[:, 0, :].rearrange("p (n t) -> p n t", t=T)
        dbv = w3(dw, 5132, 4, P)
        dW, dA, dM = w3(dw, 6028, 6, P), w3(dw, 6796, 6, P), w3(dw, 7564, 6, P)
        dC, dD, dcd = w3(dw, 8332, 4, P), w3(dw, 8844, 8, P), w3(dw, 9868, 4, P)
        du, dr2 = w3(dw, 10380, 4, P), w3(dw, 10892, 2, P)
        don, dosq = w3(dw, 11148, 2), w3(dw, 11660, 2)
        eq_h = dw(0, 1024).rearrange("p (a s t) -> p a s t", a=2, s=2)
        ekey = w3(dw, 1024, 16, P)
        esc = dw(3072, 1024).rearrange("p (a c s n) -> p a c s n", a=2, c=2, s=2)
        esc2 = dw(4096, 512).rearrange("p (c s n) -> p c s n", c=2, s=2)
        ev = dw(4608, 64).rearrange("p (c s k) -> p c s k", c=2, s=2)
        ei = dw(4672, 64).bitcast(U32).rearrange("p (c s k) -> p c s k", c=2, s=2)
        eif = dw(4736, 64).rearrange("p (c s k) -> p c s k", c=2, s=2)
        ecand, ecand2 = w3(dw, 4800, 2), w3(dw, 5312, 2)
        ebv, ebp = w3(dw, 5824, 2, 16), dw(5856, 32).bitcast(U32).rearrange("p (c k) -> p c k", k=16)
        ehl = dw(5888, 64).bitcast(U32).rearrange("p (s c k) -> p s c k", s=2, k=16)
        ehf = dw(5952, 64).rearrange("p (s c k) -> p s c k", s=2, k=16)
        eeq = dw(6016, 1024).rearrange("p (s c k j) -> p s c k j", s=2, c=2, k=16)
        e12 = dw(7040, 512).rearrange("p (s c n) -> p s c n", s=2, n=P)
        ebest, eexp, esum = w3(dw, 7552, 2, P), w3(dw, 7808, 2, P), dw(8064, 32)
        oh = late[:, :].rearrange("p (s q w n) -> p s q w n", s=4, q=4, w=2)
        MIX = HA

        CONV_CHUNKS = 16

        def out_chunk(p, n):
            return CONV_CHUNKS + 4 * p + n

        def rows_of(w):
            return w.rearrange("(k p) n -> p k n", p=P)

        w_ada = rows_of(a["w_ada"][0])
        w_in = rows_of(a["w_in"][0])
        w_pa = rows_of(a["w_proj_a"][0])
        w_pb = rows_of(a["w_proj_b"][0])
        w_out = rows_of(a["w_out"][0])
        w_in2 = rows_of(a["w_in_2"][0])
        w_out2 = rows_of(a["w_out_2"][0])
        w_q = rows_of(a["peer_w_query_2"][0].rearrange("d h k -> d (h k)"))
        p_u = a["peer_u_2"][0].rearrange("(c e p) d -> c p e d", e=4, p=P)
        p_v = a["peer_v_2"][0].rearrange("(c e p) d -> c p e d", e=2, p=P)

        block = ctx.enter_context(nc.Block())

        @block.sync
        def _(sp):
            tiles = Count(tile_done, "sp tiles")
            tiles.n = 12

            def load(slot, pieces, makes, prev, width=512):
                if prev is not None:
                    sp.wait_ge(tile_done, tiles.value(-prev))
                dst = ring[slot][:, 0:KT * width].rearrange("p (k c) -> p k c", c=width)
                at = 0
                for src, off, n in pieces:
                    sp.dma_start(dst[:, :, at:at + n], src[:, :, ds(off, n)]).then_inc(landed[slot], 16)
                    at += n
                tiles.up(makes)

            load(0, [(w_ada, 0, 512)], 1, None)
            load(1, [(w_ada, 512, 512)], 1, None)
            with rounds(sp, 5, (tiles, 2)) as i:
                load(0, [(w_ada, 1024 + i * 1024, 512)], 1, 1)
                load(1, [(w_ada, 1536 + i * 1024, 512)], 1, 1)
            sp.wait_ge(tile_evac, SETUP + ADA)
            sp.dma_start(mod_rows, mod_row.rearrange("o (r c) -> o r c", c=128)).then_inc(mod_moved, 16)

            def load_conv(j, s, half):
                offs = (OFF_U, OFF_C) if s == 0 else (OFF_B, OFF_ZB)
                for m in range(2):
                    sp.dma_start(half_ring[half][:, :, m * 256:(m + 1) * 256],
                                 w_in[:, 8 * half:8 * half + 8, ds(j * 256 + offs[m], 256)]).then_inc(landed[half], 16)

            sp.wait_ge(tile_done, tiles.value(-1))
            for half in range(2):
                load_conv(0, 0, half)
            for half in range(2):
                sp.wait_ge(wc_split, 2 * half + 2)
                load_conv(0, 1, half)
            with rounds(sp, 7) as j:
                for s in range(2):
                    for half in range(2):
                        sp.wait_ge(wc_split, 8 * j + (4 * s + 2 * half + 6))
                        load_conv(j + 1, s, half)
            tiles.n += 64

            def head_chunks(h, prev):
                load(0, [(w_in, h * 128, 128), (w_in, OFF_K + h * 128, 128),
                         (w_in, OFF_V + h * 256, 256)], 4, prev)
                if prev is None:
                    sp.wait_ge(wc_used, 64)
                    sp.dma_start(vbias, a["b_in"][0][OFF_V:OFF_V + VW].rearrange("(o n) -> o n", o=1)).then_inc(vbias_in, 16)
                load(1, [(w_in, OFF_O + h * 256, 256), (w_in, OFF_Z + h * 256, 256)], 4, None if prev is None else 4)

            sp.wait_ge(wc_split, 64)
            head_chunks(0, None)
            with rounds(sp, 7, (tiles, 8)) as h:
                head_chunks(h + 1, 4)
            with rounds(sp, 8, (tiles, 8)) as j:
                load(0, [(w_in, OFF_GA + j * 256, 256), (w_pa, j * 256, 256)], 4, 4)
                load(1, [(w_in, OFF_GB + j * 256, 256), (w_pb, j * 256, 256)], 4, 4)

            def load_projection(p, w, prev):
                sp.wait_ge(tile_done, tiles.value(-prev))
                for n in range(4):
                    for half in range(2):
                        if n:
                            sp.wait_ge(wc_split, 4 * out_chunk(p, n - 1) + 2 * half + 2)
                        sp.dma_start(half_ring[half], w[:, 8 * half:8 * half + 8, n * 512:(n + 1) * 512]).then_inc(out_landed[half], 16)
                sp.wait_ge(wc_split, 4 * out_chunk(p, 4))
                sp.wait_ge(wc_used, 4 * out_chunk(p, 4))
                tiles.n += 16

            load_projection(0, w_out, 4)
            with rounds(sp, 4, (tiles, 8)) as i:
                for s in range(2):
                    load(s, [(w_in2, i * 256 + (off + s * 128), 128) for off in (0, OFF2_F, OFF2_I, OFF2_G)], 4, 4)

            def delta_chunks(g, prev):
                load(0, [(w_in2, OFF2_BQ + g * 128, 128), (w_in2, OFF2_BK + g * 128, 128),
                         (w_in2, OFF2_BV + g * 256, 128)], 3, prev, 384)
                load(1, [(w_in2, OFF2_BV + g * 256 + 128, 128),
                         (w_in2, OFF2_BZ + g * 256, 256)], 3, 3, 384)

            delta_chunks(0, 4)
            with rounds(sp, GROUPS - 1, (tiles, 6)) as g:
                delta_chunks(g + 1, 3)

            load_projection(1, w_out2, 3)

            load(0, [(w_q, 0, 256)], 2, 4, 256)
            sp.wait_ge(normed, 4)
            sp.dma_start(keys_rows, a["peer_sub_keys_2"][0].rearrange("s h n k -> n (s h) k")).then_inc(keys_in, 16)
            tiles.n += 4
            load(1, [(w_q, 256, 256)], 2, 6, 256)
            with rounds(sp, 3, (tiles, 4)) as i:
                load(0, [(w_q, (i + 1) * 512, 256)], 2, 2, 256)
                load(1, [(w_q, (i + 1) * 512 + 256, 256)], 2, 2, 256)
            sp.dma_start(xkeep, XT).then_inc(kept, 16)

            def load_u(i, q):
                sp.dma_start(u_ring[q % 2], p_u[ds(i, 1), :, :, q * 512:(q + 1) * 512].rearrange("o p e d -> p (o e) d")).then_inc(landed[q % 2], 16)

            sp.wait_ge(tile_done, tiles.value())
            load_u(0, 0)
            load_u(0, 1)
            for q in range(2, 4):
                sp.wait_ge(turn_done, 4 * (q - 1))
                load_u(0, q)
            with rounds(sp, U_CHUNKS - 1) as i:
                for q in range(4):
                    sp.wait_ge(turn_done, 16 * i + (4 * (q + 3)))
                    load_u(i + 1, q)

            def load_v(c, s):
                sp.dma_start(peer_ring[s], p_v[ds(c, 1)].rearrange("o p e d -> p (o e) d")).then_inc(v_landed[s], 16)

            sp.wait_ge(turn_done, 16 * U_CHUNKS)
            load_v(0, 0)
            sp.wait_ge(u_used, 16 * U_CHUNKS)
            load_v(1, 1)
            with rounds(sp, 31) as i:
                for s in range(2):
                    sp.wait_ge(lo_ready, 4 * i + (2 * s + 2))
                    load_v(2 * i + (s + 2), s)
            sp.wait_ge(lo_ready, N_KEYS)
            sp.wait_ge(kept, 16)
            sp.dma_start(XT, xkeep).then_inc(x_back, 16)
            for c in range(TT):
                sp.wait_ge(tile_evac, FINAL_TILES + 4 * (c + 1))
                sp.dma_start(out[0][c * P:(c + 1) * P, :], xout[:, c, :]).then_inc(out_done, 16)
            sp.wait_ge(out_done, 16 * TT)

        @block.tensor
        def _(pe):
            tiles = Count(tile_done, "pe tiles")
            land = [Count(landed[0], "pe slot 0"), Count(landed[1], "pe slot 1")]

            def free_bank(lag=4):
                if isinstance(tiles.lead, int) and tiles.n < lag:
                    return
                pe.wait_ge(tile_evac, tiles.value(1 - lag))

            def arrive(slot, pieces):
                pe.wait_ge(landed[slot], land[slot].up(16 * pieces))

            def chunk(slot, width=512):
                return ring[slot][:, 0:KT * width].rearrange("p (k c) -> p k c", c=width)

            def feature_tile(bank, w, c0, moving, lag=4):
                free_bank(lag)
                for k in range(KT):
                    mm = nc.tensor.matmul(banks[bank][:, 0:T], w[:, k, c0:c0 + P], moving[:, k, :],
                                          start=(k == 0), stop=(k == KT - 1))
                mm.then_inc(tile_done, 1)
                tiles.up()

            def turn(bank, at, src):
                return nc.tensor.transpose(banks[bank][0:src.shape[1], at:at + src.shape[0]], src,
                                           ident[0:src.shape[0], 0:src.shape[0]])

            def mean_square(n):
                for k in range(KT):
                    if k % 4 == 0:
                        pe.wait_ge(squares, 4 * (n - 1) + k // 4 + 1)
                    mm = nc.tensor.matmul(square_bank(n), ones[:, :], HB2[:, k, :],
                                          start=(k == 0), stop=(k == KT - 1))
                mm.then_inc(ss_ready, 1)

            pe.wait_ge(consts, 1)
            pe.wait_ge(x_in, 16)
            for m in range(8):
                free_bank()
                for q in range(4):
                    k, c = 2 * m + q // 2, q % 2
                    mm = turn(m % 4, q * P, xrow[:, c, k * P:(k + 1) * P])
                mm.then_inc(tile_done, 1)
                tiles.up()
            pe.wait_ge(params_in, 16 * N_PARAMS)
            for m, rows in enumerate(PACK_ROWS):
                free_bank()
                turn(m, 0, pack[0:rows, m, :]).then_inc(tile_done, 1)
                tiles.up()

            pe.wait_ge(c_ready, 1)
            with rounds(pe, 6, (tiles, 2), (land[0], 16), (land[1], 16)) as i:
                for s in range(2):
                    arrive(s, 1)
                    w = chunk(s)
                    free_bank(2)
                    for k in range(ADA_DVE, KT):
                        nc.tensor.matmul(banks[s][0:1, :], cact[:, k:k + 1], w[:, k, :],
                                         start=(k == ADA_DVE), stop=False)
                    pe.wait_ge(ada_part, 2 * i + (s + 1))
                    nc.tensor.matmul(banks[s][0:1, :], ones[:, 0:1], ada_acc[s],
                                     start=False, stop=True).then_inc(tile_done, 1)
                    tiles.up()
            mean_square(1)
            pe.wait_ge(mod_moved, 16)
            nc.tensor.transpose(banks[4][:, 0:48], mod_rows, ident[0:48, 0:48]).then_inc(mod_turned, 1)

            pe.wait_ge(shifted, 1)
            for g in range(2):
                for k in range(KT):
                    mm = nc.tensor.matmul(banks[4 + g][0:8, 0:T], wg[:, k, 8 * g:8 * g + 8], hT[:, k, :],
                                          start=(k == 0), stop=(k == KT - 1))
                mm.then_inc(gates_mm, 1)
            pe.wait_ge(tile_evac, tiles.value())
            for slot in range(2):
                land[slot].up(16 * 2 * 16)

            def turn_rows(n, s):
                pe.wait_ge(conv_rows, n + 1)
                for m in range(4):
                    for c in range(TT):
                        mm = turn(2 * s + m // 2, (m % 2) * T + c * P, gact[:, c, m * P:(m + 1) * P])
                    tiles.up()
                    if m % 2 == 1:
                        mm.then_inc(tile_done, 2)

            def conv(j, first=False):
                for s in range(2):
                    n = 2 * j + s
                    if not first:
                        pe.wait_ge(tile_evac, tiles.value())
                    for q in range(4):
                        if first and s == 0:
                            pe.wait_ge(hc_split, q + 1)
                        pe.wait_ge(wc_split, 4 * n + (q + 1))
                        for k in range(4 * q, 4 * q + 4):
                            for c in range(TT):
                                for h, w in ((hc_hi, wc_hi), (hc_hi, wc_lo), (hc_lo, wc_hi)):
                                    mm = nc.tensor.matmul(banks[2 * s + c][:, :], h[:, k, c * P:(c + 1) * P],
                                                          w[:, 4 * (q % 2) + k % 4, :],
                                                          start=(k == 0 and h is hc_hi and w is wc_hi),
                                                          stop=(k == KT - 1 and h is hc_lo))
                        mm.then_inc(wc_used, 1)
                        if q == 1 and not (first and s == 0):
                            turn_rows(n - 1, 1 - s)

            conv(0, True)
            with rounds(pe, 7, (tiles, 8)) as j:
                conv(j + 1)
            turn_rows(15, 1)

            pe.wait_ge(gates_rows, 1)
            for c in range(TT):
                mm = turn(6, c * 8, g8[:, 5, c * P:(c + 1) * P])
            mm.then_inc(gates_tp, 1)
            pe.wait_ge(vbias_in, 16)
            pe.wait_ge(gates_done, 1)
            with rounds(pe, 8, (tiles, 8), (land[0], 48), (land[1], 32)) as h:
                arrive(0, 3)
                w = chunk(0)
                for m in range(2):
                    feature_tile(m, w, m * P, hT)
                for c in range(TT):
                    free_bank()
                    for k in range(KT):
                        nc.tensor.matmul(banks[2 + c][:, 0:T], hT[:, k, c * P:(c + 1) * P],
                                         w[:, k, 256:512], start=(k == 0), stop=False)
                    mm = nc.tensor.matmul(banks[2 + c][:, 0:T], ones[0:1, :], vbias[:, ds(h * 256, 256)],
                                          start=False, stop=True)
                    mm.then_inc(tile_done, 1)
                    tiles.up()
                pe.wait_ge(tile_evac, tiles.value(-2))
                pe.wait_ge(mlstm_done, 1 + h)
                nc.tensor.matmul(banks[4][:, 0:T], mqk[:, 1, 0:P], mqk[:, 0, :], start=True, stop=True)
                nc.tensor.matmul(banks[4][:, T:T + P], mqk[:, 1, P:T], mqk[:, 0, P:T], start=True, stop=True)
                for n in range(2):
                    mm = nc.tensor.matmul(banks[6 + n][:, 0:T], ones[0:8, :], spread[:, n, ds(h, 1), :].rearrange("p o t -> p (o t)"),
                                          start=True, stop=True)
                mm.then_inc(scores_ready, 1)
                arrive(1, 2)
                for m in range(2):
                    feature_tile(m, chunk(1), m * P, hT)
                pe.wait_ge(att_ready, h + 1)
                pe.wait_ge(tile_evac, tiles.value(-2))
                for n in range(2):
                    o = banks[5][:, n * T:(n + 1) * T]
                    nc.tensor.matmul(o, mv[:, 0, n * P:(n + 1) * P], mS[:, 0:T], start=True, stop=False)
                    nc.tensor.matmul(o[:, P:T], mv[:, 1, n * P:(n + 1) * P], mS[:, T:T + P],
                                     start=False, stop=True)
                nc.tensor.matmul(banks[6][:, 0:T], ones[:, :], mS[:, 0:T], start=True, stop=False)
                nc.tensor.matmul(banks[6][:, P:T], ones[:, :], mS[:, T:T + P],
                                 start=False, stop=True).then_inc(num_ready, 1)
                for m in range(2, 4):
                    feature_tile(m, chunk(1), m * P, hT)
                pe.wait_ge(hsq_ready, h + 1)
                for n in range(2):
                    mm = nc.tensor.matmul(banks[7][:, 0:T], ones[:, :], msq[:, n, :],
                                          start=(n == 0), stop=(n == 1))
                mm.then_inc(hss_ready, 1)

            pe.wait_ge(mlstm_done, 1 + 8)
            pe.wait_ge(conv_done, 1 + 8)
            with rounds(pe, 8, (tiles, 8), (land[0], 32), (land[1], 32)) as j:
                for s, branch in enumerate((HA, HB)):
                    arrive(s, 2)
                    for m in range(4):
                        feature_tile(m, chunk(s), m * P, hT if m < 2 else branch)

            def out_projection(p):
                for n in range(4):
                    pe.wait_ge(tile_evac, tiles.value())
                    chunk_n = out_chunk(p, n)
                    for q in range(4):
                        if n == 0:
                            pe.wait_ge(hc_split, 4 * (p + 1) + q + 1)
                        pe.wait_ge(wc_split, 4 * chunk_n + q + 1)
                        for k in range(4 * q, 4 * q + 4):
                            for c in range(TT):
                                for h, w in ((ho_hi, wc_hi), (ho_hi, wc_lo), (ho_lo, wc_hi)):
                                    mm = nc.tensor.matmul(banks[2 * (n % 2) + c][:, :], h[:, k, c * P:(c + 1) * P],
                                                          w[:, 4 * (q % 2) + k % 4, :],
                                                          start=(k == 0 and h is ho_hi and w is wc_hi),
                                                          stop=(k == KT - 1 and h is ho_lo))
                        mm.then_inc(wc_used, 1)
                        if q == 1 and n:
                            turn_rows(chunk_n - 1, 1 - n % 2)
                turn_rows(out_chunk(p, 3), 1)

            pe.wait_ge(merge_done, 1 + 8)
            out_projection(0)
            mean_square(2)
            mean_square(3)

            pe.wait_ge(normed, 3)
            with rounds(pe, 4, (tiles, 8), (land[0], 64), (land[1], 64)) as i:
                for s in range(2):
                    head = 2 * i + s
                    arrive(s, 4)
                    w = chunk(s)
                    feature_tile(0, w, 0, hT)
                    feature_tile(1, w, P, hT)
                    free_bank()
                    for c in range(TT):
                        for k in range(KT):
                            mm = nc.tensor.matmul(banks[2][:, c * P:(c + 1) * P], hT[:, k, c * P:(c + 1) * P],
                                                  w[:, k, T:T + P], start=(k == 0), stop=(k == KT - 1))
                    mm.then_inc(tile_done, 1)
                    tiles.up()
                    feature_tile(3, w, 3 * P, hT)
                    pe.wait_ge(x_levels, head + 1)
                    for l in range(9):
                        b = banks[4 + l % 4]
                        if l >= 4:
                            pe.wait_ge(gram_taken, head * 9 + l - 3)
                        if l == 0:
                            mm = nc.tensor.matmul(b[:, 0:P], hX[:, 7, 0:P], hX[:, 7, P:T], start=True, stop=True)
                        else:
                            x, y = (hX[:, l - 1, :], hX[:, l - 1, :]) if l < 8 else (hk, hq)
                            for c in range(TT):
                                mm = nc.tensor.matmul(b[:, c * P:(c + 1) * P], x[:, c * P:(c + 1) * P],
                                                      y[:, c * P:(c + 1) * P], start=True, stop=True)
                        mm.then_inc(gram_done, 1)
                    pe.wait_ge(gram_taken, head * 9 + 9)
                    pe.wait_ge(tile_evac, tiles.value(-1))
                    nc.tensor.matmul(banks[5][:, 0:T], hv[:, 0, :], hatt[:, 0:2, :].rearrange("p a t -> p (a t)"), start=True, stop=False)
                    nc.tensor.matmul(banks[5][:, P:T], hv[:, 1, :], hatt[:, 2, :],
                                     start=False, stop=True).then_inc(o_ready, 1)
                    pe.wait_ge(osq_ready, head + 1)
                    nc.tensor.matmul(banks[6][:, 0:T], ones[:, :], hsq, start=True, stop=True).then_inc(oss_ready, 1)

            pe.wait_ge(hgrn_done, 1 + 8)
            for g in range(2):
                for k in range(KT):
                    mm = nc.tensor.matmul(banks[4 + g][0:8, 0:T], wg2[:, k, 8 * g:8 * g + 8], hT[:, k, :],
                                          start=(k == 0), stop=(k == KT - 1))
                mm.then_inc(gates_mm, 1)

            def delta_tiles(x0, n):
                for x in range(x0, x0 + n):
                    m, k = divmod(x, KT)
                    if x % 48 == 0:
                        arrive(m // 3, 3 if m == 0 else 2)
                    if k == 0:
                        free_bank((4, 4, 2, 2, 6, 6)[m])
                    w = chunk(m // 3, 384)
                    c0 = m % 3 * P
                    mm = nc.tensor.matmul(banks[(0, 1, 0, 1, 2, 3)[m]][:, 0:T], w[:, k, c0:c0 + P], hT[:, k, :],
                                          start=(k == 0), stop=(k == KT - 1))
                    if k == KT - 1:
                        mm.then_inc(tile_done, 1)
                        tiles.up()

            delta_tiles(0, 96)
            pe.wait_ge(gates_rows, 2)
            for r, row in enumerate((4, 0)):
                for c in range(TT):
                    mm = turn(6, (r * TT + c) * 8, g8[:, row, c * P:(c + 1) * P])
            mm.then_inc(gates_tp, 1)
            pe.wait_ge(gates_done, 2)

            def delta(g, last=False):
                def meanwhile(x0, n):
                    if not last:
                        delta_tiles(x0, n)

                pe.wait_ge(qk_sq, g + 1)
                pe.wait_ge(orms_ready, 8 + g)
                for n in range(2):
                    mm = nc.tensor.matmul(banks[4][:, n * T:(n + 1) * T], ones[:, :], dsq[:, n, :], start=True, stop=True)
                mm.then_inc(qk_ss, 1)
                for n in range(2):
                    for c in range(TT):
                        mm = turn(5, (n * TT + c) * P, dc[:, 2 + n, c * P:(c + 1) * P])
                mm.then_inc(v_turned, 1)
                meanwhile(0, 20)
                pe.wait_ge(qk_unit, g + 1)
                for n in range(2):
                    b, y = banks[6 + n], dqk[:, 1 - n, :]
                    nc.tensor.matmul(b[:, 0:T], dqk[:, 1, 0:P], y, start=True, stop=True)
                    nc.tensor.matmul(b[:, T:T + P], dqk[:, 1, P:T], y[:, P:T], start=True, stop=True)
                pe.wait_ge(bv_ready, g + 1)
                for n in range(2):
                    for r in range(2):
                        mm = nc.tensor.matmul(banks[4 + n][:, r * T:(r + 1) * T], ones[0:8, :],
                                              spread[:, r, ds(2 * g + n, 1), :].rearrange("p o t -> p (o t)"), start=True, stop=True)
                mm.then_inc(bc_ready, 1)
                meanwhile(20, 18)
                pe.wait_ge(lv_mask, g * 7 + 1)
                for q in range(4):
                    mm = turn(5, q * P, dC[:, q, :])
                mm.then_inc(lv_dd, 1)
                meanwhile(38, 5)
                for l in range(1, 7):
                    pe.wait_ge(lv_mask, g * 7 + (l + 1))
                    for q in range(4):
                        mm = nc.tensor.matmul(banks[4][:, q * P:(q + 1) * P], dC[:, q, :], dD[:, q, :], start=True, stop=True)
                    mm.then_inc(lv_cd, 1)
                    meanwhile(36 + 7 * l, 2)
                    pe.wait_ge(lv_cd_copied, g * 6 + l)
                    if l < 6:
                        for q in range(4):
                            nc.tensor.matmul(banks[5][:, q * P:(q + 1) * P], dD[:, 4 + q, :], dcd[:, q, :], start=True, stop=True)
                    for q in range(4):
                        mm = nc.tensor.matmul(banks[6][:, q * P:(q + 1) * P], dcd[:, q, :], dD[:, 4 + q, :], start=True, stop=True)
                    mm.then_inc(lv_dd, 1)
                    meanwhile(38 + 7 * l, 5)
                pe.wait_ge(lv_new, g + 1)
                for n in range(2):
                    mm = nc.tensor.matmul(banks[4][:, n * P:(n + 1) * P], dD[:, 4 + 2 * n, :], dbv[:, 2 * n, :], start=True, stop=True)
                mm.then_inc(u1_mm, 1)
                meanwhile(85, 3)
                pe.wait_ge(u1_copied, g + 1)
                for n in range(2):
                    mm = nc.tensor.matmul(banks[5][:, n * P:(n + 1) * P], dM[:, 3 * n + 1, :], du[:, 2 * n, :], start=True, stop=True)
                mm.then_inc(r2_mm, 1)
                meanwhile(88, 2)
                pe.wait_ge(r2_ready, g + 1)
                for n in range(2):
                    mm = nc.tensor.matmul(banks[6][:, n * P:(n + 1) * P], dD[:, 5 + 2 * n, :], dr2[:, n, :], start=True, stop=True)
                mm.then_inc(u2_mm, 1)
                meanwhile(90, 2)
                pe.wait_ge(u2_copied, g + 1)
                for n in range(2):
                    o = banks[7][:, n * T:(n + 1) * T]
                    nc.tensor.matmul(o, du[:, 2 * n, :], dA[:, 3 * n:3 * n + 2, :].rearrange("p a t -> p (a t)"), start=True, stop=False)
                    mm = nc.tensor.matmul(o[:, P:T], du[:, 2 * n + 1, :], dA[:, 3 * n + 2, :], start=False, stop=True)
                mm.then_inc(o_ready, 1)
                meanwhile(92, 4)
                pe.wait_ge(osq_ready, 8 + g + 1)
                for n in range(2):
                    mm = nc.tensor.matmul(banks[4][:, n * T:(n + 1) * T], ones[:, :], dosq[:, n, :], start=True, stop=True)
                mm.then_inc(oss_ready, 1)

            with rounds(pe, GROUPS - 1, (tiles, 6), (land[0], 48), (land[1], 32)) as g:
                delta(g)
            delta(GROUPS - 1, last=True)

            pe.wait_ge(delta_done, 1 + GROUPS)
            pe.wait_ge(tile_evac, tiles.value())
            out_projection(1)
            mean_square(4)

            pe.wait_ge(keys_in, 16)
            for m in range(4):
                free_bank()
                for q in range(4):
                    mm = turn(m, q * P, keys_rows[:, 4 * m + q, :])
                mm.then_inc(tile_done, 1)
                tiles.up()
            pe.wait_ge(normed, 4)
            with rounds(pe, 4, (tiles, 4), (land[0], 16), (land[1], 16)) as i:
                for s in range(2):
                    arrive(s, 1)
                    for m in range(2):
                        feature_tile(2 * s + m, chunk(s, 256), m * P, hT)
                    pe.wait_ge(tile_evac, tiles.value())
                    pe.wait_ge(keyscore_copied, 1 + 2 * i + s)
                    for c in range(TT):
                        for half in range(2):
                            mm = nc.tensor.matmul(banks[4 + s][:, (2 * c + half) * P:(2 * c + half + 1) * P],
                                                  eq_h[:, s, half, c * P:(c + 1) * P],
                                                  ekey[:, ds(2 * i + (s + 8 * half), 1), :].rearrange("p o n -> p (o n)"),
                                                  start=True, stop=True)
                    mm.then_inc(keyscore, 1)

            pe.wait_ge(slots_ready, 1)
            for c in range(TT):
                free_bank()
                for r, src in enumerate((e12[:, 0, c, :], e12[:, 1, c, :], eexp[:, c, :])):
                    mm = turn(c, r * P, src)
                mm.then_inc(tile_done, 1)
                tiles.up()

            def gate_products(i, first):
                for s in range(4):
                    n = 4 * i + s
                    pe.wait_ge(gated_act, n + 1)
                    pe.wait_ge(gated_pool, n + 1)
                    if not first:
                        pe.wait_ge(gmat_out, n - 3)
                    for q in range(4):
                        mm = nc.tensor.matmul(banks[4 + s][:, q * P:(q + 1) * P], oh[:, s, q, 1, :], oh[:, s, q, 0, :],
                                              start=True, stop=True)
                    mm.then_inc(gmat, 1)

            gate_products(0, True)
            with rounds(pe, T // 16 - 1) as i:
                gate_products(i + 1, False)
            pe.wait_ge(gmat_out, T // 4)

            def turn_u(j, k, first=False):
                if k % 4 == 0:
                    arrive(k // 4 % 2, 1)
                if not first:
                    pe.wait_ge(u_split, j - 3)
                for e in range(4):
                    mm = turn(k % 4, e * P, u_ring[k // 4 % 2][:, e, (k % 4) * P:(k % 4 + 1) * P])
                mm.then_inc(turn_done, 1)

            def turn_activated(b):
                for e in range(4):
                    for c in range(TT):
                        mm = turn(b + e // 2, (e % 2) * T + c * P, gact[:, c, e * P:(e + 1) * P])
                mm.then_inc(act_turned, 1)

            def hidden(n, b, first=False, last=False):
                for k in range(KT):
                    j = 16 * n + k
                    if not (last and k + 3 >= KT):
                        turn_u(j + 3, (k + 3) % KT, first and k == 0)
                    if first and k % 4 == 0:
                        pe.wait_ge(h_split, k // 4 + 1)
                    if not first and k == 0:
                        pe.wait_ge(wmul, 1 + 2 * n - 2)
                    pe.wait_ge(u_split, j + 1)
                    for c in range(TT):
                        for h, u in ((h_hi, u_hi), (h_hi, u_lo), (h_lo, u_hi)):
                            mm = nc.tensor.matmul(banks[b + c][:, :], h[:, k, c * P:(c + 1) * P], u[:, k % 4, :],
                                                  start=(k == 0 and h is h_hi and u is u_hi),
                                                  stop=(k == KT - 1 and h is h_lo))
                    mm.then_inc(u_used, 1)
                    if not first and k == 7:
                        pe.wait_ge(gelu_done, 2 * n)
                        turn_activated(10 - b)

            for k in range(3):
                turn_u(k, k, True)
            hidden(0, 4, first=True)
            with rounds(pe, U_CHUNKS // 2 - 1, (land[0], 64), (land[1], 64)) as i:
                hidden(2 * i + 1, 6)
                hidden(2 * i + 2, 4)
            hidden(U_CHUNKS - 1, 6, last=True)
            pe.wait_ge(gelu_done, 2 * U_CHUNKS)
            turn_activated(6)

            def outputs(i, first):
                for u in range(4):
                    pe.wait_ge(lo_ready, 4 * i + (u + 1))
                    for c in range(TT):
                        for w, v, opens in ((w_hi, v_hi, first and u == 0), (w_hi, v_lo, False), (w_lo, v_hi, False)):
                            for b in range(4):
                                mm = nc.tensor.matmul(banks[4 * c + b][:, :], w[:, u % 2, c * P:(c + 1) * P],
                                                      v[:, u % 2, b * 512:(b + 1) * 512],
                                                      start=opens, stop=False, skip_group_check=True)
                    mm.then_inc(y_done, 1)

            outputs(0, True)
            with rounds(pe, N_KEYS // 4 - 1) as i:
                outputs(i + 1, False)
            pe.wait_ge(y_rows_act, 4)
            pe.wait_ge(y_rows_dve, 4)
            for m in range(8):
                for q in range(4):
                    mm = turn(m, q * P, xrow[:, q % 2, (2 * m + q // 2) * P:(2 * m + q // 2 + 1) * P])
                mm.then_inc(y_turned, 1)

            mean_square(5)
            pe.wait_ge(normed, 5)
            for n in range(8):
                free_bank()
                for q in range(4):
                    mm = turn(n % 4, q * P, hT[:, 4 * (n % 4) + q, (n // 4) * P:(n // 4 + 1) * P])
                mm.then_inc(tile_done, 1)
                tiles.up()

        @block.scalar
        def _(act):
            tiles = Count(tile_evac, "act tiles")
            steps = Count(act_step, "act steps")

            def evac(dst, src, func=ACT.Copy, bias=None, scale=None):
                act.wait_ge(tile_done, tiles.up())
                kw = {}
                if bias is not None:
                    kw["bias"] = bias
                if scale is not None:
                    kw["scale"] = scale
                nc.scalar.activation(dst, src, func, **kw).then_inc(tile_evac, 1)

            def link(ins):
                ins.then_inc(act_step, 1)
                act.wait_ge(act_step, steps.up())

            def square(q):
                part = slice(4 * q, 4 * q + 4)
                nc.scalar.activation(HB2[:, part, :], XT[:, part, :], ACT.Square).then_inc(squares, 1)

            def root(n):
                act.wait_ge(ss_ready, n)
                nc.scalar.activation(rms_t[:, 0, :], square_bank(n), ACT.Sqrt, bias=eps_col[:, :],
                                     scale=1.0 / D).then_inc(rms_ready, 1)

            def pcol(at, n=1):
                return par[:, ds(at, n)]

            def rows128(src, dst):
                act.dma_start(dst, src).then_inc(params_in, 16)

            def r(ap):
                return ap.rearrange("(r c) -> r c", c=128)

            act.dma_start(xrow[:, :, :], a["x"][0].rearrange("(c p) d -> p c d", p=P)).then_inc(x_in, 16)
            b = a["b_in"][0]
            rows128(r(b[0:OFF_I]), pack[0:64, 0, :])
            rows128(r(a["norm1_w"][0]), pack[64:80, 0, :])
            rows128(r(a["headnorm_w"][0]), pack[80:96, 0, :])
            rows128(r(a["normf_w"]), pack[96:112, 0, :])
            rows128(r(a["attn_norm_g_2"][0]), pack[112:128, 0, :])
            rows128(r(b[OFF_U:IN_1]), pack[0:96, 1, :])
            rows128(r(a["ffn_norm_g_2"][0]), pack[96:112, 1, :])
            rows128(r(a["final_norm_g_2"]), pack[112:128, 1, :])
            rows128(a["conv_w"][0].rearrange("j (r c) -> (j r) c", c=128), pack[0:48, 2, :])
            rows128(r(a["b_ada"][0]), pack[48:96, 2, :])
            rows128(r(a["c"][0]), pack[96:112, 2, :])
            rows128(a["hgrn_norm_g_2"], pack[112:113, 2, :])
            rows128(a["gdn_norm_g_2"], pack[113:114, 2, :])
            rows128(a["gdn_conv_w_2"][0].rearrange("j (r c) -> (j r) c", c=128), pack[0:64, 3, :])
            rows128(a["hgrn_lb_logits_2"].rearrange("l h c -> (l h) c"), pack[64:80, 3, :])
            col = lambda v: v.rearrange("(h o) -> h o", o=1)
            with nc.allow_non_contiguous_dma("a few words"):
                rows128(col(b[OFF_I:OFF_I + 8]), gbias[:, 0:1])
                rows128(col(b[OFF_I + 8:OFF_I + 16]), gbias[:, 1:2])
                rows128(col(a["gdn_A_log_2"][0]), gbias[:, 2:3])
                rows128(col(a["gdn_dt_bias_2"][0]), gbias[:, 3:4])
                rows128(w_in[:, :, OFF_I:OFF_I + 16], wg[:, :, :])
                rows128(w_in2[:, :, OFF2_BB:OFF2_BB + 16], wg2[:, :, :])

            act.wait_ge(consts, 1)
            for m in range(8):
                evac(XT[:, 2 * m:2 * m + 2, :], banks[m % 4].rearrange("p (k t) -> p k t", t=T))
            for m, rows in enumerate(PACK_ROWS):
                evac(par[:, 128 * m:128 * m + rows], banks[m][:, 0:rows])
            act.wait_ge(tile_evac, tiles.value())
            nc.scalar.activation(cact[:, :], par[:, PK_C:PK_C + KT], ACT.Silu).then_inc(c_ready, 1)
            link(nc.scalar.activation(lbc[:, 0:2, :], par[:, PK_LB:PK_LB + 16].rearrange("p (l h) -> p l h", l=2), ACT.Exp))
            for q in range(4):
                square(q)
            with rounds(act, 6, (tiles, 2)) as i:
                for s in range(2):
                    evac(mod_row[:, ds(1024 * i + 512 * s, 512)], banks[s][0:1, :])
            root(1)

            act.wait_ge(normed, 1)
            act.wait_ge(mod_ready, 1)
            for k in range(KT):
                ins = nc.scalar.activation(hT[:, k, :], hT[:, k, :], ACT.Identity, bias=mod[:, k:k + 1])
            ins.then_inc(shifted, 1)
            act.wait_ge(shifted, 1)
            for q in range(4):
                nc.scalar.activation(hc_hi[:, 4 * q:4 * q + 4, :], hT[:, 4 * q:4 * q + 4, :], ACT.Copy).then_inc(hc_rounded, 1)

            LANDED = 16 * 6

            def round_weights(n, q, free=True):
                if q % 2 == 0:
                    if isinstance(n, int) and n >= CONV_CHUNKS:
                        act.wait_ge(out_landed[q // 2], 16 * (n - CONV_CHUNKS + 1))
                    else:
                        act.wait_ge(landed[q // 2], 32 * n + (LANDED + 32))
                if free:
                    act.wait_ge(wc_used, 4 * n + (q - 1))
                nc.scalar.activation(wc_hi[:, 4 * (q % 2):4 * (q % 2) + 4, :], half_ring[q // 2][:, 4 * (q % 2):4 * (q % 2) + 4, :],
                                     ACT.Copy).then_inc(wc_rounded, 1)

            def rows_of_tokens(n, s):
                act.wait_ge(wc_used, 4 * n + 4)
                for c in range(TT):
                    ins = nc.scalar.activation(gact[:, c, :], banks[2 * s + c][:, :], ACT.Copy)
                ins.then_inc(conv_rows, 1)

            def conv_tiles(j, s):
                act.wait_ge(*((conv_mixed, 1 + j) if s == 0 else (conv_done, 1 + j)))
                for m in range(4):
                    base = (PK_REST_B, PK_REST_B + 32, PK_REST_B + 16, PK_REST_B + 48)[2 * s + m // 2]
                    evac(cv[:, 4 * s + m, :], banks[2 * s + m // 2][:, (m % 2) * T:(m % 2 + 1) * T],
                         ACT.Identity if (s == 0 or m < 2) else ACT.Silu, bias=pcol(base + m % 2 + 2 * j))

            def conv(j, first=False):
                for s in range(2):
                    n = 2 * j + s
                    start = first and s == 0
                    if not start:
                        round_weights(n, 0)
                        round_weights(n, 1)
                        rows_of_tokens(n - 1, 1 - s)
                    round_weights(n, 2)
                    round_weights(n, 3)
                    if not start:
                        conv_tiles(j - 1 + s, 1 - s)

            def soft(n):
                act.wait_ge(gates_abs, n)
                link(nc.scalar.activation(g8[:, 2, :], g8[:, 2, :], ACT.Exp, scale=-1.0))
                nc.scalar.activation(g8[:, 2, :], g8[:, 2, :], ACT.Ln, bias=1.0).then_inc(gates_log, 1)

            round_weights(0, 0, False)
            round_weights(0, 1, False)
            soft(1)
            conv(0, True)
            with rounds(act, 7, (tiles, 8)) as j:
                conv(j + 1)
            rows_of_tokens(15, 1)
            conv_tiles(7, 1)

            with rounds(act, 8, (tiles, 8)) as h:
                act.wait_ge(mlstm_done, 1 + h)
                evac(mqk[:, 0, :], banks[0][:, 0:T], ACT.Identity, bias=pcol(h + PK_QKVOZ_B))
                evac(mqk[:, 1, :], banks[1][:, 0:T], ACT.Identity, bias=pcol(h + (PK_QKVOZ_B + 8)))
                for c in range(TT):
                    evac(mv[:, c, :], banks[2 + c][:, 0:T])
                act.wait_ge(expo_ready, h + 1)
                nc.scalar.activation(mE, mE, ACT.Exp).then_inc(exp_done, 1)
                nc.scalar.activation(mfloor, banks[7][:, 0:T], ACT.Exp).then_inc(floor_done, 1)
                for m in range(2):
                    evac(mo[:, m, :], banks[m][:, 0:T], ACT.Sigmoid, bias=pcol(2 * h + (PK_QKVOZ_B + 32 + m)))
                act.wait_ge(h_ready, h + 1)
                nc.scalar.activation(msq, mh, ACT.Square).then_inc(hsq_ready, 1)
                for m in range(2):
                    evac(mz[:, m, :], banks[2 + m][:, 0:T], ACT.Silu, bias=pcol(2 * h + (PK_QKVOZ_B + 48 + m)))
                act.wait_ge(hss_ready, h + 1)
                nc.scalar.activation(mden[:, 1, :], banks[7][:, 0:T], ACT.Sqrt, bias=eps_col[:, :],
                                     scale=1.0 / 256).then_inc(hrms_ready, 1)

            with rounds(act, 8, (tiles, 8)) as j:
                act.wait_ge(merge_done, 1 + j)
                for s in range(2):
                    for m in range(2):
                        evac(sg[:, 2 * s + m, :], banks[m][:, 0:T], ACT.Sigmoid,
                             bias=pcol(2 * j + (PK_REST_B + 64 + 16 * s + m)))
                    for m in range(2):
                        evac(yy[:, 2 * s + m, :], banks[2 + m][:, 0:T])

            def residual(p, src, gate):
                for q in range(4):
                    nc.scalar.activation(ho_hi[:, 4 * q:4 * q + 4, :], src[:, 4 * q:4 * q + 4, :], ACT.Copy).then_inc(hc_rounded, 1)

                def update_tiles(n):
                    if n >= 2:
                        act.wait_ge(resid_done, 1 + 4 * p + n - 1)
                    for m in range(4):
                        evac(upd[:, 4 * (n % 2) + m, :], banks[2 * (n % 2) + m // 2][:, (m % 2) * T:(m % 2 + 1) * T],
                             scale=mod[:, 32 + 4 * n + m:33 + 4 * n + m] if gate else None)

                for n in range(4):
                    round_weights(out_chunk(p, n), 0)
                    round_weights(out_chunk(p, n), 1)
                    if n:
                        rows_of_tokens(out_chunk(p, n - 1), 1 - n % 2)
                    round_weights(out_chunk(p, n), 2)
                    round_weights(out_chunk(p, n), 3)
                    if n:
                        update_tiles(n - 1)

                def square_sum(q):
                    act.wait_ge(resid_done, 1 + 4 * p + q + 1)
                    square(q)

                square_sum(0)
                rows_of_tokens(out_chunk(p, 3), 1)
                square_sum(1)
                update_tiles(3)
                square_sum(2)
                square_sum(3)

            act.wait_ge(merge_done, 1 + 8)
            residual(0, MG, True)
            root(2)
            for q in range(4):
                act.wait_ge(*((norm_part, 3 + q + 1) if q < 3 else (normed, 2)))
                square(q)
            root(3)

            with rounds(act, 4, (tiles, 8)) as i:
                for s in range(2):
                    head = 2 * i + s
                    act.wait_ge(hgrn_done, 1 + head)
                    evac(hq, banks[0][:, 0:T])
                    act.wait_ge(tile_done, tiles.value(1))
                    nc.scalar.activation(hneg, banks[1][:, 0:T], ACT.Sigmoid, scale=-1.0).then_inc(decay_in, 1)
                    evac(hsig, banks[1][:, 0:T], ACT.Sigmoid)
                    act.wait_ge(tile_evac, tiles.value())
                    nc.scalar.activation(hlf, hsig, ACT.Ln, bias=lbc[:, 2, ds(head, 1)], scale=lbc[:, 3, ds(head, 1)]).then_inc(decay_in, 1)
                    evac(hv[:, :, :], banks[2][:, 0:T].rearrange("p (c v) -> p c v", v=P))
                    act.wait_ge(decay_exp, head + 1)
                    nc.scalar.activation(hE, hE, ACT.Exp).then_inc(decayed, 1)
                    evac(hz, banks[3][:, 0:T], ACT.Silu)
                    act.wait_ge(o_ready, head + 1)
                    nc.scalar.activation(hsq, banks[5][:, 0:T], ACT.Square).then_inc(osq_ready, 1)
                    act.wait_ge(oss_ready, head + 1)
                    nc.scalar.activation(hon, banks[6][:, 0:T], ACT.Sqrt, bias=eps_col[:, :],
                                         scale=1.0 / P).then_inc(orms_ready, 1)

            act.wait_ge(gates_mm, 4)
            nc.scalar.activation(g8[:, 0, :], banks[4][0:8, 0:T], ACT.Sigmoid).then_inc(decay_in, 1)
            nc.scalar.activation(gbias[:, 4:5], gbias[:, 2:3], ACT.Exp).then_inc(decay_in, 1)
            soft(2)

            def take_qkv(m):
                evac(draw[:, m, 3:T + 3], banks[m % 2][:, 0:T])

            def silus(g):
                act.wait_ge(conv_in, g + 1)
                nc.scalar.activation(dc, dy, ACT.Silu).then_inc(silu_done, 1)
                act.wait_ge(silu_done, g + 1)
                nc.scalar.activation(dsq, dc[:, 0:2, :], ACT.Square).then_inc(qk_sq, 1)

            for m in range(4):
                take_qkv(m)
            silus(0)

            def delta(g, last=False):
                act.wait_ge(qk_ss, g + 1)
                nc.scalar.activation(drt, banks[4].rearrange("p (k t) -> p k t", t=T), ACT.Sqrt,
                                     bias=eps_col[:, :]).then_inc(qk_rms, 1)
                act.wait_ge(v_turned, g + 1)
                for n in range(2):
                    for c in range(TT):
                        ins = nc.scalar.activation(dbv[:, n * TT + c, :], banks[5][:, (n * TT + c) * P:(n * TT + c + 1) * P],
                                                   ACT.Copy, scale=colT[:, 2, c, ds(2 * g + n, 1)])
                ins.then_inc(bv_ready, 1)
                act.wait_ge(delta_done, 1 + g)
                for m in range(2):
                    evac(dz[:, m, :], banks[2 + m][:, 0:T], ACT.Silu)
                if not last:
                    act.wait_ge(conv_in, g + 1)
                    take_qkv(0)
                act.wait_ge(dex_ready, g + 1)
                nc.scalar.activation(dW, dW, ACT.Exp).then_inc(dex_done, 1)
                if not last:
                    take_qkv(1)
                for l in range(1, 7):
                    act.wait_ge(lv_cd, g * 6 + l)
                    nc.scalar.activation(dcd, banks[4].rearrange("p (q t) -> p q t", t=P), ACT.Copy).then_inc(lv_cd_copied, 1)
                    if not last and l in (2, 4):
                        take_qkv(1 + l // 2)
                if not last:
                    silus(g + 1)
                act.wait_ge(u1_mm, g + 1)
                nc.scalar.activation(du[:, 0:4:2, :], banks[4][:, 0:T].rearrange("p (q t) -> p q t", t=P), ACT.Copy).then_inc(u1_copied, 1)
                act.wait_ge(u2_mm, g + 1)
                nc.scalar.activation(du[:, 1:4:2, :], banks[6][:, 0:T].rearrange("p (q t) -> p q t", t=P), ACT.Copy).then_inc(u2_copied, 1)
                act.wait_ge(o_ready, 8 + g + 1)
                nc.scalar.activation(dosq, banks[7].rearrange("p (q t) -> p q t", t=T), ACT.Square).then_inc(osq_ready, 1)
                act.wait_ge(oss_ready, 8 + g + 1)
                nc.scalar.activation(don, banks[4].rearrange("p (q t) -> p q t", t=T), ACT.Sqrt, bias=eps_col[:, :],
                                     scale=1.0 / P).then_inc(orms_ready, 1)

            with rounds(act, GROUPS - 1, (tiles, 6)) as g:
                delta(g)
            delta(GROUPS - 1, last=True)

            act.wait_ge(delta_done, 1 + GROUPS)
            residual(1, MIX, False)
            root(4)

            act.wait_ge(normed, 4)
            for m in range(4):
                evac(ekey[:, 4 * m:4 * m + 4, :], banks[m].rearrange("p (q n) -> p q n", n=P))
            with rounds(act, 4, (tiles, 4)) as i:
                for s in range(2):
                    for m in range(2):
                        evac(eq_h[:, s, m, :], banks[2 * s + m][:, 0:T])
                    act.wait_ge(keyscore, 2 * i + s + 1)
                    act.wait_ge(picked, 1 + 2 * i)
                    nc.scalar.activation(esc[:, s, :, :, :], banks[4 + s].rearrange("p (c a n) -> p c a n", c=2, a=2),
                                         ACT.Copy).then_inc(keyscore_copied, 1)
            act.wait_ge(best_in, 1)
            nc.scalar.activation(eexp, ebest, ACT.Exp).then_inc(best_exp, 1)
            for c in range(TT):
                evac(slt[:, :, c * P:(c + 1) * P], banks[c][:, 0:3 * P].rearrange("p (r t) -> p r t", t=P))

            act.wait_ge(kept, 16)

            def scale_keys(n, s):
                act.wait_ge(onehot, n + 1)
                for q in range(2):
                    hot = oh[:, s, q, 0, :]
                    ins = nc.scalar.activation(hot, hot, ACT.Copy, scale=slt[:, 2, ds(4 * n + q, 1)])
                ins.then_inc(gated_act, 1)

            def take_weights(n, s):
                act.wait_ge(gmat, n + 1)
                nc.scalar.activation(G[:, :, ds(4 * n, 4)], banks[4 + s].rearrange("p (q e) -> p e q", e=P),
                                     ACT.Copy).then_inc(gmat_out, 1)

            scale_keys(0, 0)
            scale_keys(1, 1)
            with rounds(act, T // 16 - 1) as i:
                for s in range(4):
                    scale_keys(4 * i + (s + 2), (s + 2) % 4)
                    take_weights(4 * i + s, s)
            for s in range(4):
                n = T // 4 - 4 + s
                if s < 2:
                    scale_keys(n + 2, s + 2)
                take_weights(n, s)

            act.wait_ge(onehot, T // 4)
            act.wait_ge(gmat, T // 4)
            for q in range(4):
                nc.scalar.activation(h_hi[:, 4 * q:4 * q + 4, :], hT[:, 4 * q:4 * q + 4, :], ACT.Copy).then_inc(h_rounded, 1)

            def gelu(n, b, c):
                if c == 0:
                    act.wait_ge(u_used, 16 * n + 16)
                nc.scalar.activation(gact[:, c, :], banks[b + c][:, :], ACT.Gelu).then_inc(gelu_done, 1)

            def round_u(n, b, first=False):
                for k in range(KT):
                    j = 16 * n + k
                    act.wait_ge(turn_done, j + 1)
                    if not (first and k < 4):
                        act.wait_ge(u_used, j - 3)
                    nc.scalar.activation(u_hi[:, k % 4, :], banks[k % 4][:, :], ACT.Copy).then_inc(u_rounded, 1)
                    if not first and k in (3, 4):
                        gelu(n - 1, b, k - 3)

            round_u(0, 6, True)
            round_u(1, 4)
            with rounds(act, U_CHUNKS // 2 - 1) as i:
                act.wait_ge(act_turned, 2 * i + 1)
                round_u(2 * i + 2, 6)
                act.wait_ge(act_turned, 2 * i + 2)
                round_u(2 * i + 3, 4)
            act.wait_ge(act_turned, U_CHUNKS - 1)
            gelu(U_CHUNKS - 1, 6, 0)
            gelu(U_CHUNKS - 1, 6, 1)

            act.wait_ge(act_turned, U_CHUNKS)
            act.wait_ge(wmul, 1 + 2 * U_CHUNKS)

            def round_halves(i, first):
                for u in range(4):
                    if u % 2 == 0:
                        act.wait_ge(v_landed[u // 2], 16 * i + 16)
                    if not (first and u < 2):
                        act.wait_ge(y_done, 4 * i + (u - 1))
                    nc.scalar.activation(v_hi[:, u % 2, :], peer_ring[u // 2][:, u % 2, :], ACT.Copy)
                    nc.scalar.activation(w_hi[:, u % 2, :], G[:, ds(4 * i + u, 1), :].rearrange("p o t -> p (o t)"),
                                         ACT.Copy).then_inc(hi_ready, 1)

            round_halves(0, True)
            with rounds(act, N_KEYS // 4 - 1) as i:
                round_halves(i + 1, False)
            act.wait_ge(y_done, N_KEYS)
            act.wait_ge(lo_ready, N_KEYS)
            for b in range(4):
                nc.scalar.activation(xrow[:, 0, b * 512:(b + 1) * 512], banks[b][:, :], ACT.Copy).then_inc(y_rows_act, 1)

            for q in range(4):
                act.wait_ge(y_added, q + 1)
                square(q)
            root(5)
            act.wait_ge(normed, 5)
            for n in range(8):
                evac(xout[:, n // 4, (n % 4) * 512:(n % 4 + 1) * 512], banks[n % 4][:, :])

        @block.vector
        def _(dve):
            v = nc.vector
            steps = Count(dve_step, "dve steps")
            tiles = Count(tile_evac, "dve tiles")

            def link(ins):
                ins.then_inc(dve_step, 1)
                dve.wait_ge(dve_step, steps.up())

            carried = [0]

            def carry():
                carried[0] += 1
                v.memset(carrier[:, carried[0] % 64:carried[0] % 64 + 1], 0.0)

            def pcol(at, n=1):
                return par[:, ds(at, n)]

            def norm(n, dst, wcol):
                dve.wait_ge(rms_ready, n)
                link(v.reciprocal(rms_t[:, 1, :], rms_t[:, 0, :]))
                for k in range(KT):
                    ins = v.scalar_tensor_tensor(out=dst[:, k, :], in0=XT[:, k, :], scalar=wcol[:, k:k + 1],
                                                 in1=rms_t[:, 1, :], op0=ALU.mult, op1=ALU.mult)
                    if k % 4 == 3:
                        ins.then_inc(normed if k == KT - 1 else norm_part, 1)

            for n, free in enumerate((conv_done, conv_mixed, mlstm_done, merge_done, resid_done, hgrn_done, delta_done,
                                      keyscore_copied, picked, wmul)):
                v.memset(w1s[:, n:n + 1], 0.0).then_inc(free, 1)
            dve.wait_ge(c_ready, 1)
            land = [Count(landed[0], "dve slot 0"), Count(landed[1], "dve slot 1")]
            with rounds(dve, 6, (steps, 2 * ADA_DVE - 2), (land[0], 16), (land[1], 16)) as i:
                for n in range(2):
                    dve.wait_ge(landed[n], land[n].up(16))
                    w = ring[n][:, 0:KT * 512].rearrange("p (k c) -> p k c", c=512)
                    ins = v.tensor_scalar(ada_acc[n], w[:, 0, :], cact[:, 0:1], None, ALU.mult)
                    for k in range(1, ADA_DVE):
                        link(ins)
                        ins = v.scalar_tensor_tensor(out=ada_acc[n], in0=w[:, k, :], scalar=cact[:, k:k + 1],
                                                     in1=ada_acc[n], op0=ALU.mult, op1=ALU.add)
                    ins.then_inc(ada_part, 1)
            dve.wait_ge(mod_turned, 1)
            v.memset(cu, 0.0).then_inc(pads_done, 1)
            tiles.n = SETUP + ADA
            dve.wait_ge(act_step, 1)
            link(v.tensor_tensor(lbc[:, 2, :], lbc[:, 0, :], lbc[:, 1, :], ALU.add))
            link(v.reciprocal(lbc[:, 3, :], lbc[:, 2, :]))
            link(v.tensor_tensor(lbc[:, 2, :], lbc[:, 0, :], lbc[:, 3, :], ALU.mult))
            link(v.tensor_scalar(lbc[:, 3, :], lbc[:, 2, :], -1.0, 1.0, ALU.mult, ALU.add))
            link(v.tensor_tensor(mod[:, :], banks[4][:, 0:48], par[:, PK_BADA:PK_BADA + 48], ALU.add))
            v.scalar_tensor_tensor(out=w1s[:, :], in0=mod[:, 16:32], scalar=1.0, in1=par[:, PK_NORM1:PK_NORM1 + KT],
                                   op0=ALU.add, op1=ALU.mult).then_inc(mod_ready, 1)
            dve.wait_ge(mod_ready, 1)
            norm(1, hT, w1s)

            I, F_, AB, LF, F, A, MX, Z = (g8[:, n, :] for n in range(8))
            link(v.memset(Z, 0.0))
            for q in range(4):
                dve.wait_ge(hc_rounded, q + 1)
                v.tensor_tensor(hc_lo[:, 4 * q:4 * q + 4, :], hT[:, 4 * q:4 * q + 4, :],
                                hc_hi[:, 4 * q:4 * q + 4, :].bitcast(F32), ALU.subtract).then_inc(hc_split, 1)

            def split_weights(n, q):
                dve.wait_ge(wc_rounded, 4 * n + (q + 1))
                at = slice(4 * (q % 2), 4 * (q % 2) + 4)
                v.tensor_tensor(wc_lo[:, at, :], half_ring[q // 2][:, at, :], wc_hi[:, at, :].bitcast(F32),
                                ALU.subtract).then_inc(wc_split, 1)

            split_weights(0, 0)
            split_weights(0, 1)
            dve.wait_ge(gates_mm, 2)
            v.tensor_scalar(I, banks[4][0:8, 0:T], gbias[:, 0:1], None, ALU.add)
            link(v.tensor_scalar(F_, banks[5][0:8, 0:T], gbias[:, 1:2], None, ALU.add))
            v.scalar_tensor_tensor(out=AB, in0=F_, scalar=-1.0, in1=F_, op0=ALU.mult, op1=ALU.max).then_inc(gates_abs, 1)
            dve.wait_ge(gates_log, 1)
            link(v.scalar_tensor_tensor(out=LF, in0=F_, scalar=0.0, in1=AB, op0=ALU.min, op1=ALU.subtract))
            link(v.tensor_tensor_scan(F, LF, Z, 0.0, ALU.add, ALU.add))
            link(v.tensor_tensor(A, I, F, ALU.subtract))
            v.tensor_tensor_scan(MX, A, A, 0.0, ALU.max, ALU.max).then_inc(gates_rows, 1)
            dve.wait_ge(gates_rows, 1)
            link(v.tensor_scalar(AB, MX, -1.0, None, ALU.mult))
            link(v.tensor_tensor(LF, AB, F, ALU.subtract))

            def spread_rows(n, row):
                link(v.tensor_tensor(spread[:, n, :, :], b3(row, 8),
                                     ident[0:8, 0:8].unsqueeze(2).broadcast_to([8, 8, T]), ALU.mult))

            spread_rows(0, AB)
            spread_rows(1, LF)

            dve.wait_ge(pads_done, 1)
            def conv_tap(j, tap):
                for n in range(2):
                    wc = pcol(2 * j + (PK_CONV + tap * 16 + n))
                    if tap == 2:
                        ins = v.tensor_scalar(cy[:, n, :], cu[:, n, 2:T + 2], wc, None, ALU.mult)
                    else:
                        ins = v.scalar_tensor_tensor(out=cy[:, n, :], in0=cu[:, n, tap:tap + T], scalar=wc,
                                                     in1=cy[:, n, :], op0=ALU.mult, op1=ALU.add)
                return ins

            def mix(j, part):
                if part == 0:
                    tiles.up(4)
                    dve.wait_ge(tile_evac, tiles.value())
                    link(v.tensor_tensor(cu[:, :, 2:T + 2], cv[:, 0:2, :], cv[:, 2:4, :], ALU.mult))
                    link(conv_tap(j, 2))
                elif part == 1:
                    link(conv_tap(j, 1))
                    conv_tap(j, 0).then_inc(conv_mixed, 1)
                else:
                    tiles.up(4)
                    dve.wait_ge(tile_evac, tiles.value())
                    dve.wait_ge(conv_mixed, 1 + j + 1)
                    link(v.tensor_tensor(cy, cy, cv[:, 4:6, :], ALU.mult))
                    link(v.tensor_tensor(cy, cy, cv[:, 6:8, :], ALU.mult))
                    v.tensor_copy(HB[:, ds(2 * j, 2), :], cy).then_inc(conv_done, 1)

            for q in (2, 3):
                split_weights(0, q)
            for q in range(4):
                split_weights(1, q)
            with rounds(dve, 7, (steps, 5), (tiles, 8)) as j:
                split_weights(2 * j + 2, 0)
                mix(j, 0)
                split_weights(2 * j + 2, 1)
                mix(j, 1)
                split_weights(2 * j + 2, 2)
                split_weights(2 * j + 2, 3)
                split_weights(2 * j + 3, 0)
                mix(j, 2)
                for q in range(1, 4):
                    split_weights(2 * j + 3, q)
            for part in range(3):
                mix(7, part)

            dve.wait_ge(gates_tp, 1)
            v.tensor_copy(colT[:, 0, :, :], banks[6][:, 0:16].rearrange("p (c h) -> p c h", h=8)).then_inc(gates_done, 1)

            with rounds(dve, 8, (steps, 7), (tiles, 8)) as h:
                dve.wait_ge(scores_ready, h + 1)
                v.tensor_scalar(mE[:, 0:T], banks[6][:, 0:T], colT[:, 0, 0, ds(h, 1)], 0.0, ALU.add, ALU.min)
                v.tensor_scalar(mE[:, T:T + P], banks[6][:, P:T], colT[:, 0, 1, ds(h, 1)], 0.0, ALU.add,
                                ALU.min).then_inc(expo_ready, 1)
                dve.wait_ge(causal_done, h + 1)
                v.scalar_tensor_tensor(out=mS, in0=banks[4][:, 0:384], scalar=float(128 ** -0.5), in1=mE,
                                       op0=ALU.mult, op1=ALU.mult).then_inc(att_ready, 1)
                dve.wait_ge(num_ready, h + 1)
                dve.wait_ge(floor_done, h + 1)
                link(v.tensor_tensor(mden[:, 0, :], banks[6][:, 0:T], mfloor, ALU.max))
                link(v.scalar_tensor_tensor(out=mden[:, 0, :], in0=banks[6][:, 0:T], scalar=-1.0, in1=mden[:, 0, :],
                                            op0=ALU.mult, op1=ALU.max))
                link(v.reciprocal(mden[:, 0, :], mden[:, 0, :]))
                link(v.tensor_tensor(mh, banks[5].rearrange("p (n t) -> p n t", t=T), b3(mden[:, 0, :], 2), ALU.mult))
                dve.wait_ge(tile_evac, tiles.value(6))
                v.tensor_tensor(mh, mh, mo, ALU.mult).then_inc(h_ready, 1)
                dve.wait_ge(h_ready, h + 1)
                dve.wait_ge(hrms_ready, h + 1)
                link(v.reciprocal(mden[:, 1, :], mden[:, 1, :]))
                for n in range(2):
                    ins = v.scalar_tensor_tensor(out=mh[:, n, :], in0=mh[:, n, :], scalar=pcol(2 * h + (PK_HEADN + n)),
                                                 in1=mden[:, 1, :], op0=ALU.mult, op1=ALU.mult)
                link(ins)
                dve.wait_ge(tile_evac, tiles.value(8))
                link(v.tensor_tensor(mh, mh, mz, ALU.mult))
                v.tensor_copy(HA[:, ds(2 * h, 2), :], mh).then_inc(mlstm_done, 1)
                tiles.up(8)

            with rounds(dve, 8, (steps, 1), (tiles, 8)) as j:
                tiles.up(8)
                dve.wait_ge(tile_evac, tiles.value())
                link(v.tensor_tensor(prod, sg, yy, ALU.mult))
                v.tensor_tensor(MG[:, ds(2 * j, 2), :], prod[:, 0:2, :], prod[:, 2:4, :], ALU.add).then_inc(merge_done, 1)

            def residual(p, src, made):
                dve.wait_ge(*made)
                for q in range(4):
                    dve.wait_ge(hc_rounded, 4 * (p + 1) + q + 1)
                    v.tensor_tensor(ho_lo[:, 4 * q:4 * q + 4, :], src[:, 4 * q:4 * q + 4, :],
                                    ho_hi[:, 4 * q:4 * q + 4, :].bitcast(F32), ALU.subtract).then_inc(hc_split, 1)

                def add(n):
                    tiles.up(4)
                    dve.wait_ge(tile_evac, tiles.value())
                    part = XT[:, 4 * n:4 * n + 4, :]
                    v.tensor_tensor(part, part, upd[:, 4 * (n % 2):4 * (n % 2) + 4, :], ALU.add).then_inc(resid_done, 1)

                for n in range(4):
                    split_weights(out_chunk(p, n), 0)
                    if n >= 2:
                        add(n - 2)
                    for q in range(1, 4):
                        split_weights(out_chunk(p, n), q)
                add(2)
                add(3)
                dve.wait_ge(resid_done, 1 + 4 * (p + 1))

            residual(0, MG, (merge_done, 1 + 8))
            norm(2, XT, par[:, PK_NORMF:PK_NORMF + KT])
            norm(3, hT, par[:, PK_ATTN:PK_ATTN + KT])

            link(v.memset(zrow, 0.0))
            link(v.memset(hatt, 0.0))
            dve.wait_ge(masks_done, 1)
            with rounds(dve, 4, (steps, 10), (tiles, 8)) as i:
                for s in range(2):
                    head = 2 * i + s
                    dve.wait_ge(decay_in, 2 * head + 2)
                    v.tensor_scalar(hk, hneg, lbc[:, 3, ds(head, 1)], None, ALU.mult)
                    link(v.tensor_tensor_scan(hb, hlf, zrow, 0.0, ALU.add, ALU.add))
                    for l, half in enumerate(LEVELS + [128]):
                        bb = hb.rearrange("p (n s t) -> p n s t", s=2, t=half)
                        ee = hE[:, l, :].rearrange("p (n s t) -> p n s t", s=2, t=half)
                        nb = T // (2 * half)
                        ref = bb[:, :, 0, half - 1:half].broadcast_to([P, nb, half])
                        v.tensor_tensor(ee[:, :, 1, :], bb[:, :, 1, :], ref, ALU.subtract)
                        ins = v.tensor_tensor(ee[:, :, 0, :], ref, bb[:, :, 0, :], ALU.subtract)
                    ins.then_inc(decay_exp, 1)
                    dve.wait_ge(decayed, head + 1)
                    dve.wait_ge(dve_step, steps.value())
                    for l, half in enumerate(LEVELS + [128]):
                        qq, kk, ee, xx = (y.rearrange("p (n s t) -> p n s t", s=2, t=half)
                                          for y in (hq, hk, hE[:, l, :], hX[:, l, :]))
                        v.tensor_tensor(xx[:, :, 1, :], qq[:, :, 1, :], ee[:, :, 1, :], ALU.mult)
                        ins = v.tensor_tensor(xx[:, :, 0, :], kk[:, :, 0, :], ee[:, :, 0, :], ALU.mult)
                    ins.then_inc(x_levels, 1)
                    for l in range(9):
                        dve.wait_ge(gram_done, head * 9 + l + 1)
                        dve.wait_ge(gram_taken, head * 9 + l)
                        if l:
                            carry()
                        b = banks[4 + l % 4]
                        if l == 0:
                            ins = v.tensor_copy(hatt[:, 1, :], b[:, 0:P])
                        else:
                            mask = masks[:, l - 1, :] if l < 8 else ident[:, :]
                            ins = v.copy_predicated(hatt[:, 0:3:2, :], b3(mask, 2).bitcast(U32),
                                                    b[:, 0:T].rearrange("p (c t) -> p c t", t=P))
                        ins.then_inc(gram_taken, 1)
                    dve.wait_ge(orms_ready, head + 1)
                    link(v.reciprocal(hsig, hon))
                    link(v.scalar_tensor_tensor(out=hneg, in0=banks[5][:, 0:T], scalar=par[:, PK_HGN:PK_HGN + 1],
                                                in1=hsig, op0=ALU.mult, op1=ALU.mult))
                    tiles.up(4)
                    dve.wait_ge(tile_evac, tiles.value())
                    link(v.tensor_tensor(hneg, hneg, hz, ALU.mult))
                    link(v.tensor_copy(MIX[:, ds(head, 1), :].rearrange("p o t -> p (o t)"), hneg))
                    v.memset(hb[:, 0:1], 0.0).then_inc(hgrn_done, 1)

            link(v.memset(Z, 0.0))
            link(v.memset(draw, 0.0))
            dve.wait_ge(gates_mm, 4)
            link(v.tensor_scalar(F_, banks[5][0:8, 0:T], gbias[:, 3:4], None, ALU.add))
            v.scalar_tensor_tensor(out=AB, in0=F_, scalar=-1.0, in1=F_, op0=ALU.mult, op1=ALU.max).then_inc(gates_abs, 1)
            dve.wait_ge(gates_log, 2)
            link(v.scalar_tensor_tensor(out=LF, in0=F_, scalar=0.0, in1=AB, op0=ALU.max, op1=ALU.add))
            dve.wait_ge(decay_in, 18)
            link(v.tensor_scalar(LF, LF, gbias[:, 4:5], -1.0, ALU.mult, ALU.mult))
            v.tensor_tensor_scan(F, LF, Z, 0.0, ALU.add, ALU.add).then_inc(gates_rows, 1)
            dve.wait_ge(gates_rows, 2)
            spread_rows(0, F)
            spread_rows(1, I)
            dve.wait_ge(gates_tp, 2)
            v.tensor_copy(colT[:, 1:3, :, :], banks[6][:, 0:32].rearrange("p (r c h) -> p r c h", r=2, h=8)).then_inc(gates_done, 1)

            def conv_taps(g, pair, taps):
                for tap in taps:
                    for m in (2 * pair, 2 * pair + 1):
                        wc = pcol((g, 4 + g, 8 + 2 * g, 9 + 2 * g)[m] + (PK_GCONV + 16 * tap))
                        if tap == 0:
                            ins = v.tensor_scalar(dy[:, m, :], draw[:, m, 0:T], wc, None, ALU.mult)
                        else:
                            ins = v.scalar_tensor_tensor(out=dy[:, m, :], in0=draw[:, m, tap:tap + T], scalar=wc,
                                                         in1=dy[:, m, :], op0=ALU.mult, op1=ALU.add)
                    if tap < TAPS - 1:
                        link(ins)
                    elif pair == 1:
                        ins.then_inc(conv_in, 1)

            tiles.up(4)
            dve.wait_ge(tile_evac, tiles.value())
            for pair in range(2):
                conv_taps(0, pair, range(TAPS))

            def delta(g, last=False):
                dve.wait_ge(qk_rms, g + 1)
                link(v.reciprocal(drt, drt))
                v.scalar_tensor_tensor(out=dqk[:, 0, :], in0=dc[:, 0, :], scalar=float(128 ** -0.5), in1=drt[:, 0, :],
                                       op0=ALU.mult, op1=ALU.mult)
                v.tensor_tensor(dqk[:, 1, :], dc[:, 1, :], drt[:, 1, :], ALU.mult).then_inc(qk_unit, 1)
                dve.wait_ge(bc_ready, g + 1)
                for n in range(2):
                    for c in range(TT):
                        dst = dW[:, 3 * n:3 * n + 2, :].rearrange("p a t -> p (a t)") if c == 0 else dW[:, 3 * n + 2, :]
                        ins = v.tensor_scalar(dst, banks[4 + n][:, c * P:T], colT[:, 1, c, ds(2 * g + n, 1)], 0.0,
                                              ALU.subtract, ALU.min)
                ins.then_inc(dex_ready, 1)
                dve.wait_ge(dmask_done, g + 1)
                for n in range(2):
                    w = dW[:, 3 * n:3 * n + 3, :]
                    ins = v.tensor_tensor(dM[:, 3 * n:3 * n + 3, :], banks[6][:, 0:384].rearrange("p (a t) -> p a t", t=P), w, ALU.mult)
                link(ins)
                for n in range(2):
                    w = dM[:, 3 * n:3 * n + 2, :]
                    v.tensor_tensor(w, w, banks[4 + n][:, T:2 * T].rearrange("p (a t) -> p a t", t=P), ALU.mult)
                    w = dM[:, 3 * n + 2, :]
                    ins = v.tensor_tensor(w, w, banks[4 + n][:, T + P:2 * T], ALU.mult)
                link(ins)

                def cross(l):
                    for n in range(2):
                        ins = v.tensor_tensor(dC[:, 2 * n:2 * n + 2, :], dM[:, 3 * n:3 * n + 3:2, :], b3(masks[:, l, :], 2), ALU.mult)
                    return ins

                cross(0).then_inc(lv_mask, 1)
                for n in range(2):
                    w = dW[:, 3 * n:3 * n + 3, :]
                    v.tensor_tensor(dA[:, 3 * n:3 * n + 3, :], banks[7][:, 0:384].rearrange("p (a t) -> p a t", t=P), w, ALU.mult)
                dve.wait_ge(lv_mask, g * 7 + 1)
                v.tensor_tensor(dD[:, 4:8, :], b3(ident[:, :], 4), dC, ALU.subtract)
                dve.wait_ge(lv_dd, g * 7 + 1)
                link(v.tensor_tensor(dD[:, 0:4, :], b3(ident[:, :], 4), banks[5].rearrange("p (q t) -> p q t", t=P), ALU.subtract))
                cross(1).then_inc(lv_mask, 1)
                for l in range(2, 7):
                    dve.wait_ge(lv_dd, g * 7 + l)
                    v.tensor_tensor(dD[:, 0:4, :], dD[:, 0:4, :], banks[5].rearrange("p (q t) -> p q t", t=P), ALU.subtract)
                    v.tensor_tensor(dD[:, 4:8, :], dD[:, 4:8, :], banks[6].rearrange("p (q t) -> p q t", t=P), ALU.subtract)
                    cross(l).then_inc(lv_mask, 1)
                    if not last and l > 2:
                        if l in (3, 5):
                            dve.wait_ge(tile_evac, tiles.value(l + 1))
                        conv_taps(g + 1, (l - 3) // 2, ((2, 3) if l % 2 == 0 else (0, 1)))
                dve.wait_ge(lv_dd, g * 7 + 7)
                v.tensor_tensor(dD[:, 4:8, :], dD[:, 4:8, :], banks[6].rearrange("p (q t) -> p q t", t=P), ALU.subtract).then_inc(lv_new, 1)
                dve.wait_ge(r2_mm, g + 1)
                v.tensor_tensor(dr2, dbv[:, 1:4:2, :], banks[5][:, 0:T].rearrange("p (q t) -> p q t", t=P), ALU.subtract).then_inc(r2_ready, 1)
                dve.wait_ge(orms_ready, 8 + g + 1)
                link(v.reciprocal(don, don))
                link(v.scalar_tensor_tensor(out=dosq, in0=banks[7].rearrange("p (q t) -> p q t", t=T),
                                            scalar=par[:, PK_GDN:PK_GDN + 1], in1=don, op0=ALU.mult, op1=ALU.mult))
                v.tensor_tensor(MIX[:, ds(8 + 2 * g, 2), :], dosq, dz, ALU.mult).then_inc(delta_done, 1)
                tiles.up(2 if last else 6)

            with rounds(dve, GROUPS - 1, (steps, 3 + 1 + 2 + 6), (tiles, 6)) as g:
                delta(g)
            delta(GROUPS - 1, last=True)

            residual(1, MIX, (delta_done, 1 + GROUPS))
            norm(4, hT, par[:, PK_FFN:PK_FFN + KT])

            def top16(vals, idx, src, spare):
                carry()
                link(v.max(vals[:, 0:8], src))
                carry()
                v.max_index(idx[:, 0:8], vals[:, 0:8], src)
                link(v.match_replace(spare, vals[:, 0:8], src, -3.0e38))
                carry()
                link(v.max(vals[:, 8:16], spare))
                carry()
                return v.max_index(idx[:, 8:16], vals[:, 8:16], spare)

            with rounds(dve, 4, (steps, 54)) as i:
                for s in range(2):
                    head = 2 * i + s
                    dve.wait_ge(keyscore_copied, 1 + head + 1)
                    for c in range(TT):
                        for half in range(2):
                            ins = top16(ev[:, c, half, :], ei[:, c, half, :], esc[:, s, c, half, :], esc2[:, c, half, :])
                    link(ins)
                    link(v.tensor_copy(eif, ei))
                    for c in range(TT):
                        ins = v.tensor_tensor(ecand[:, c, :].rearrange("p (i j) -> p i j", j=TOPK),
                                              ev[:, c, 0, :].unsqueeze(2).broadcast_to([P, TOPK, TOPK]),
                                              b3(ev[:, c, 1, :], TOPK), ALU.add)
                    link(ins)
                    for c in range(TT):
                        ins = top16(ebv[:, c, :], ebp[:, c, :], ecand[:, c, :], ecand2[:, c, :])
                    link(ins)
                    v.tensor_scalar(ehl[:, 0, :, :], ebp, 4, None, ALU.logical_shift_right)
                    link(v.tensor_scalar(ehl[:, 1, :, :], ebp, 15, None, ALU.bitwise_and))
                    link(v.tensor_copy(ehf, ehl))
                    for q in range(2):
                        ins = v.tensor_tensor(eeq[:, q, :, :, :], ehf[:, q, :, :].unsqueeze(3).broadcast_to([P, 2, TOPK, TOPK]),
                                              iota[:, 0:TOPK].unsqueeze(1).unsqueeze(1).broadcast_to([P, 2, TOPK, TOPK]), ALU.is_equal)
                    link(ins)
                    for q in range(2):
                        ins = v.tensor_tensor(eeq[:, q, :, :, :], eeq[:, q, :, :, :],
                                              eif[:, :, q, :].unsqueeze(2).broadcast_to([P, 2, TOPK, TOPK]), ALU.mult)
                    link(ins)
                    for q in range(2):
                        v.tensor_reduce(e12[:, q, :, ds(head * TOPK, TOPK)], eeq[:, q, :, :, :], AX.X, ALU.add)
                    link(v.tensor_tensor(ebest[:, :, ds(head * TOPK, TOPK)], ebv, ebv[:, :, 0:1].broadcast_to([P, 2, TOPK]), ALU.subtract))
                    v.memset(esum[:, 0:1], 0.0).then_inc(picked, 1)
            dve.wait_ge(picked, 1 + 8)
            v.memset(esum[:, 1:2], 0.0).then_inc(best_in, 1)
            dve.wait_ge(best_exp, 1)
            es = esum[:, 0:16].rearrange("p (c h) -> p c h", h=8)
            ex = eexp.rearrange("p c (h k) -> p c h k", k=TOPK)
            link(v.tensor_reduce(es, ex, AX.X, ALU.add))
            link(v.reciprocal(es, es))
            v.tensor_tensor(ex, ex, es.unsqueeze(3).broadcast_to([P, 2, 8, TOPK]), ALU.mult).then_inc(slots_ready, 1)

            tiles.n = FINAL_TILES
            dve.wait_ge(tile_evac, tiles.value())

            def onehots(i, first):
                for s in range(4):
                    n = 4 * i + s
                    if not first:
                        dve.wait_ge(gmat, n - 3)
                    keys = slt[:, 0:2, ds(4 * n, 4)].rearrange("p w q -> p q w")
                    v.tensor_tensor(oh[:, s, :, :, :], iota[:, :].unsqueeze(1).unsqueeze(1).broadcast_to([P, 4, 2, P]),
                                    keys.unsqueeze(3).broadcast_to([P, 4, 2, P]), ALU.is_equal).then_inc(onehot, 1)

            onehots(0, True)
            with rounds(dve, T // 16 - 1) as i:
                onehots(i + 1, False)

            dve.wait_ge(gmat_out, T // 4)
            for q in range(4):
                dve.wait_ge(h_rounded, q + 1)
                v.tensor_tensor(h_lo[:, 4 * q:4 * q + 4, :], hT[:, 4 * q:4 * q + 4, :],
                                h_hi[:, 4 * q:4 * q + 4, :].bitcast(F32), ALU.subtract).then_inc(h_split, 1)

            def weigh(n, b, m):
                if m == 0:
                    dve.wait_ge(act_turned, n + 1)
                g = G[:, ds(4 * n + 2 * m, 2), :]
                v.tensor_tensor(g, g, banks[b + m].rearrange("p (e t) -> p e t", t=T), ALU.mult).then_inc(wmul, 1)

            def split_u(n, b, first=False):
                for k in range(KT):
                    dve.wait_ge(u_rounded, 16 * n + (k + 1))
                    v.tensor_tensor(u_lo[:, k % 4, :], banks[k % 4][:, :], u_hi[:, k % 4, :].bitcast(F32),
                                    ALU.subtract).then_inc(u_split, 1)
                    if not first and k in (11, 12):
                        weigh(n - 1, b, k - 11)

            split_u(0, 6, True)
            split_u(1, 4)
            with rounds(dve, U_CHUNKS // 2 - 1) as i:
                split_u(2 * i + 2, 6)
                split_u(2 * i + 3, 4)
            weigh(U_CHUNKS - 1, 6, 0)
            weigh(U_CHUNKS - 1, 6, 1)

            def leave_halves(i):
                for u in range(4):
                    dve.wait_ge(hi_ready, 4 * i + (u + 1))
                    v.tensor_tensor(v_lo[:, u % 2, :], peer_ring[u // 2][:, u % 2, :], v_hi[:, u % 2, :].bitcast(F32), ALU.subtract)
                    v.tensor_tensor(w_lo[:, u % 2, :], G[:, ds(4 * i + u, 1), :].rearrange("p o t -> p (o t)"),
                                    w_hi[:, u % 2, :].bitcast(F32), ALU.subtract).then_inc(lo_ready, 1)

            with rounds(dve, N_KEYS // 4) as i:
                leave_halves(i)
            dve.wait_ge(y_done, N_KEYS)
            dve.wait_ge(lo_ready, N_KEYS)
            for b in range(4):
                v.tensor_copy(xrow[:, 1, b * 512:(b + 1) * 512], banks[4 + b][:, :]).then_inc(y_rows_dve, 1)
            dve.wait_ge(x_back, 16)
            for b in range(8):
                dve.wait_ge(y_turned, b + 1)
                part = XT[:, 2 * b:2 * b + 2, :]
                ins = v.tensor_tensor(part, part, banks[b].rearrange("p (k t) -> p k t", t=T), ALU.add)
                if b % 2 == 1:
                    ins.then_inc(y_added, 1)
            dve.wait_ge(y_added, 4)
            norm(5, hT, par[:, PK_FINAL:PK_FINAL + KT])

        @block.gpsimd
        def _(pool):
            steps = Count(pool_step, "pool steps")

            def link(ins):
                ins.then_inc(pool_step, 1)
                pool.wait_ge(pool_step, steps.up())

            nc.gpsimd.memset(ones[:, :], 1.0)
            nc.gpsimd.memset(eps_col[:, :], EPS)
            link(nc.gpsimd.memset(ident[:, :], 0.0))
            nc.gpsimd.iota(iota[:, :], [[1, P]], base=0, channel_multiplier=0, allow_small_or_imprecise_dtypes=True)
            nc.gpsimd.affine_select(out=ident[:, :], in_=ident[:, :], compare_op=ALU.not_equal, fill=1.0, base=0,
                                    pattern=[[-1, P]], channel_multiplier=1).then_inc(consts, 1)
            link(nc.gpsimd.memset(masks, 1.0))
            for l, half in enumerate(LEVELS):
                nb = P // (2 * half)
                m = masks[:, l, :]
                for sign, base in ((1, 0), (-1, half - 1)):
                    link(nc.gpsimd.affine_select(out=m, in_=m, compare_op=ALU.is_ge, fill=0.0, base=base,
                                                 pattern=[[-sign * 2 * half, nb], [0, 2], [0, half]],
                                                 channel_multiplier=sign))
                ins = nc.gpsimd.affine_select(out=m, in_=m, compare_op=ALU.is_gt, fill=0.0, base=0,
                                              pattern=[[0, nb], [1, 2], [0, half]], channel_multiplier=0)
                link(ins)
            link(nc.gpsimd.memset(causal_mask, 1.0))
            nc.gpsimd.affine_select(out=causal_mask, in_=causal_mask, compare_op=ALU.is_ge, fill=0.0, base=0,
                                    pattern=[[1, P]], channel_multiplier=-1).then_inc(masks_done, 1)
            pool.wait_ge(masks_done, 1)

            def causal(view):
                return nc.gpsimd.tensor_tensor(view, view, b3(causal_mask, 2), ALU.mult)

            with rounds(pool, 8) as h:
                pool.wait_ge(exp_done, h + 1)
                causal(mE.rearrange("p (a t) -> p a t", t=P)[:, 0:3:2, :]).then_inc(causal_done, 1)
            with rounds(pool, GROUPS) as g:
                pool.wait_ge(dex_done, g + 1)
                for n in range(2):
                    ins = causal(dW[:, 3 * n:3 * n + 3:2, :])
                ins.then_inc(dmask_done, 1)

            with rounds(pool, T // 16) as i:
                for s in range(4):
                    n = 4 * i + s
                    pool.wait_ge(onehot, n + 1)
                    nc.gpsimd.tensor_tensor(pool_carrier[:, s:s + 1], ones[:, 0:1], ones[:, 0:1], ALU.mult)
                    hot = oh[:, s, 2:4, 0, :]
                    nc.gpsimd.tensor_tensor(hot, hot, slt[:, 2, ds(4 * n + 2, 2)].unsqueeze(2).broadcast_to([P, 2, P]),
                                            ALU.mult).then_inc(gated_pool, 1)


_INS = ['x', 'c', 'norm1_w', 'w_ada', 'b_ada', 'w_in', 'b_in', 'conv_w', 'headnorm_w', 'w_proj_a', 'w_proj_b',
        'w_out', 'normf_w', 'attn_norm_g_2', 'w_in_2', 'hgrn_lb_logits_2', 'hgrn_norm_g_2', 'gdn_conv_w_2',
        'gdn_A_log_2', 'gdn_dt_bias_2', 'gdn_norm_g_2', 'w_out_2', 'ffn_norm_g_2', 'peer_w_query_2',
        'peer_sub_keys_2', 'peer_u_2', 'peer_v_2', 'final_norm_g_2']


def kernel(**inputs):
    import numpy as _np
    import concourse.bacc as _bacc
    from concourse import mybir as _mybir
    from concourse.bass_utils import run_bass_kernel_spmd as _run

    nc = _bacc.Bacc("TRN2", target_bir_lowering=False, num_devices=1)
    arrays, aps = {}, {}
    for name in _INS:
        v = _np.ascontiguousarray(inputs[name])
        arrays[f"in_{name}_dram"] = v
        aps[name] = nc.dram_tensor(f"in_{name}_dram", v.shape, _mybir.dt.from_np(v.dtype), kind="ExternalInput").ap()
    out = nc.dram_tensor("out_dram", (1, T, D), F32, kind="ExternalOutput").ap()
    build(nc, aps, out)
    r = _run(nc, [arrays], core_ids=[0])
    return r.results[0]["out_dram"]
```
